# Optimizing a Trainium2 kernel written in Bass

```python
import math
import jax, jax.numpy as jnp
from jax import lax
import numpy as np

D_MODEL = 1024
BATCH = 1
SEQ = 256
DEPTH = 2
DEC_BATCH = 8
DEC_SEQ = 8
PAST_LEN = 2048
PAGE_SIZE = 128

GDN_HEADS = 4
GDN_DK = 128
GDN_DV = 128
CONV_W = 4
HG_HEADS = 4
HG_DK = 128
HG_DV = 128
RET_HEADS = 4
RET_DK = 128
RET_DV = 256
ROPE_BASE = 10000.0
D_FF = 4 * D_MODEL
CHUNK = 64
EPS = 1e-6

GDN_QK = GDN_HEADS * GDN_DK
GDN_V = GDN_HEADS * GDN_DV
GDN_CONV_DIM = 2 * GDN_QK + GDN_V
HG_K = HG_HEADS * HG_DK
HG_V = HG_HEADS * HG_DV
RET_K = RET_HEADS * RET_DK
RET_V = RET_HEADS * RET_DV
SPLITS = (GDN_CONV_DIM, GDN_V, GDN_HEADS, GDN_HEADS, HG_K, HG_K, HG_V, HG_V, RET_K, RET_K, RET_V, RET_V, D_MODEL, D_MODEL, D_MODEL)
N_IN = GDN_CONV_DIM + GDN_V + 2 * GDN_HEADS + 2 * HG_K + 2 * HG_V + 2 * RET_K + 2 * RET_V + 3 * D_MODEL

kernel_name = "hybrid_gdn_hgrn2_retention_decoder_step"

def rmsnorm(x, w):
    xf = x.astype(jnp.float32)
    y = xf * lax.rsqrt(jnp.mean(xf * xf, axis=-1, keepdims=True) + EPS)
    return y.astype(x.dtype) * w.astype(x.dtype)

def norm32(x):
    return x * lax.rsqrt(jnp.mean(x * x, axis=-1, keepdims=True) + EPS)

def l2norm(x):
    return x * lax.rsqrt(jnp.sum(x * x, axis=-1, keepdims=True) + EPS)

def to_chunks(t, c):
    b, n = t.shape[0], t.shape[1] // c
    t = t.reshape((b, n, c) + t.shape[2:])
    return jnp.moveaxis(t, (1, 3), (0, 2))

def from_chunks(o):
    n, b, h, c, d = o.shape
    return jnp.moveaxis(o, (0, 2), (1, 3)).reshape(b, n * c, h, d)

def chunked_gated_delta(q, k, v, log_a, beta, s0):
    t_len = q.shape[1]
    c = math.gcd(t_len, CHUNK)
    dv = v.shape[-1]
    q, k, v, log_a, beta = (to_chunks(t, c) for t in (q, k, v, log_a, beta))
    gam = jnp.cumsum(log_a, axis=-1)
    causal = jnp.tril(jnp.ones((c, c), bool))
    strict = jnp.tril(jnp.ones((c, c), bool), -1)
    diff = gam[..., :, None] - gam[..., None, :]
    ldec = jnp.where(causal, jnp.exp(jnp.where(causal, diff, 0.0)), 0.0)
    kb = k * beta[..., None]
    a_mat = jnp.where(strict, jnp.einsum('nbhik,nbhjk->nbhij', kb, k) * ldec, 0.0)
    rhs = jnp.concatenate([v * beta[..., None], kb * jnp.exp(gam)[..., None]], axis=-1)
    sol = lax.linalg.triangular_solve(a_mat + jnp.eye(c, dtype=a_mat.dtype), rhs,
                                      left_side=True, lower=True, unit_diagonal=True)
    u, w = sol[..., :dv], sol[..., dv:]

    def step(s, xs):
        qc, kc, uc, wc, gc, lc = xs
        v_new = uc - jnp.einsum('bhck,bhkv->bhcv', wc, s)
        attn = jnp.einsum('bhik,bhjk->bhij', qc, kc) * lc
        o = (jnp.einsum('bhck,bhkv->bhcv', qc * jnp.exp(gc)[..., None], s)
             + jnp.einsum('bhij,bhjv->bhiv', attn, v_new))
        g_last = gc[..., -1]
        s = (s * jnp.exp(g_last)[..., None, None]
             + jnp.einsum('bhck,bhcv->bhkv', kc * jnp.exp(g_last[..., None] - gc)[..., None], v_new))
        return s, o

    s, o = lax.scan(step, s0, (q, k, u, w, gam, ldec))
    return from_chunks(o), s

def chunked_gla(q, k, v, log_f, s0):
    t_len = q.shape[1]
    c = math.gcd(t_len, CHUNK)
    q, k, v, log_f = (to_chunks(t, c) for t in (q, k, v, log_f))
    bcum = jnp.cumsum(log_f, axis=-2)
    causal = jnp.tril(jnp.ones((c, c), bool))[:, :, None]

    def step(s, xs):
        qc, kc, vc, bc = xs
        diff = bc[..., :, None, :] - bc[..., None, :, :]
        dec = jnp.where(causal, jnp.exp(jnp.where(causal, diff, 0.0)), 0.0)
        attn = jnp.einsum('bhik,bhjk,bhijk->bhij', qc, kc, dec)
        o = (jnp.einsum('bhck,bhkv->bhcv', qc * jnp.exp(bc), s)
             + jnp.einsum('bhij,bhjv->bhiv', attn, vc))
        b_last = bc[..., -1, :]
        s = (s * jnp.exp(b_last)[..., :, None]
             + jnp.einsum('bhck,bhcv->bhkv', kc * jnp.exp(b_last[..., None, :] - bc), vc))
        return s, o

    s, o = lax.scan(step, s0, (q, k, v, bcum))
    return from_chunks(o), s

def chunked_retention(q, k, v, s0):
    t_len = q.shape[1]
    c = math.gcd(t_len, CHUNK)
    log_gamma = jnp.log(1.0 - 2.0 ** (-5.0 - jnp.arange(RET_HEADS, dtype=jnp.float32)))
    q, k, v = (to_chunks(t, c) for t in (q, k, v))
    idx = jnp.arange(c, dtype=jnp.float32)
    causal = jnp.tril(jnp.ones((c, c), bool))
    rel = jnp.where(causal, idx[:, None] - idx[None, :], 0.0)
    dmask = jnp.where(causal, jnp.exp(rel * log_gamma[:, None, None]), 0.0)
    inner = jnp.exp((idx + 1.0) * log_gamma[:, None])
    tail = jnp.exp((c - 1.0 - idx) * log_gamma[:, None])
    full = jnp.exp(c * log_gamma)

    def step(s, xs):
        qc, kc, vc = xs
        attn = jnp.einsum('bhik,bhjk->bhij', qc, kc) * dmask
        o = (jnp.einsum('bhck,bhkv->bhcv', qc * inner[..., None], s)
             + jnp.einsum('bhij,bhjv->bhiv', attn, vc))
        s = s * full[:, None, None] + jnp.einsum('bhck,bhcv->bhkv', kc * tail[..., None], vc)
        return s, o

    s, o = lax.scan(step, s0, (q, k, v))
    return from_chunks(o), s

def rotary(x, pos0):
    t_len, d = x.shape[1], x.shape[-1]
    half = d // 2
    inv = ROPE_BASE ** (-jnp.arange(half, dtype=jnp.float32) / half)
    ang = (pos0 + jnp.arange(t_len, dtype=jnp.float32))[:, None] * inv[None, :]
    cos, sin = jnp.cos(ang)[None, :, None, :], jnp.sin(ang)[None, :, None, :]
    x1, x2 = x[..., :half], x[..., half:]
    return jnp.concatenate([x1 * cos - x2 * sin, x2 * cos + x1 * sin], axis=-1)

def mixer_block(h, pos0, conv_buf, s_gdn, s_hg, s_ret, lb, w_in, gdn_conv, gdn_a_log, gdn_dt_bias,
                gdn_norm, hgrn_norm, w_br_gdn, w_br_hgrn, w_br_ret, w_out):
    f32 = jnp.float32
    b, t_len, _ = h.shape
    proj = h @ w_in
    offsets = np.cumsum(SPLITS)[:-1].tolist()
    (qkv, z_a, b_a, a_a, q_b, f_b, i_b, z_b, q_c, k_c, v_c, g_c,
     gate_a, gate_b, gate_c) = jnp.split(proj, offsets, axis=-1)

    xc = jnp.concatenate([conv_buf.astype(qkv.dtype), qkv], axis=1)
    conv = xc[:, 0:t_len] * gdn_conv[0]
    for j in range(1, CONV_W):
        conv = conv + xc[:, j:j + t_len] * gdn_conv[j]
    new_buf = xc[:, t_len:]
    qkv_act = jax.nn.silu(conv.astype(f32))
    qa, ka, va = jnp.split(qkv_act, [GDN_QK, 2 * GDN_QK], axis=-1)
    qa = l2norm(qa.reshape(b, t_len, GDN_HEADS, GDN_DK)) * (GDN_DK ** -0.5)
    ka = l2norm(ka.reshape(b, t_len, GDN_HEADS, GDN_DK))
    va = va.reshape(b, t_len, GDN_HEADS, GDN_DV)
    beta = jax.nn.sigmoid(b_a.astype(f32))
    log_a = -jnp.exp(gdn_a_log.astype(f32)) * jax.nn.softplus(a_a.astype(f32) + gdn_dt_bias.astype(f32))
    o_a, s_gdn_new = chunked_gated_delta(qa, ka, va, log_a, beta, s_gdn.astype(f32))
    o_a = norm32(o_a) * gdn_norm.astype(f32) * jax.nn.silu(z_a.astype(f32).reshape(b, t_len, GDN_HEADS, GDN_DV))
    br_a = o_a.reshape(b, t_len, GDN_V).astype(h.dtype) @ w_br_gdn

    fl = f_b.astype(f32).reshape(b, t_len, HG_HEADS, HG_DK)
    lbh = lb.reshape(HG_HEADS, HG_DK)
    log_f = jnp.logaddexp(jnp.log(lbh), jnp.log1p(-lbh) + jax.nn.log_sigmoid(fl))
    k_b = (1.0 - lbh) * jax.nn.sigmoid(-fl)
    qb = jax.nn.silu(q_b.astype(f32).reshape(b, t_len, HG_HEADS, HG_DK)) * (HG_DK ** -0.5)
    ib = i_b.astype(f32).reshape(b, t_len, HG_HEADS, HG_DV)
    o_b, s_hg_new = chunked_gla(qb, k_b, ib, log_f, s_hg.astype(f32))
    o_b = norm32(o_b) * hgrn_norm.astype(f32) * jax.nn.silu(z_b.astype(f32).reshape(b, t_len, HG_HEADS, HG_DV))
    br_b = o_b.reshape(b, t_len, HG_V).astype(h.dtype) @ w_br_hgrn

    qr = rotary(q_c.astype(f32).reshape(b, t_len, RET_HEADS, RET_DK), pos0)
    kr = rotary(k_c.astype(f32).reshape(b, t_len, RET_HEADS, RET_DK), pos0) * (RET_DK ** -0.5)
    vr = v_c.astype(f32).reshape(b, t_len, RET_HEADS, RET_DV)
    o_c, s_ret_new = chunked_retention(qr, kr, vr, s_ret.astype(f32))
    o_c = norm32(o_c) * jax.nn.silu(g_c.astype(f32).reshape(b, t_len, RET_HEADS, RET_DV))
    br_c = o_c.reshape(b, t_len, RET_V).astype(h.dtype) @ w_br_ret

    merged = jax.nn.sigmoid(gate_a) * br_a + jax.nn.sigmoid(gate_b) * br_b + jax.nn.sigmoid(gate_c) * br_c
    return merged @ w_out, new_buf, s_gdn_new, s_hg_new, s_ret_new

def trunk(x, pos0, conv_buf, s_gdn, s_hg, s_ret, norm_mix, norm_ffn, norm_final, w_in, gdn_conv, gdn_a_log,
          gdn_dt_bias, gdn_norm, hgrn_lb, hgrn_norm, w_br_gdn, w_br_hgrn, w_br_ret, w_out, w_up, w_down):
    lb_all = jnp.cumsum(jax.nn.softmax(hgrn_lb.astype(jnp.float32), axis=0), axis=0)
    lb_all = lb_all - lb_all[0]
    new_conv, new_gdn, new_hg, new_ret = [], [], [], []
    for l in range(DEPTH):
        h = rmsnorm(x, norm_mix[l])
        mix, cb, sg, sh, sr = mixer_block(h, pos0, conv_buf[l], s_gdn[l], s_hg[l], s_ret[l], lb_all[l], w_in[l],
                                          gdn_conv[l], gdn_a_log[l], gdn_dt_bias[l], gdn_norm[l], hgrn_norm[l],
                                          w_br_gdn[l], w_br_hgrn[l], w_br_ret[l], w_out[l])
        x = x + mix.astype(x.dtype)
        h = rmsnorm(x, norm_ffn[l])
        x = x + (jnp.square(jax.nn.relu(h @ w_up[l])) @ w_down[l]).astype(x.dtype)
        new_conv.append(cb)
        new_gdn.append(sg)
        new_hg.append(sh)
        new_ret.append(sr)
    y = rmsnorm(x, norm_final)
    return y, jnp.stack(new_gdn), jnp.stack(new_conv), jnp.stack(new_hg), jnp.stack(new_ret)

def setup_inputs(seed: int = 0) -> dict:
    key = jax.random.key(seed)
    ks = jax.random.split(key, 24)

    def nrm(k, shape, scale):
        return scale * jax.random.normal(k, shape, jnp.float32)

    dt = jnp.exp(jax.random.uniform(ks[9], (DEPTH, GDN_HEADS), jnp.float32, math.log(1e-3), math.log(1e-1)))
    return {
        "x_prompt": nrm(ks[0], (BATCH, SEQ, D_MODEL), 1.0),
        "x_sample": nrm(ks[1], (DEC_BATCH, DEC_SEQ, D_MODEL), 1.0),
        "state_gdn": nrm(ks[2], (DEPTH, DEC_BATCH, GDN_HEADS, GDN_DK, GDN_DV), 0.3),
        "state_gdn_conv": nrm(ks[3], (DEPTH, DEC_BATCH, CONV_W - 1, GDN_CONV_DIM), 1.0),
        "state_hgrn": nrm(ks[4], (DEPTH, DEC_BATCH, HG_HEADS, HG_DK, HG_DV), 0.3),
        "state_ret": nrm(ks[5], (DEPTH, DEC_BATCH, RET_HEADS, RET_DK, RET_DV), 1.0),
        "norm_mix": 1.0 + nrm(ks[6], (DEPTH, D_MODEL), 0.02),
        "norm_ffn": 1.0 + nrm(ks[7], (DEPTH, D_MODEL), 0.02),
        "norm_final": 1.0 + nrm(ks[8], (D_MODEL,), 0.02),
        "w_in": nrm(ks[10], (DEPTH, D_MODEL, N_IN), D_MODEL ** -0.5),
        "gdn_conv": nrm(ks[11], (DEPTH, CONV_W, GDN_CONV_DIM), 0.5),
        "gdn_a_log": jnp.log(jax.random.uniform(ks[12], (DEPTH, GDN_HEADS), jnp.float32, 1.0, 16.0)),
        "gdn_dt_bias": dt + jnp.log(-jnp.expm1(-dt)),
        "gdn_norm": 1.0 + nrm(ks[13], (DEPTH, GDN_DV), 0.02),
        "hgrn_lb": nrm(ks[14], (DEPTH, HG_K), 0.5),
        "hgrn_norm": 1.0 + nrm(ks[15], (DEPTH, HG_DV), 0.02),
        "w_br_gdn": nrm(ks[16], (DEPTH, GDN_V, D_MODEL), GDN_V ** -0.5),
        "w_br_hgrn": nrm(ks[17], (DEPTH, HG_V, D_MODEL), HG_V ** -0.5),
        "w_br_ret": nrm(ks[18], (DEPTH, RET_V, D_MODEL), RET_V ** -0.5),
        "w_out": nrm(ks[19], (DEPTH, D_MODEL, D_MODEL), D_MODEL ** -0.5),
        "w_up": nrm(ks[20], (DEPTH, D_MODEL, D_FF), D_MODEL ** -0.5),
        "w_down": nrm(ks[21], (DEPTH, D_FF, D_MODEL), D_FF ** -0.5),
    }

def reference(x_prompt, x_sample, state_gdn, state_gdn_conv, state_hgrn, state_ret, norm_mix, norm_ffn, norm_final,
              w_in, gdn_conv, gdn_a_log, gdn_dt_bias, gdn_norm, hgrn_lb, hgrn_norm, w_br_gdn, w_br_hgrn, w_br_ret,
              w_out, w_up, w_down):
    f32 = jnp.float32
    nb = x_prompt.shape[0]
    zero_conv = jnp.zeros((DEPTH, nb, CONV_W - 1, GDN_CONV_DIM), x_prompt.dtype)
    zero_gdn = jnp.zeros((DEPTH, nb, GDN_HEADS, GDN_DK, GDN_DV), f32)
    zero_hg = jnp.zeros((DEPTH, nb, HG_HEADS, HG_DK, HG_DV), f32)
    zero_ret = jnp.zeros((DEPTH, nb, RET_HEADS, RET_DK, RET_DV), f32)
    y_prompt, new_gdn_p, new_conv_p, new_hgrn_p, new_ret_p = trunk(
        x_prompt, 0, zero_conv, zero_gdn, zero_hg, zero_ret, norm_mix, norm_ffn, norm_final, w_in, gdn_conv,
        gdn_a_log, gdn_dt_bias, gdn_norm, hgrn_lb, hgrn_norm, w_br_gdn, w_br_hgrn, w_br_ret, w_out, w_up, w_down)
    y_sample, new_gdn_s, new_conv_s, new_hgrn_s, new_ret_s = trunk(
        x_sample, PAST_LEN, state_gdn_conv, state_gdn, state_hgrn, state_ret, norm_mix, norm_ffn, norm_final, w_in,
        gdn_conv, gdn_a_log, gdn_dt_bias, gdn_norm, hgrn_lb, hgrn_norm, w_br_gdn, w_br_hgrn, w_br_ret, w_out,
        w_up, w_down)
    return (y_prompt, y_sample, new_gdn_p, new_conv_p, new_hgrn_p, new_ret_p,
            new_gdn_s, new_conv_s, new_hgrn_s, new_ret_s)


_drawn_inputs = setup_inputs


def setup_inputs(seed=0):
    import zlib

    import numpy as np

    out = dict(_drawn_inputs(seed))
    spreads = {}
    factors = {'norm_final': 27.067, 'gdn_norm': 52.542, 'hgrn_norm': 61.431, 'norm_ffn': 4.675}
    for name, (base, spread) in spreads.items():
        noise = np.random.default_rng([zlib.crc32(name.encode()), seed]).standard_normal(out[name].shape)
        drawn = base * np.exp(spread * noise) if base else spread * noise
        out[name] = __import__('jax').numpy.asarray(drawn.astype(out[name].dtype))
    for name, factor in factors.items():
        out[name] = (out[name] * factor).astype(out[name].dtype)
    return out
```

```python
import math
from contextlib import ExitStack

import numpy as np

import concourse.bass as bass
from concourse import mybir
from concourse.alu_op_type import AluOpType as ALU

ACT = mybir.ActivationFunctionType
F32 = mybir.dt.float32
U8 = mybir.dt.uint8

P = 128
DEPTH = 2
D = 1024
KT = D // P
SEQ, SB, ST = 256, 8, 8
T = SEQ + SB * ST
HEADS = 4
DV_RET = 256
D_FF = 4 * D
EPS = 1e-6
PAST = 2048
CHUNKS = ((0, P), (P, P), (SEQ, SB * ST))
SAMPLE = 2
HIST = 3
RAW_P = HIST + SEQ
RAW_S = HIST + ST
RAW = RAW_P + SB * RAW_S
CONV = RAW - HIST
LEVELS = (1, 2, 4, 8, 16, 32, 64)
DIAG = 7
NEG_BIG = -1e30

SLOT = 4096
RING = 3
AHEAD = 2
SLOT_NAMES = (["q_a", "k_a", "v_a", "f_b", "z_a", "q_b", "i_b", "z_b", "gate_a0", "gate_a1", "br_a", "q_c", "k_c",
               "v_c0", "v_c1", "g_c0", "g_c1", "gate_b0", "gate_b1", "br_b", "gate_c0", "gate_c1", "br_c0", "br_c1",
               "out0", "out1"] + [f"up{i}" for i in range(8)] + [f"down{i}" for i in range(8)])
NSLOT = len(SLOT_NAMES)
W_IN_COLUMN = {"q_a": 0, "k_a": 512, "v_a": 1024, "z_a": 1536, "q_b": 2056, "f_b": 2568, "i_b": 3080, "z_b": 3592,
               "q_c": 4104, "k_c": 4616, "v_c0": 5128, "v_c1": 5640, "g_c0": 6152, "g_c1": 6664,
               "gate_a0": 7176, "gate_a1": 7688, "gate_b0": 8200, "gate_b1": 8712, "gate_c0": 9224, "gate_c1": 9736}
BA_COLUMN = 2048

PAR = {}
NPAR = 0
for _name, _n in (("nm", 8), ("nf", 8), ("cw", 48), ("gn", 1), ("hn", 1), ("alog", 4), ("dt", 4), ("llb", 4), ("nllb", 4),
                  ("oml", 4)):
    PAR[_name] = (NPAR, NPAR + _n)
    NPAR += _n

CST = {}
NCONST = 0
for _name, _n in (("ident", P), ("ones", P), ("upP", P), ("upS", 64), ("sameS", 64), ("cos", T), ("sin", T),
                  ("dmP", 4 * P), ("dmS", 4 * 64), ("innP", 4 * P), ("innS", 4 * 64), ("tailP", 4), ("tailS", 4),
                  ("reset", T), ("seqm", 4), ("eps", 1), ("one", 1), ("lnq", 1), ("zero", 1)):
    CST[_name] = (NCONST, NCONST + _n)
    NCONST += _n
GAMMA = [1.0 - 2.0 ** (-5.0 - h) for h in range(HEADS)]


def shape_constants():
    c = np.zeros((P, NCONST), np.float32)

    def put(name, a):
        s, e = CST[name]
        c[:a.shape[0], s:e] = a.reshape(a.shape[0], -1)

    i = np.arange(P)
    put("ident", np.eye(P))
    put("ones", np.ones((P, P)))
    put("upP", (i[:, None] <= i[None, :]) * 1.0)
    s = np.arange(64)
    same = (s[:, None] // ST) == (s[None, :] // ST)
    put("upS", ((s[:, None] <= s[None, :]) & same) * 1.0)
    put("sameS", same * 1.0)
    half = P // 2
    inv = (np.float32(10000.0) ** (-np.arange(half, dtype=np.float32) / np.float32(half))).astype(np.float32)
    pos = np.concatenate([np.arange(SEQ), np.tile(PAST + np.arange(ST), SB)]).astype(np.float32)
    ang = (pos[None, :] * inv[:, None]).astype(np.float32).astype(np.float64)
    put("cos", np.concatenate([np.cos(ang), np.cos(ang)]))
    put("sin", np.concatenate([-np.sin(ang), np.sin(ang)]))
    g = np.array(GAMMA)
    rel = i[None, :] - i[:, None]
    put("dmP", np.where(rel[:, None, :] >= 0, g[None, :, None] ** np.maximum(rel, 0)[:, None, :], 0.0))
    rel = s[None, :] - s[:, None]
    put("dmS", np.where((rel >= 0)[:, None, :] & same[:, None, :], g[None, :, None] ** np.maximum(rel, 0)[:, None, :], 0))
    put("innP", np.broadcast_to((g[:, None] ** (i + 1)[None, :])[None], (P, 4, P)))
    put("innS", np.broadcast_to((g[:, None] ** (s % ST + 1)[None, :])[None], (P, 4, 64)))
    put("tailP", g[None, :] ** (P - 1 - i)[:, None])
    put("tailS", g[None, :] ** (ST - 1 - s % ST)[:, None])
    start = np.ones(T)
    start[[0, P]] = 0
    start[SEQ::ST] = 0
    put("reset", np.broadcast_to(start, (P, T)))
    put("seqm", ((s // ST) % 4)[:, None] == np.arange(4)[None, :])
    put("eps", np.full((P, 1), EPS))
    put("one", np.full((P, 1), 1.0))
    put("lnq", np.full((P, 1), -0.5 * math.log(P)))
    m = np.zeros((P, 15, P), np.float32)
    for lv, h in enumerate(LEVELS):
        pair = (i[:, None] // (2 * h)) == (i[None, :] // (2 * h))
        up = pair & (i[:, None] % (2 * h) < h) & (i[None, :] % (2 * h) >= h)
        m[:, lv] = up
        m[:, 8 + lv] = up.T
    m[:, DIAG] = np.eye(P)
    return c, m


UNITS = []
UNIT_AT = {}


def _units(kind, slots, tiles):
    k = 0
    for s in slots:
        for m in range(tiles):
            UNIT_AT[(kind, k)] = len(UNITS)
            UNITS.append((kind, SLOT_NAMES.index(s) if s else None, m, k))
            k += 1


for _kind, _slots, _tiles in (
        ("raw", ["q_a", "k_a", "v_a"], 4), ("f_b", ["f_b"], 4), ("z_a", ["z_a"], 4), ("ba", [None], 1),
        ("q_b", ["q_b"], 4), ("i_b", ["i_b"], 3), ("z_b", ["z_b"], 4), ("gate_a", ["gate_a0", "gate_a1"], 4),
        ("br_a", ["br_a"], 8), ("q_c", ["q_c"], 4), ("k_c", ["k_c"], 4), ("v_c", ["v_c0", "v_c1"], 3),
        ("g_c", ["g_c0", "g_c1"], 4), ("gate_b", ["gate_b0", "gate_b1"], 4), ("br_b", ["br_b"], 8),
        ("gate_c", ["gate_c0", "gate_c1"], 4), ("br_c", ["br_c0", "br_c1"], 4), ("out", ["out0", "out1"], 4),
        ("up", [f"up{i}" for i in range(8)], 4), ("down", [f"down{i}" for i in range(8)], 1)):
    _units(_kind, _slots, _tiles)
NU = len(UNITS)
LAST_UNIT = {}
for _u, (_k, _s, _m, _i) in enumerate(UNITS):
    if _s is not None:
        LAST_UNIT[_s] = _u
BANKS = 3
SILU_KINDS = ("z_a", "q_b", "z_b", "g_c")
TEMP_UNITS = [u for u, x in enumerate(UNITS) if x[0] in SILU_KINDS + ("q_c", "k_c")]
TEMP_ORDER = {u: n for n, u in enumerate(TEMP_UNITS)}
SILU_NO = {u: n for n, u in enumerate(u for u in TEMP_UNITS if UNITS[u][0] in SILU_KINDS)}
ROT_NO = {u: n for n, u in enumerate(u for u in TEMP_UNITS if UNITS[u][0] not in SILU_KINDS)}
EXP_BOUND = 1e18
TABLE_SET = "natural_log_exp_and_others"


def unit_list(*kinds):
    return [("unit", u) for u, x in enumerate(UNITS) if x[0] in kinds]


SLACK = {"g_bc": 4.0, "g_gram": 3.0, "g_p": 0.8, "g_z": 1.2, "g_s": 0.5, "h_m": 0.7, "h_l": 0.3, "r_s": 0.5, "l2": 0.3,
         "conv": 3.0, "silu": 3.0}


def merge(core, units):
    slack = [SLACK.get(item[0], 1.0) for item in core]
    out, done, sum_ = [], 0, 0.0
    for item, w in zip(core, slack):
        out.append(item)
        sum_ += w
        upto = int(sum_ * len(units) / sum(slack) + 0.5)
        out += units[done:upto]
        done = upto
    return out + units[done:]


def levels_of(c):
    return 3 if c == SAMPLE else 7


GDN_CORE = []
for _c in range(3):
    GDN_CORE += [("g_bc", _c), ("g_gram", _c)]
    for _lv in range(1, levels_of(_c)):
        GDN_CORE += [("g_p", _c, _lv), ("g_z", _c, _lv)]
    GDN_CORE += [("g_ks", _c)] if _c else []
    GDN_CORE += [("g_ks2", _c)] if _c == SAMPLE else []
    GDN_CORE += [("g_v", _c), ("g_o", _c), ("g_n", _c)]
HG_CORE = []
for _c in range(3):
    HG_CORE += [("h_e", _c), ("h_l", _c, 0), ("h_t", _c)]
    for _lv in range(levels_of(_c)):
        if _lv + 1 < levels_of(_c):
            HG_CORE.append(("h_l", _c, _lv + 1))
        HG_CORE.append(("h_m", _c, _lv))
    HG_CORE += [("h_o", _c)] if _c != SAMPLE else [("h_s", h) for h in range(HEADS)]
    HG_CORE.append(("h_n", _c))
RET_CORE = []
for _c in range(3):
    RET_CORE += [("r_a", _c)]
    RET_CORE += [("r_o", _c)] if _c != SAMPLE else [("r_s", p) for p in range(2 * HEADS)]
    RET_CORE += [("r_n", _c)]

_raw = unit_list("raw")


def with_squares(units, norm):
    out = []
    for m, item in enumerate(units):
        out += [item] + ([("square", norm, m - 1)] if m else [])
    return out + [("square", norm, len(units) - 1), ("rms", norm)]


GDN_TAIL = [("g_s", _h) for _h in range(HEADS)]
SCHEDULE = ([("scale", 0)] + _raw[0:4] + [("conv", 0)] + _raw[4:8] + [("silu", 0), ("conv", 1)] + _raw[8:12]
            + merge([("silu", 1), ("conv", 2)] + [("l2", m) for m in range(8)] + [("silu", 2)], unit_list("f_b", "z_a"))
            + unit_list("ba") + [("ba",)]
            + merge(GDN_CORE, unit_list("q_b", "i_b", "z_b", "gate_a"))
            + [("h_f",)] + GDN_TAIL + unit_list("br_a")
            + merge(HG_CORE, unit_list("q_c", "k_c", "v_c", "g_c", "gate_b")) + unit_list("br_b")
            + merge(RET_CORE, unit_list("gate_c")) + unit_list("br_c")
            + with_squares(unit_list("out"), 1) + [("scale", 1)]
            + unit_list("up") + with_squares(unit_list("down"), 0))
STAGE_NO = {}
for _item in SCHEDULE:
    STAGE_NO[_item] = sum(1 for x in STAGE_NO if x[0] == _item[0])


def nth(*item):
    return STAGE_NO[item] + 1


def trunk(nc, x_in, wpack, wba, par_in, nfin_in, lbd_in, const_in, mask_in, st_conv, st_gdn, st_hg, st_ret,
          y_out, o_conv, o_gdn_p, o_hg_p, o_ret_p, o_gdn_s, o_hg_s, o_ret_s):
    with ExitStack() as ctx:
        def sb(name, shape, dt=F32):
            return ctx.enter_context(nc.sbuf_tensor(name, shape, dt))

        all_sems = []

        def sem(name):
            s = ctx.enter_context(nc.semaphore(name))
            all_sems.append(s)
            return s

        ring = sb("ring", [P, RING, SLOT])
        x = sb("x", [P, KT, T])
        h = sb("h", [P, KT, T])
        HID = 32 * T
        arena = sb("arena", [P, HID])
        hid = arena[:, 0:32 * T].rearrange("p (m t) -> p m t", m=32)
        RAWN = 12 * RAW
        raw = arena[:, 0:RAWN].rearrange("p (m t) -> p m t", m=12)
        act = arena[:, RAWN:RAWN + 12 * T].rearrange("p (m t) -> p m t", m=12)
        _o = RAWN + 12 * T
        zA = arena[:, _o:_o + 4 * T].rearrange("p (m t) -> p m t", m=4)
        _o += 4 * T
        newc = arena[:, _o:_o + 324].rearrange("p (m b t) -> p m b t", m=12, b=9)
        gstate = arena[:, 0:4096].rearrange("p (h b v) -> p h b v", h=4, b=8)
        qC = arena[:, 0:4 * T].rearrange("p (m t) -> p m t", m=4)
        kC = arena[:, 4 * T:8 * T].rearrange("p (m t) -> p m t", m=4)
        gC = arena[:, 8 * T:16 * T].rearrange("p (m t) -> p m t", m=8)
        vC = arena[:, 16 * T:16 * T + 3072].rearrange("p (c v) -> p c v", c=3)
        merged = sb("merged", [P, KT, T])
        gate = sb("gate", [P, KT, T])
        mflat = merged[:, :, :].rearrange("p m t -> p (m t)")
        gflat = gate[:, :, :].rearrange("p m t -> p (m t)")
        CV = gflat[:, 0:4 * CONV].rearrange("p (m t) -> p m t", m=4)
        CE = mflat[:, 0:4 * CONV].rearrange("p (m t) -> p m t", m=4)
        fB = sb("fB", [P, 4, T])
        qB = sb("qB", [P, 4, T])
        kB = sb("kB", [P, 4, T])
        zB = sb("zB", [P, 4, T])
        iB = sb("iB", [P, 3, 512])
        t1, t2 = act[:, 0:4, :], act[:, 4:8, :]
        l2buf = lambda m: (kB, zB)[m // 4][:, m % 4, :]
        temp = sb("temp", [P, 2, T])
        hist = temp[:, :, :].rearrange("p a t -> p (a t)")[:, 0:288]
        cst = sb("cst", [P, NCONST])
        masks = sb("masks", [P, 15, P], U8)
        parAll = sb("parAll", [P, DEPTH, NPAR])
        par = sb("par", [P, NPAR])
        nfin = sb("nfin", [P, KT])
        lb2 = sb("lb2", [P, DEPTH, HEADS])
        wbaT = sb("wbaT", [P, 64])
        lbt = temp[:, 0, :]
        small = sb("small", [P, 160])
        rs = sb("rs", [P, T])
        eg = sb("eg", [P, 4, P])
        DT = sb("DT", [P, 4, P])
        DD = sb("DD", [P, 4, P])
        NT = sb("NT", [P, 4, P])
        XX = sb("XX", [P, 4, P])
        XT = sb("XT", [P, 4, P])
        PP = sb("PP", [P, 4, P])
        Kd = sb("Kd", [P, 4, P])
        VR = sb("VR", [P, 4, P])
        vn = sb("vn", [P, 4, P])
        qg = sb("qg", [P, 4, P])
        sq0 = sb("sq0", [P, 4, P])
        sq = (sq0, DD)
        S = sb("S", [P, 512])
        S_ret = iB[:, :, :].rearrange("p c v -> p (c v)")[:, 0:1024]
        sst = sb("sst", [P, 2, 8, P])
        _tail = [arena[:, 8192 + 1024 * i:8192 + 1024 * i + 1024] for i in range(2)]
        _own = [sst[:, i].rearrange("p b v -> p (b v)") for i in range(2)]
        _after = [z[:, :, :].rearrange("p m t -> p (m t)")[:, 0:1024] for z in (qB, kB, fB, zB)]
        hg_piece = _own + _tail
        ret_piece = _tail + _own + _after

        def by_seq(piece):
            return piece.rearrange("p (b v) -> p b v", b=SB)

        ps = ctx.enter_context(nc.psum_tensor("ps", [P, 8, 512], F32))

        def K(i):
            return ps[:, BANKS + i, :]

        def K4(i, rows, n):
            return ps[0:rows, BANKS + i, 0:4 * n].rearrange("p (h n) -> p h n", h=4)

        def C(name, rows=P):
            s, e = CST[name]
            return cst[0:rows, s:e]

        def Q(name, i=None):
            s, e = PAR[name]
            return par[:, s:e] if i is None else par[:, s + i:s + i + 1]

        ident, ones = C("ident"), C("ones")
        bab = small[:, 0:24].rearrange("p (c n) -> p c n", c=3)
        eb = small[:, 24:36].rearrange("p (c n) -> p c n", c=3)
        beta = small[:, 36:48].rearrange("p (c n) -> p c n", c=3)
        nbeta = small[:, 48:60].rearrange("p (c n) -> p c n", c=3)
        la = small[:, 60:72].rearrange("p (c n) -> p c n", c=3)
        ap_ = small[:, 72:84].rearrange("p (c n) -> p c n", c=3)
        nea = small[:, 84:88]
        gc = small[:, 88:96]
        tl = small[:, 96:100]
        egc = small[:, 100:104]
        etl = small[:, 104:108]
        nbeg = small[:, 108:112]

        def chunk(ap, c):
            t0, n = CHUNKS[c]
            return ap[:, :, t0:t0 + n]

        def up_mask(c):
            return C("upS", 64) if c == SAMPLE else C("upP")

        def over_heads(ap, rows, n):
            return ap[0:rows, None, 0:n].to_broadcast([rows, 4, n])

        def seqs(ap):
            return ap.rearrange("p m (b t) -> p m b t", b=SB)

        def blocks(ap, half):
            return ap.rearrange("p h (k t) -> p h k t", t=2 * half)

        loaded = sem("inputs_loaded")
        slot_in = [sem(f"slot{i}_loaded") for i in range(RING)]
        unit_done = sem("unit_done")
        bank_read = [sem(f"bank{i}_read") for i in range(BANKS)]
        act_seq, dve_seq, pool_seq = sem("act_seq"), sem("dve_seq"), sem("pool_seq")
        x_squared = sem("x_squared")
        sumsq_ready = sem("sumsq_ready")
        rms_ready = sem("rms_ready")
        h_ready = sem("h_ready")
        hist_loaded = sem("hist_loaded")
        hist_placed = sem("hist_placed")
        par_ready = sem("par_ready")
        wba_loaded = sem("wba_loaded")
        conv_ready = sem("conv_ready")
        conv_exp_ready = sem("conv_exp_ready")
        silu_ready = sem("silu_ready")
        l2sq_ready = sem("l2sq_ready")
        l2sum_ready = sem("l2sum_ready")
        l2rs_ready = sem("l2rs_ready")
        l2_ready = sem("l2_ready")
        adt_ready = sem("adt_ready")
        softplus_ready = sem("softplus_ready")
        ba_ready = sem("ba_ready")
        bc_ready = sem("bc_ready")
        eg_ready = sem("eg_ready")
        negb_ready = sem("negb_ready")
        ddiff_ready = sem("ddiff_ready")
        decay_ready = sem("decay_ready")
        gates_ready = sem("gates_ready")
        masked_ready = sem("masked_ready")
        qg_ready = sem("qg_ready")
        gram_ready = sem("gram_ready")
        attn_ready = sem("attn_ready")
        kdv_ready = sem("kdv_ready")
        p_ready = sem("p_ready")
        p_copied = sem("p_copied")
        z_ready = sem("z_ready")
        x_updated = sem("x_updated")
        ks_ready = sem("ks_ready")
        ks_copied = sem("ks_copied")
        ks2_ready = sem("ks2_ready")
        rhs_ready = sem("rhs_ready")
        v_ready = sem("v_ready")
        v_copied = sem("v_copied")
        o_ready = sem("o_ready")
        o_squared = sem("o_squared")
        s_updated = sem("s_updated")
        osum_ready = sem("osum_ready")
        ors_ready = sem("ors_ready")
        onormed = sem("onormed")
        g_gated = sem("g_gated")
        gst_loaded = sem("gst_loaded")
        vm_ready = sem("vm_ready")
        sstep_ready = sem("sstep_ready")
        sdecayed = sem("sdecayed")
        sst_updated = sem("sst_updated")
        f_temp1 = sem("f_temp1")
        f_temp2 = sem("f_temp2")
        f_expf = sem("f_expf")
        f_lb1 = sem("f_lb1")
        f_ready = sem("f_ready")
        h_eb_ready = sem("h_eb_ready")
        h_kdiff = sem("h_kdiff")
        h_kdexp = sem("h_kdexp")
        h_kd = sem("h_kd")
        h_qg_ready = sem("h_qg_ready")
        h_attn0 = sem("h_attn0")
        h_t_ready = sem("h_t_ready")
        h_kdT = sem("h_kdT")
        h_diag_done = sem("h_diag_done")
        h_ldiff = sem("h_ldiff")
        h_lexp = sem("h_lexp")
        h_lev_ready = sem("h_lev_ready")
        h_m_ready = sem("h_m_ready")
        h_m_read = sem("h_m_read")
        h_o_ready = sem("h_o_ready")
        h_o_squared = sem("h_o_squared")
        h_s_updated = sem("h_s_updated")
        h_osum = sem("h_osum")
        h_ors = sem("h_ors")
        h_onormed = sem("h_onormed")
        h_gated = sem("h_gated")
        h_vm = sem("h_vm")
        h_sstep = sem("h_sstep")
        h_sdec = sem("h_sdec")
        h_sst = sem("h_sst")
        r_a_ready = sem("r_a_ready")
        r_kd = sem("r_kd")
        r_attn = sem("r_attn")
        r_qg = sem("r_qg")
        r_o_ready = sem("r_o_ready")
        r_squared = sem("r_squared")
        r_s_updated = sem("r_s_updated")
        r_osum = sem("r_osum")
        r_ors = sem("r_ors")
        r_onormed = sem("r_onormed")
        r_gated = sem("r_gated")
        r_vm = sem("r_vm")
        r_sstep = sem("r_sstep")
        r_sst = sem("r_sst")
        temp_ready = sem("temp_ready")
        temp_bounded = sem("temp_bounded")
        temp_sigmoid = sem("temp_sigmoid")
        conv_bounded = sem("conv_bounded")
        conv_sigmoid = sem("conv_sigmoid")
        gates_bounded = sem("gates_bounded")
        gates_sigmoid = sem("gates_sigmoid")
        f_bounded = sem("f_bounded")
        f_sigmoid = sem("f_sigmoid")
        temp_used = sem("temp_used")
        merged_added = sem("merged_added")
        hid_ready = sem("hid_ready")
        conv_out = sem("conv_out")
        gdn_out = sem("gdn_out")
        hg_out = sem("hg_out")
        ret_out = sem("ret_out")
        hg_moved = [sem(f"hg_moved{i}") for i in range(4)]
        ret_moved = [sem(f"ret_moved{i}") for i in range(8)]
        h_old_read, r_old_read = sem("h_old_read"), sem("r_old_read")
        slots_ahead = sem("slots_ahead")
        y_ready, y_out_sem = sem("y_ready"), sem("y_stored")

        class Steps:

            def __init__(self):
                self.n = {}

            def __call__(self, q):
                self.n[q.name] = self.n.get(q.name, 0) + 1
                return self.n[q.name]

        def unit_no(u):
            return u + 1

        def bank_no(u):
            return u // BANKS + 1

        with nc.Block() as block:
            @block.sync
            def _(sp):
                sp.dma_start(x[:], x_in).then_inc(loaded, 16)
                sp.dma_start(cst[:], const_in).then_inc(loaded, 16)
                sp.dma_start(mflat[:, 0:15 * P], mask_in.rearrange("p m n -> p (m n)")).then_inc(loaded, 16)
                sp.dma_start(parAll[:], par_in).then_inc(loaded, 16)
                sp.dma_start(nfin[:], nfin_in).then_inc(loaded, 16)
                sp.dma_start(lb2[:], lbd_in).then_inc(loaded, 16)
                for s in range(AHEAD):
                    sp.dma_start(ring[:, s, :], wpack[0, s]).then_inc(slots_ahead, 16)
                sp.wait_ge(slots_ahead, 16 * AHEAD)

            @block.tensor
            def _(pe):
                pe.wait_ge(x_squared, 1)
                for kt in range(KT):
                    last = nc.tensor.matmul(K(0)[:, 0:T], ones, h[:, kt, :], start=(kt == 0), stop=(kt == KT - 1))
                last.then_inc(sumsq_ready, 1)

            @block.gpsimd
            def _(pool):
                pl = Steps()
                nc.gpsimd.memset(small[:], 0.0).then_inc(pool_seq, 1)
                pool.wait_ge(pool_seq, pl(pool_seq))

            @block.vector
            def _(dve):
                v = Steps()
                dve.wait_ge(loaded, 96)
                nc.vector.tensor_copy(masks[:].rearrange("p m n -> p (m n)"), mflat[:, 0:15 * P]).then_inc(dve_seq, 1)
                dve.wait_ge(dve_seq, v(dve_seq))
                o = {k: PAR[k][0] for k in ("llb", "nllb", "oml")}
                nc.vector.memset(parAll[:, 0, o["llb"]:o["llb"] + 4], NEG_BIG).then_inc(dve_seq, 1)
                dve.wait_ge(dve_seq, v(dve_seq))
                nc.vector.memset(parAll[:, 0, o["nllb"]:o["nllb"] + 4], -NEG_BIG).then_inc(dve_seq, 1)
                dve.wait_ge(dve_seq, v(dve_seq))
                nc.vector.memset(parAll[:, 0, o["oml"]:o["oml"] + 4], 1.0).then_inc(dve_seq, 1)
                dve.wait_ge(dve_seq, v(dve_seq))
                m, d = lbt[:, 0:4], lbt[:, 16:20]
                nc.vector.tensor_tensor(d, lb2[:, 1, :], lb2[:, 0, :], ALU.subtract).then_inc(f_temp2, 1)
                dve.wait_ge(f_temp2, v(f_temp2))
                nc.vector.tensor_scalar(m, d, 0.0, None, ALU.min).then_inc(dve_seq, 1)
                dve.wait_ge(dve_seq, v(dve_seq))
                dve.wait_ge(f_temp1, 1)
                llb = parAll[:, 1, o["llb"]:o["llb"] + 4]
                nc.vector.tensor_tensor(llb, m, lbt[:, 8:12], ALU.subtract).then_inc(dve_seq, 1)
                dve.wait_ge(dve_seq, v(dve_seq))
                nc.vector.tensor_scalar(parAll[:, 1, o["nllb"]:o["nllb"] + 4], llb, -1.0, None, ALU.mult).then_inc(dve_seq, 1)
                dve.wait_ge(dve_seq, v(dve_seq))
                nc.vector.tensor_scalar(lbt[:, 12:16], lbt[:, 4:8], 1.0, None, ALU.add).then_inc(dve_seq, 1)
                dve.wait_ge(dve_seq, v(dve_seq))
                nc.vector.reciprocal(parAll[:, 1, o["oml"]:o["oml"] + 4], lbt[:, 12:16]).then_inc(dve_seq, 1)
                dve.wait_ge(dve_seq, v(dve_seq))

            @block.scalar
            def _(a):
                s = Steps()
                a.preload_act_table_set(TABLE_SET)
                a.wait_ge(loaded, 96)
                nc.scalar.activation(h[:], x[:], ACT.Square).then_inc(x_squared, 1)
                a.wait_ge(f_temp2, 1)
                nc.scalar.activation(lbt[:, 4:8], lbt[:, 16:20], ACT.Exp).then_inc(act_seq, 1)
                a.wait_ge(act_seq, s(act_seq))
                nc.scalar.activation(lbt[:, 8:12], lbt[:, 16:20], ACT.Abs).then_inc(act_seq, 1)
                a.wait_ge(act_seq, s(act_seq))
                nc.scalar.activation(lbt[:, 8:12], lbt[:, 8:12], ACT.Exp, scale=-1.0).then_inc(act_seq, 1)
                a.wait_ge(act_seq, s(act_seq))
                nc.scalar.activation(lbt[:, 8:12], lbt[:, 8:12], ACT.Ln, bias=C("one")).then_inc(f_temp1, 1)
                a.wait_ge(sumsq_ready, 1)
                nc.scalar.activation(rs[:], K(0)[:, 0:T], ACT.Ln, bias=C("eps"), scale=1.0 / D).then_inc(act_seq, 1)
                a.wait_ge(act_seq, s(act_seq))
                nc.scalar.activation(rs[:], rs[:], ACT.Exp, scale=-0.5)
                a.wait_ge(f_temp1, s(f_temp1))

        def clear_semaphores():
            with nc.Block() as block:
                @block.gpsimd
                def _(pool):
                    pool.dma_reset()
                    for q in all_sems:
                        pool.sem_clear(q)

        clear_semaphores()

        with nc.Fori(0, DEPTH) as layer:
            with nc.Block() as block:
                @block.sync
                def _(sp):
                    sp.dma_start(wbaT[:], wba[bass.ds(layer, 1)].rearrange("a p n -> (a p) n")) \
                        .then_inc(wba_loaded, 16)
                    for s in range(AHEAD, NSLOT):
                        if s >= RING:
                            sp.wait_ge(unit_done, LAST_UNIT[s - RING] + 1)
                        sp.dma_start(ring[:, s % RING, :], wpack[bass.ds(layer, 1), s].rearrange("a p n -> (a p) n")) \
                            .then_inc(slot_in[s % RING], 16)
                    for s in range(AHEAD):
                        sp.wait_ge(unit_done, LAST_UNIT[NSLOT + s - RING] + 1)
                        sp.dma_start(ring[:, s, :], wpack[bass.ds(DEPTH - 1 - layer, 1), s].rearrange("a p n -> (a p) n")) \
                            .then_inc(slots_ahead, 16)
                    sp.wait_ge(slots_ahead, 16 * AHEAD)

                @block.tensor
                def _(pe):
                    mm = nc.tensor.matmul

                    def unit(u):
                        kind, slot, m, k = UNITS[u]
                        bank = ps[:, u % BANKS, :]
                        if u >= BANKS:
                            pe.wait_ge(bank_read[u % BANKS], u // BANKS)
                        if slot is not None:
                            if slot >= AHEAD:
                                pe.wait_ge(slot_in[slot % RING], 16 * (slot // RING + (slot % RING >= AHEAD)))
                            w = ring[:, slot % RING, :]
                        if kind == "ba":
                            pe.wait_ge(wba_loaded, 16)
                            wb = wbaT[:].rearrange("p (k n) -> p k n", k=KT)
                            for c, (t0, n) in enumerate(CHUNKS):
                                for kt in range(KT):
                                    last = mm(bank[0:n, 8 * c:8 * c + 8], h[:, kt, t0:t0 + n], wb[:, kt, :],
                                              start=(kt == 0), stop=(kt == KT - 1))
                            last.then_inc(unit_done, 1)
                            return
                        if kind in ("i_b", "v_c"):
                            t0, n = CHUNKS[m]
                            w3 = w.rearrange("p (k n) -> p k n", k=KT)
                            for kt in range(KT):
                                last = mm(bank[0:n, :], h[:, kt, t0:t0 + n], w3[:, kt, :],
                                          start=(kt == 0), stop=(kt == KT - 1))
                            last.then_inc(unit_done, 1)
                            return
                        nk, src = KT, h
                        if kind == "br_a":
                            nk, src = 4, zA
                            pe.wait_ge(g_gated, 3)
                        elif kind == "br_b":
                            nk, src = 4, zB
                            pe.wait_ge(h_gated, 3)
                        elif kind == "br_c":
                            src = gC
                            pe.wait_ge(r_gated, 3)
                        elif kind == "out":
                            src = merged
                            pe.wait_ge(merged_added, 2 * KT)
                        elif kind == "down":
                            nk, src = 32, hid
                            pe.wait_ge(hid_ready, 32)
                        elif kind == "up":
                            ready = KT
                        else:
                            ready = 0
                        w3 = w.rearrange("p (k n) -> p k n", k=nk)
                        for kt in range(nk):
                            if src is h:
                                pe.wait_ge(h_ready, ready + kt + 1)
                            last = mm(bank[:, 0:T], w3[:, kt, m * P:(m + 1) * P], src[:, kt, :],
                                      start=(kt == 0), stop=(kt == nk - 1))
                        last.then_inc(unit_done, 1)

                    def four(bank, n_out, lhs, rhs, rows):
                        for hd in range(HEADS):
                            last = mm(K4(bank, rows, n_out)[:, hd, :], lhs(hd), rhs(hd), start=True, stop=True)
                        return last

                    for item in SCHEDULE:
                        kind, args = item[0], item[1:]
                        if kind == "unit":
                            unit(args[0])
                        elif kind == "square":
                            norm, m = args
                            pe.wait_ge(x_squared, nth(*item))
                            if norm == 1 and m == 0:
                                pe.wait_ge(r_s_updated, 2)
                            last = mm(K(0)[:, 0:T], ones, h[:, m, :], start=(m == 0), stop=(m == KT - 1))
                            if m == KT - 1:
                                last.then_inc(sumsq_ready, 1)
                        elif kind == "l2":
                            m = args[0]
                            pe.wait_ge(l2sq_ready, m // 4 + 1)
                            if m >= 2:
                                pe.wait_ge(l2rs_ready, m - 1)
                            mm(K(m % 2)[:, 0:T], ones, l2buf(m), start=True, stop=True) \
                                .then_inc(l2sum_ready, 1)
                        elif kind == "g_bc":
                            c, n = args[0], CHUNKS[args[0]][1]
                            pe.wait_ge(ba_ready, 1)
                            pe.wait_ge(l2rs_ready, 8)
                            if c:
                                pe.wait_ge(onormed, c)
                                pe.wait_ge(s_updated, c)
                                pe.wait_ge(kdv_ready, c)
                            for hd in range(HEADS):
                                mm(K4(0, P, n)[:, hd, :], la[0:n, c, hd:hd + 1].to_broadcast([n, P]), up_mask(c),
                                   start=True, stop=True)
                            for hd in range(HEADS):
                                mm(K4(1, P, n)[:, hd, :], beta[0:n, c, hd:hd + 1].to_broadcast([n, P]),
                                   ident[0:n, 0:n], start=True, stop=True)
                            mm(K(2)[0:n, 0:4], up_mask(c), la[0:n, c, :], start=True, stop=True)
                            mm(K(2)[0:n, 4:8], C("sameS", 64) if c == SAMPLE else ones, la[0:n, c, :],
                               start=True, stop=True).then_inc(bc_ready, 1)
                        elif kind == "g_gram":
                            c, (t0, n) = args[0], CHUNKS[args[0]]
                            pe.wait_ge(l2_ready, 8)
                            pe.wait_ge(eg_ready, c + 1)
                            pe.wait_ge(negb_ready, c + 1)
                            pe.wait_ge(ddiff_ready, c + 1)
                            q = lambda hd: act[:, hd, t0:t0 + n]
                            k = lambda hd: act[:, 4 + hd, t0:t0 + n]
                            four(3, n, k, k, n)
                            four(4, n, k, q, n).then_inc(gram_ready, 1)
                            for hd in range(HEADS):
                                nc.tensor.transpose(K4(0, n, P)[:, hd, :], k(hd), ident)
                            for hd in range(HEADS):
                                last = nc.tensor.transpose(K4(1, n, P)[:, hd, :], act[:, 8 + hd, t0:t0 + n], ident)
                            last.then_inc(gram_ready, 1)
                        elif kind == "g_p":
                            c, n = args[0], CHUNKS[args[0]][1]
                            pe.wait_ge(attn_ready, c + 1)
                            if nth(*item) > 1:
                                pe.wait_ge(x_updated, nth(*item) - 1)
                            four(2, n, lambda hd: NT[0:n, hd, 0:n], lambda hd: XX[0:n, hd, 0:n], n).then_inc(p_ready, 1)
                        elif kind == "g_z":
                            c, n = args[0], CHUNKS[args[0]][1]
                            pe.wait_ge(p_copied, nth(*item))
                            if args[1] < levels_of(c) - 1:
                                four(3, n, lambda hd: XT[0:n, hd, 0:n], lambda hd: PP[0:n, hd, 0:n], n)
                            four(4, n, lambda hd: PP[0:n, hd, 0:n], lambda hd: XT[0:n, hd, 0:n], n).then_inc(z_ready, 1)
                        elif kind == "g_ks":
                            c, (t0, n) = args[0], CHUNKS[args[0]]
                            pe.wait_ge(kdv_ready, c + 1)
                            if c == SAMPLE:
                                pe.wait_ge(gst_loaded, 16)
                                for hd in range(HEADS):
                                    for b in range(SB):
                                        last = mm(K4(0, P, n)[:, hd, ST * b:ST * b + ST], gstate[:, hd, b, :],
                                                  act[:, 4 + hd, t0 + ST * b:t0 + ST * b + ST], start=True, stop=True)
                                last.then_inc(ks_ready, 1)
                            else:
                                four(0, P, lambda hd: act[:, 4 + hd, t0:t0 + n], lambda hd: S[:, hd * P:hd * P + P],
                                     n).then_inc(ks_ready, 1)
                        elif kind == "g_ks2":
                            pe.wait_ge(ks_copied, 1)
                            n = CHUNKS[SAMPLE][1]
                            for hd in range(HEADS):
                                last = nc.tensor.transpose(K4(0, n, P)[:, hd, :], PP[:, hd, 0:n], ident)
                            last.then_inc(ks2_ready, 1)
                        elif kind == "g_v":
                            c, n = args[0], CHUNKS[args[0]][1]
                            pe.wait_ge(kdv_ready, c + 1)
                            pe.wait_ge(x_updated, sum(levels_of(i) - 1 for i in range(c + 1)))
                            if c:
                                pe.wait_ge(rhs_ready, c)
                            four(1, P, lambda hd: XT[0:n, hd, 0:n], lambda hd: VR[0:n, hd, :], n).then_inc(v_ready, 1)
                        elif kind in ("g_o", "h_o"):
                            c, n = args[0], CHUNKS[args[0]][1]
                            gdn = kind == "g_o"
                            if gdn:
                                pe.wait_ge(v_copied, c + 1)
                                pe.wait_ge(qg_ready, c + 1)
                                if c == SAMPLE:
                                    pe.wait_ge(gst_loaded, 16)
                            else:
                                pe.wait_ge(h_m_read, sum(levels_of(i) for i in range(c + 1)))
                                pe.wait_ge(h_qg_ready, c + 1)
                                pe.wait_ge(h_kdT, c + 1)
                                pe.wait_ge(onormed, 3)
                                if c:
                                    pe.wait_ge(h_onormed, c)
                            val = (lambda hd: vn[0:n, hd, :]) if gdn else (lambda hd: iB[0:n, c, hd * P:hd * P + P])
                            for hd in range(HEADS):
                                o = K4(2, P, n)[:, hd, :]
                                last = mm(o, val(hd), DT[0:n, hd, 0:n], start=True, stop=(c == 0))
                                if c == 1:
                                    last = mm(o, S[:, hd * P:hd * P + P], qg[:, hd, :], start=False, stop=True)
                                if c == SAMPLE:
                                    for b in range(SB):
                                        t = slice(ST * b, ST * b + ST)
                                        last = mm(o[:, t], gstate[:, hd, b, :], qg[:, hd, t], start=False, stop=(b == SB - 1))
                            if c != SAMPLE:
                                for hd in range(HEADS):
                                    last = mm(K4(3, P, P)[:, hd, :], Kd[0:n, hd, :], val(hd), start=True, stop=True)
                            last.then_inc(o_ready if gdn else h_o_ready, 1)
                        elif kind in ("g_n", "h_n"):
                            c, n = args[0], CHUNKS[args[0]][1]
                            pe.wait_ge((o_squared if kind == "g_n" else h_o_squared), c + 1)
                            if kind == "h_n" and c:
                                pe.wait_ge(h_s_updated, min(c, 2))
                            if kind == "h_n" and c == SAMPLE:
                                pe.wait_ge(h_sst, HEADS)
                            mm(K(4)[:, 0:4 * n], ones, sq[0][:].rearrange("p h n -> p (h n)")[:, 0:4 * n], start=True, stop=True) \
                                .then_inc(osum_ready if kind == "g_n" else h_osum, 1)
                        elif kind == "g_s":
                            hd = args[0]
                            pe.wait_ge(vm_ready, hd + 1)
                            if hd == 1:
                                pe.wait_ge(ors_ready, 3)
                            if hd > 1:
                                pe.wait_ge(sst_updated, hd - 1)
                            for g in range(2):
                                r = slice(32 * g, 32 * g + 32)
                                last = mm(K(3 * (hd % 2) + g), Kd[r, hd, :], (PP, XT)[hd % 2][r, :, :], start=True, stop=True)
                            last.then_inc(sstep_ready, 1)
                        elif kind == "h_t":
                            c, (t0, n) = args[0], CHUNKS[args[0]]
                            pe.wait_ge(h_kd, c + 1)
                            pe.wait_ge(sst_updated, HEADS)
                            if c:
                                pe.wait_ge(h_diag_done, c)
                                pe.wait_ge(h_kdT, c)
                            for hd in range(HEADS):
                                nc.tensor.transpose(K4(0, n, P)[:, hd, :], DD[:, hd, 0:n], ident)
                            four(1, n, lambda hd: kB[:, hd, t0:t0 + n], lambda hd: qB[:, hd, t0:t0 + n], n).then_inc(h_t_ready, 1)
                        elif kind == "h_m":
                            c, n, lv = args[0], CHUNKS[args[0]][1], nth(*item)
                            pe.wait_ge(h_lev_ready, lv)
                            if lv > 2:
                                pe.wait_ge(h_m_read, lv - 2)
                            if lv == 1:
                                pe.wait_ge(s_updated, 2)
                            if lv > 1:
                                pe.wait_ge(h_diag_done, c + 1)
                            if c and args[1] == 0:
                                pe.wait_ge(h_s_updated, c)
                                pe.wait_ge(h_ors, c)
                            buf = (NT, XX)[lv % 2]
                            four(3 + lv % 2, n, lambda hd: buf[:, hd, 0:n], lambda hd: buf[:, hd, 0:n], n).then_inc(h_m_ready, 1)
                        elif kind == "h_s":
                            hd, n = args[0], CHUNKS[SAMPLE][1]
                            pe.wait_ge(hg_moved[hd], 16)
                            pe.wait_ge(h_m_read, sum(levels_of(i) for i in range(3)))
                            pe.wait_ge(h_qg_ready, 3)
                            pe.wait_ge(h_kdT, 3)
                            pe.wait_ge(h_onormed, 2)
                            o = K4(2, P, n)[:, hd, :]
                            mm(o, iB[0:n, SAMPLE, hd * P:hd * P + P], DT[0:n, hd, 0:n], start=True, stop=False)
                            for b in range(SB):
                                t = slice(ST * b, ST * b + ST)
                                last = mm(o[:, t], by_seq(hg_piece[hd])[:, b, :], qg[:, hd, t], start=False, stop=(b == SB - 1))
                            last.then_inc(h_old_read, 1)
                            pe.wait_ge(h_vm, hd + 1)
                            if hd > 1:
                                pe.wait_ge(h_sst, hd - 1)
                            for g in range(2):
                                r = slice(32 * g, 32 * g + 32)
                                last = mm(K(3 * (hd % 2) + g), Kd[r, hd, :], (PP, XT)[hd % 2][r, :, :], start=True, stop=True)
                            last.then_inc(h_sstep, 1)
                        elif kind == "r_a":
                            c, (t0, n) = args[0], CHUNKS[args[0]]
                            if c == 0:
                                pe.wait_ge(bank_read[UNIT_AT["k_c", 3] % BANKS], UNIT_AT["k_c", 3] // BANKS + 1)
                                pe.wait_ge(temp_used, ROT_NO[UNIT_AT["k_c", 3]] + 1)
                                pe.wait_ge(h_sst, HEADS)
                            else:
                                pe.wait_ge(r_s_updated, c)
                                pe.wait_ge(r_ors, c)
                            for hd in range(HEADS):
                                nc.tensor.transpose(K4(0, n, P)[:, hd, :], kC[:, hd, t0:t0 + n], ident)
                            four(1, n, lambda hd: kC[:, hd, t0:t0 + n], lambda hd: qC[:, hd, t0:t0 + n], n).then_inc(r_a_ready, 1)
                        elif kind == "r_o":
                            c, n = args[0], CHUNKS[args[0]][1]
                            pe.wait_ge(r_kd, c + 1)
                            pe.wait_ge(r_attn, c + 1)
                            pe.wait_ge(r_qg, c + 1)
                            pe.wait_ge(h_onormed, 3)
                            pe.wait_ge(h_ors, 3)
                            if c:
                                pe.wait_ge(r_onormed, c)
                            for f in range(2):
                                for hd in range(HEADS):
                                    o = K4(2 + f, P, n)[:, hd, :]
                                    v = slice(hd * DV_RET + f * P, hd * DV_RET + f * P + P)
                                    last = mm(o, vC[0:n, c, v], DT[0:n, hd, 0:n], start=True, stop=(c == 0))
                                    if c:
                                        mm(o, S_ret[:, v], qg[:, hd, :], start=False, stop=True)
                            for hd in range(HEADS):
                                b = (4, 0)[hd // 2]
                                last = mm(K(b)[:, (hd % 2) * DV_RET:(hd % 2 + 1) * DV_RET], Kd[0:n, hd, :],
                                          vC[0:n, c, hd * DV_RET:(hd + 1) * DV_RET], start=True, stop=True)
                            last.then_inc(r_o_ready, 1)
                        elif kind == "r_s":
                            p_, n = args[0], CHUNKS[SAMPLE][1]
                            hd, f = p_ // 2, p_ % 2
                            pe.wait_ge(ret_moved[p_], 16)
                            pe.wait_ge(r_kd, 3)
                            pe.wait_ge(r_attn, 3)
                            pe.wait_ge(r_qg, 3)
                            pe.wait_ge(r_onormed, 2)
                            o = K4(2 + f, P, n)[:, hd, :]
                            v = slice(hd * DV_RET + f * P, hd * DV_RET + f * P + P)
                            mm(o, vC[0:n, SAMPLE, v], DT[0:n, hd, 0:n], start=True, stop=False)
                            for b in range(SB):
                                t = slice(ST * b, ST * b + ST)
                                last = mm(o[:, t], by_seq(ret_piece[p_])[:, b, :], qg[:, hd, t], start=False, stop=(b == SB - 1))
                            last.then_inc(r_old_read, 1)
                            pe.wait_ge(r_vm, p_ + 1)
                            if p_:
                                pe.wait_ge(r_sst, p_)
                            for g, b in ((0, 4), (1, 0)):
                                r = slice(32 * g, 32 * g + 32)
                                last = mm(K(b), Kd[r, hd, :], (PP, XT)[p_ % 2][r, :, :], start=True, stop=True)
                            last.then_inc(r_sstep, 1)
                        elif kind == "r_n":
                            c, n = args[0], CHUNKS[args[0]][1]
                            pe.wait_ge(r_squared, c + 1)
                            for f in range(2):
                                last = mm(K(1)[:, 0:4 * n], ones, sq[f][:].rearrange("p h n -> p (h n)")[:, 0:4 * n],
                                          start=(f == 0), stop=(f == 1))
                            last.then_inc(r_osum, 1)

                @block.scalar
                def _(a):
                    s = Steps()
                    fn = nc.scalar.activation
                    a.preload_act_table_set(TABLE_SET)

                    def sigmoid_of(z):
                        fn(z, z, ACT.Ln).then_inc(act_seq, 1)
                        a.wait_ge(act_seq, s(act_seq))
                        return fn(z, z, ACT.Exp, scale=-1.0)

                    def rsqrt_of(out, src, scale, bias=None):
                        fn(out, src, ACT.Ln, bias=C("eps"), scale=scale).then_inc(act_seq, 1)
                        a.wait_ge(act_seq, s(act_seq))
                        return fn(out, out, ACT.Exp, scale=-0.5, bias=C("zero") if bias is None else bias)

                    for item in SCHEDULE:
                        kind, args = item[0], item[1:]
                        if kind == "square":
                            norm, m = args
                            u = UNIT_AT["out" if norm else "down", m]
                            a.wait_ge(bank_read[u % BANKS], bank_no(u))
                            if m == 0:
                                a.wait_ge(unit_done, unit_no(UNIT_AT["gate_c", 7] if norm else UNIT_AT["up", 31]))
                            fn(h[:, m, :], x[:, m, :], ACT.Square).then_inc(x_squared, 1)
                        elif kind == "rms":
                            a.wait_ge(sumsq_ready, nth(*item))
                            rsqrt_of(rs[:], K(0)[:, 0:T], 1.0 / D).then_inc(rms_ready, 1)
                        elif kind == "unit":
                            u = args[0]
                            k, slot, m, i = UNITS[u]
                            bank = ps[:, u % BANKS, :]
                            if k in ("raw", "f_b", "i_b", "v_c", "gate_a", "gate_b", "gate_c", "up", "q_c", "k_c") \
                                    or k in SILU_KINDS:
                                a.wait_ge(unit_done, unit_no(u))
                            if k == "raw":
                                fn(raw[:, i, HIST:RAW_P], bank[:, 0:SEQ], ACT.Copy).then_inc(act_seq, 1)
                                a.wait_ge(act_seq, s(act_seq))
                                fn(raw[:, i, RAW_P:].rearrange("p (b t) -> p b t", b=SB)[:, :, HIST:],
                                               bank[:, SEQ:T].rearrange("p (b t) -> p b t", b=SB), ACT.Copy).then_inc(bank_read[u % BANKS], 1)
                                a.wait_ge(bank_read[u % BANKS], bank_no(u))
                            elif k == "f_b":
                                fn(fB[:, i, :], bank[:, 0:T], ACT.Copy).then_inc(bank_read[u % BANKS], 1)
                                a.wait_ge(bank_read[u % BANKS], bank_no(u))
                            elif k == "i_b":
                                n = CHUNKS[m][1]
                                fn(iB[0:n, m, :], bank[0:n, :], ACT.Copy).then_inc(bank_read[u % BANKS], 1)
                                a.wait_ge(bank_read[u % BANKS], bank_no(u))
                            elif k == "v_c":
                                n, half = CHUNKS[m][1], i // 3
                                a.wait_ge(unit_done, unit_no(UNIT_AT["br_a", 7]))
                                a.wait_ge(gdn_out, 32)
                                fn(vC[0:n, m, 512 * half:512 * half + 512], bank[0:n, :], ACT.Copy).then_inc(bank_read[u % BANKS], 1)
                                a.wait_ge(bank_read[u % BANKS], bank_no(u))
                            elif k in SILU_KINDS or k in ("q_c", "k_c"):
                                j = TEMP_ORDER[u]
                                if j >= 2:
                                    before = TEMP_UNITS[j - 2]
                                    if before in SILU_NO:
                                        a.wait_ge(bank_read[before % BANKS], bank_no(before))
                                    else:
                                        a.wait_ge(temp_used, ROT_NO[before] + 1)
                                if k in SILU_KINDS:
                                    fn(temp[:, j % 2, :], bank[:, 0:T], ACT.Exp, scale=-1.0).then_inc(temp_ready, 1)
                                    a.wait_ge(temp_bounded, SILU_NO[u] + 1)
                                    sigmoid_of(temp[:, j % 2, :]).then_inc(temp_sigmoid, 1)
                                else:
                                    fn(temp[0:64, j % 2, :], bank[64:P, 0:T], ACT.Copy).then_inc(act_seq, 1)
                                    a.wait_ge(act_seq, s(act_seq))
                                    fn(temp[64:P, j % 2, :], bank[0:64, 0:T], ACT.Copy).then_inc(temp_ready, 1)
                                    a.wait_ge(temp_ready, s(temp_ready))
                            elif k in ("gate_a", "gate_b", "gate_c"):
                                if k == "gate_a":
                                    a.wait_ge(silu_ready, 3)
                                elif k == "gate_b":
                                    a.wait_ge(bank_read[(UNIT_AT["br_a", i]) % BANKS], bank_no(UNIT_AT["br_a", i]))
                                else:
                                    a.wait_ge(merged_added, i + 1)
                                fn(gate[:, i, :], bank[:, 0:T], ACT.Exp, scale=-1.0).then_inc(bank_read[u % BANKS], 1)
                                a.wait_ge(bank_read[u % BANKS], bank_no(u))
                            elif k in ("br_a", "br_b", "br_c") and i == 0:
                                a.wait_ge(gates_bounded, "abc".index(k[3]) + 1)
                                sigmoid_of(gate[:]).then_inc(gates_sigmoid, 1)
                            elif k == "up":
                                if i == 0:
                                    a.wait_ge(unit_done, unit_no(UNIT_AT["br_c", 7]))
                                if i * T <= 8192 < (i + 1) * T:
                                    a.wait_ge(ret_moved[0], 32)
                                    a.wait_ge(ret_moved[1], 32)
                                fn(hid[:, i, :], bank[:, 0:T], ACT.Relu).then_inc(bank_read[u % BANKS], 1)
                                a.wait_ge(bank_read[u % BANKS], bank_no(u))
                        elif kind == "conv":
                            g = args[0]
                            a.wait_ge(conv_ready, g + 1)
                            fn(CE[:], CV[:], ACT.Exp, scale=-1.0).then_inc(conv_exp_ready, 1)
                            a.wait_ge(conv_exp_ready, s(conv_exp_ready))
                        elif kind == "silu":
                            a.wait_ge(conv_bounded, args[0] + 1)
                            sigmoid_of(CE[:]).then_inc(conv_sigmoid, 1)
                        elif kind == "l2":
                            m = args[0]
                            a.wait_ge(l2sum_ready, m + 1)
                            rsqrt_of(l2buf(m), K(m % 2)[:, 0:T], 1.0, C("lnq") if m < 4 else None).then_inc(l2rs_ready, 1)
                            a.wait_ge(l2rs_ready, s(l2rs_ready))
                        elif kind == "ba":
                            a.wait_ge(adt_ready, 1)
                            fn(nea, Q("alog"), ACT.Exp).then_inc(act_seq, 1)
                            a.wait_ge(act_seq, s(act_seq))
                            fn(eb, bab[:, :, 0:4], ACT.Exp, scale=-1.0).then_inc(act_seq, 1)
                            a.wait_ge(act_seq, s(act_seq))
                            fn(la, ap_, ACT.Abs).then_inc(act_seq, 1)
                            a.wait_ge(act_seq, s(act_seq))
                            fn(la, la, ACT.Exp, scale=-1.0).then_inc(act_seq, 1)
                            a.wait_ge(act_seq, s(act_seq))
                            fn(la, la, ACT.Ln, bias=C("one")).then_inc(softplus_ready, 1)
                            a.wait_ge(softplus_ready, s(softplus_ready))
                        elif kind == "g_bc":
                            c, (t0, n) = args[0], CHUNKS[args[0]]
                            a.wait_ge(bc_ready, c + 1)
                            if c:
                                a.wait_ge(s_updated, c)
                                a.wait_ge(g_gated, c)
                            fn(eg[:, :, 0:n], K4(0, P, n), ACT.Exp).then_inc(eg_ready, 1)
                            a.wait_ge(eg_ready, s(eg_ready))
                            fn(NT[0:n, :, 0:n], K4(1, P, n)[0:n], ACT.Copy, scale=-1.0).then_inc(negb_ready, 1)
                            a.wait_ge(negb_ready, s(negb_ready))
                            a.wait_ge(ddiff_ready, c + 1)
                            fn(egc[0:n], gc[0:n, 0:4], ACT.Exp).then_inc(act_seq, 1)
                            a.wait_ge(act_seq, s(act_seq))
                            fn(etl[0:n], tl[0:n], ACT.Exp).then_inc(act_seq, 1)
                            a.wait_ge(act_seq, s(act_seq))
                            fn(DD[0:n, :, 0:n], DD[0:n, :, 0:n], ACT.Exp, scale=-1.0).then_inc(act_seq, 1)
                            a.wait_ge(act_seq, s(act_seq))
                            fn(DT[0:n, :, 0:n], DT[0:n, :, 0:n], ACT.Exp).then_inc(decay_ready, 1)
                            a.wait_ge(decay_ready, s(decay_ready))
                        elif kind == "g_gram":
                            c, n = args[0], CHUNKS[args[0]][1]
                            a.wait_ge(gram_ready, 2 * (c + 1))
                            for hd in range(HEADS):
                                fn(Kd[0:n, hd, :], K4(0, n, P)[:, hd, :], ACT.Copy, scale=etl[0:n, hd:hd + 1]).then_inc(act_seq, 1)
                                a.wait_ge(act_seq, s(act_seq))
                                last = fn(VR[0:n, hd, :], K4(1, n, P)[:, hd, :], ACT.Copy, scale=beta[0:n, c, hd:hd + 1])
                                if hd < HEADS - 1:
                                    last.then_inc(act_seq, 1)
                                    a.wait_ge(act_seq, s(act_seq))
                            last.then_inc(kdv_ready, 1)
                            a.wait_ge(kdv_ready, s(kdv_ready))
                        elif kind == "g_p":
                            n = CHUNKS[args[0]][1]
                            a.wait_ge(p_ready, nth(*item))
                            fn(PP[0:n, :, 0:n], K4(2, n, n), ACT.Copy).then_inc(p_copied, 1)
                            a.wait_ge(p_copied, s(p_copied))
                        elif kind == "g_ks" and args[0] == SAMPLE:
                            a.wait_ge(ks_ready, 2)
                            fn(PP[:, :, 0:64], K4(0, P, 64), ACT.Copy).then_inc(ks_copied, 1)
                            a.wait_ge(ks_copied, s(ks_copied))
                        elif kind == "g_v":
                            c, n = args[0], CHUNKS[args[0]][1]
                            a.wait_ge(v_ready, c + 1)
                            fn(vn[0:n], K4(1, n, P), ACT.Copy).then_inc(v_copied, 1)
                            a.wait_ge(v_copied, s(v_copied))
                        elif kind in ("g_o", "h_o"):
                            c, n = args[0], CHUNKS[args[0]][1]
                            gdn = kind == "g_o"
                            a.wait_ge((o_ready if gdn else h_o_ready), c + 1)
                            fn(sq[0][:].rearrange("p h n -> p (h n)")[:, 0:4 * n], K(2)[:, 0:4 * n], ACT.Square).then_inc((o_squared if gdn else h_o_squared), 1)
                            a.wait_ge((o_squared if gdn else h_o_squared), s((o_squared if gdn else h_o_squared)))
                        elif kind in ("g_n", "h_n"):
                            c, n = args[0], CHUNKS[args[0]][1]
                            gdn = kind == "g_n"
                            a.wait_ge((osum_ready if gdn else h_osum), c + 1)
                            rsqrt_of(sq[0][:].rearrange("p h n -> p (h n)")[:, 0:4 * n], K(4)[:, 0:4 * n], 1.0 / P).then_inc((ors_ready if gdn else h_ors), 1)
                            a.wait_ge((ors_ready if gdn else h_ors), s((ors_ready if gdn else h_ors)))
                        elif kind == "h_f":
                            a.wait_ge(l2_ready, 8)
                            a.wait_ge(ks_ready, 2)
                            a.wait_ge(qg_ready, 3)
                            fn(kB[:], fB[:], ACT.Exp).then_inc(f_expf, 1)
                            fn(t1, fB[:], ACT.Abs).then_inc(act_seq, 1)
                            a.wait_ge(act_seq, s(act_seq))
                            fn(t1, t1, ACT.Exp, scale=-1.0).then_inc(act_seq, 1)
                            a.wait_ge(act_seq, s(act_seq))
                            fn(t1, t1, ACT.Ln, bias=C("one")).then_inc(act_seq, 1)
                            a.wait_ge(act_seq, s(act_seq))
                            for hd in range(HEADS):
                                fn(t2[:, hd, :], fB[:, hd, :], ACT.Abs, bias=Q("nllb", hd)).then_inc(act_seq, 1)
                                a.wait_ge(act_seq, s(act_seq))
                            fn(t2, t2, ACT.Exp, scale=-1.0).then_inc(act_seq, 1)
                            a.wait_ge(act_seq, s(act_seq))
                            fn(t2, t2, ACT.Ln, bias=C("one")).then_inc(f_lb1, 1)
                            a.wait_ge(f_bounded, 1)
                            sigmoid_of(kB[:]).then_inc(f_sigmoid, 1)
                        elif kind == "h_e":
                            c, n = args[0], CHUNKS[args[0]][1]
                            a.wait_ge(f_ready, 1)
                            if c:
                                a.wait_ge(h_s_updated, c)
                            else:
                                a.wait_ge(sdecayed, HEADS)
                            fn(eg[:, :, 0:n], chunk(fB, c), ACT.Exp).then_inc(h_eb_ready, 1)
                            a.wait_ge(h_eb_ready, s(h_eb_ready))
                            a.wait_ge(h_kdiff, c + 1)
                            fn(DD[:, :, 0:n], DD[:, :, 0:n], ACT.Exp).then_inc(h_kdexp, 1)
                            a.wait_ge(h_kdexp, s(h_kdexp))
                        elif kind == "h_t":
                            c, n = args[0], CHUNKS[args[0]][1]
                            a.wait_ge(h_t_ready, c + 1)
                            fn(Kd[0:n], K4(0, n, P), ACT.Copy).then_inc(h_kdT, 1)
                            a.wait_ge(h_kdT, s(h_kdT))
                        elif kind == "h_l":
                            c, n, lv = args[0], CHUNKS[args[0]][1], nth(*item)
                            buf = (NT, XX)[lv % 2]
                            a.wait_ge(h_ldiff, lv)
                            fn(buf[:, :, 0:n], buf[:, :, 0:n], ACT.Exp).then_inc(h_lexp, 1)
                            a.wait_ge(h_lexp, s(h_lexp))
                        elif kind == "h_s" and args[0] == HEADS - 1:
                            a.wait_ge(h_sstep, HEADS)
                            fn(sq[0][:].rearrange("p h n -> p (h n)")[:, 0:256], K(2)[:, 0:256], ACT.Square).then_inc(h_o_squared, 1)
                            a.wait_ge(h_o_squared, s(h_o_squared))
                        elif kind == "r_a":
                            c, n = args[0], CHUNKS[args[0]][1]
                            a.wait_ge(r_a_ready, c + 1)
                            tail = C("tailS", 64) if c == SAMPLE else C("tailP")
                            for hd in range(HEADS):
                                last = fn(Kd[0:n, hd, :], K4(0, n, P)[:, hd, :], ACT.Copy, scale=tail[:, hd:hd + 1])
                                if hd < HEADS - 1:
                                    last.then_inc(act_seq, 1)
                                    a.wait_ge(act_seq, s(act_seq))
                            last.then_inc(r_kd, 1)
                            a.wait_ge(r_kd, s(r_kd))
                        elif kind == "r_o" or (kind == "r_s" and args[0] == 7):
                            c = args[0] if kind == "r_o" else SAMPLE
                            n = CHUNKS[c][1]
                            if kind == "r_o":
                                a.wait_ge(r_o_ready, c + 1)
                            else:
                                a.wait_ge(r_sstep, 8)
                            fn(sq[0][:].rearrange("p h n -> p (h n)")[:, 0:4 * n], K(2)[:, 0:4 * n], ACT.Square).then_inc(act_seq, 1)
                            a.wait_ge(act_seq, s(act_seq))
                            fn(sq[1][:].rearrange("p h n -> p (h n)")[:, 0:4 * n], K(3)[:, 0:4 * n], ACT.Square).then_inc(r_squared, 1)
                            a.wait_ge(r_squared, s(r_squared))
                        elif kind == "r_n":
                            c, n = args[0], CHUNKS[args[0]][1]
                            a.wait_ge(r_osum, c + 1)
                            rsqrt_of(XX[:].rearrange("p h n -> p (h n)")[:, 0:4 * n], K(1)[:, 0:4 * n], 1.0 / DV_RET).then_inc(r_ors, 1)
                            a.wait_ge(r_ors, s(r_ors))

                @block.vector
                def _(dve):
                    v = Steps()
                    tt, ts, stt = nc.vector.tensor_tensor, nc.vector.tensor_scalar, nc.vector.scalar_tensor_tensor
                    nc.vector.tensor_copy(par[:], parAll[:, bass.ds(layer, 1), :].rearrange("p a n -> p (a n)")).then_inc(par_ready, 1)
                    dve.wait_ge(par_ready, v(par_ready))

                    def state_piece(S3, lo, hi, hd=None):
                        tt(S3[:, 0:4, :], S3[:, 0:4, :], lo, ALU.add).then_inc(dve_seq, 1)
                        dve.wait_ge(dve_seq, v(dve_seq))
                        return tt(S3[:, 4:8, :], S3[:, 4:8, :], hi, ALU.add)

                    def fourb(ap):
                        return ap.rearrange("p (b v) -> p b v", b=4)

                    for item in SCHEDULE:
                        kind, args = item[0], item[1:]
                        if kind == "scale":
                            norm = args[0]
                            if norm:
                                dve.wait_ge(rms_ready, 1)
                                dve.wait_ge(sumsq_ready, 1)
                            for kt in range(KT):
                                stt(h[:, kt, :], x[:, kt, :], Q("nf" if norm else "nm", kt), rs[:], ALU.mult, ALU.mult) \
                                    .then_inc(h_ready, 1)
                        elif kind == "unit":
                            u = args[0]
                            k, slot, m, i = UNITS[u]
                            bank = ps[:, u % BANKS, :]
                            if k == "ba":
                                dve.wait_ge(unit_done, unit_no(u))
                                nc.vector.tensor_copy(bab[:, 0:2, :], bank[:, 0:16].rearrange("p (c n) -> p c n", c=2)).then_inc(dve_seq, 1)
                                dve.wait_ge(dve_seq, v(dve_seq))
                                nc.vector.tensor_copy(bab[0:64, 2, :], bank[0:64, 16:24]).then_inc(bank_read[u % BANKS], 1)
                                dve.wait_ge(bank_read[u % BANKS], bank_no(u))
                            elif k in SILU_KINDS:
                                j = TEMP_ORDER[u]
                                dve.wait_ge(temp_ready, j + 1)
                                tm = temp[:, j % 2, :]
                                ts(tm, tm, EXP_BOUND, 1.0, ALU.min, ALU.add).then_inc(temp_bounded, 1)
                                dve.wait_ge(temp_sigmoid, SILU_NO[u] + 1)
                                if k == "q_b" and i == 0:
                                    dve.wait_ge(l2_ready, 8)
                                if k == "z_b" and i == 0:
                                    dve.wait_ge(l2_ready, 8)
                                dst = {"z_a": zA, "z_b": zB, "q_b": qB, "g_c": gC}[k][:, i, :]
                                stt(dst, bank[:, 0:T], P ** -0.5 if k == "q_b" else 1.0, tm,
                                                ALU.mult, ALU.mult).then_inc(bank_read[u % BANKS], 1)
                                dve.wait_ge(bank_read[u % BANKS], bank_no(u))
                            elif k in ("q_c", "k_c"):
                                j = TEMP_ORDER[u]
                                dve.wait_ge(temp_ready, j + 1)
                                if i == 0:
                                    dve.wait_ge(unit_done, unit_no(UNIT_AT["br_a", 7]))
                                    dve.wait_ge(gdn_out, 32)
                                dst = (qC if k == "q_c" else kC)[:, i, :]
                                sc = 1.0 if k == "q_c" else P ** -0.5
                                tm = temp[:, j % 2, :]
                                stt(dst, bank[:, 0:T], sc, C("cos"), ALU.mult, ALU.mult).then_inc(bank_read[u % BANKS], 1)
                                dve.wait_ge(bank_read[u % BANKS], bank_no(u))
                                stt(tm, tm, sc, C("sin"), ALU.mult, ALU.mult).then_inc(dve_seq, 1)
                                dve.wait_ge(dve_seq, v(dve_seq))
                                tt(dst, dst, tm, ALU.add).then_inc(temp_used, 1)
                                dve.wait_ge(temp_used, v(temp_used))
                            elif k in ("br_a", "br_b", "br_c"):
                                g = gate[:, i, :]
                                if i == 0:
                                    first = UNIT_AT["gate_" + k[3], 0]
                                    for b in range(BANKS):
                                        dve.wait_ge(bank_read[(first + 5 + b) % BANKS], bank_no(first + 5 + b))
                                    ts(gate[:], gate[:], EXP_BOUND, 1.0, ALU.min, ALU.add).then_inc(gates_bounded, 1)
                                    dve.wait_ge(gates_sigmoid, "abc".index(k[3]) + 1)
                                dve.wait_ge(unit_done, unit_no(u))
                                tt(merged[:, i, :] if k == "br_a" else g, bank[:, 0:T], g, ALU.mult).then_inc(bank_read[u % BANKS], 1)
                                dve.wait_ge(bank_read[u % BANKS], bank_no(u))
                            elif k in ("out", "down"):
                                dve.wait_ge(unit_done, unit_no(u))
                                tt(x[:, i, :], x[:, i, :], bank[:, 0:T], ALU.add).then_inc(bank_read[u % BANKS], 1)
                                dve.wait_ge(bank_read[u % BANKS], bank_no(u))
                        elif kind == "conv":
                            g = args[0]
                            for b in range(BANKS):
                                dve.wait_ge(bank_read[(UNIT_AT["raw", 4 * g + 1 + b]) % BANKS], bank_no(UNIT_AT["raw", 4 * g + 1 + b]))
                            dve.wait_ge(hist_placed, 2)
                            if g:
                                dve.wait_ge(conv_exp_ready, g)
                            for mm_ in range(4):
                                m = 4 * g + mm_
                                for j in range(4):
                                    w = Q("cw", 12 * j + m)
                                    if j == 0:
                                        last = ts(CV[:, mm_, :], raw[:, m, 0:CONV], w, None, ALU.mult)
                                    else:
                                        last = stt(CV[:, mm_, :], raw[:, m, j:j + CONV], w, CV[:, mm_, :], ALU.mult, ALU.add)
                                    if (mm_, j) != (3, 3):
                                        last.then_inc(dve_seq, 1)
                                        dve.wait_ge(dve_seq, v(dve_seq))
                            last.then_inc(conv_ready, 1)
                            dve.wait_ge(conv_ready, v(conv_ready))
                        elif kind == "silu":
                            g = args[0]
                            dve.wait_ge(conv_exp_ready, g + 1)
                            ts(CE[:], CE[:], EXP_BOUND, 1.0, ALU.min, ALU.add).then_inc(conv_bounded, 1)
                            dve.wait_ge(conv_sigmoid, g + 1)
                            tt(act[:, 4 * g:4 * g + 4, 0:SEQ], CV[:, :, 0:SEQ], CE[:, :, 0:SEQ], ALU.mult).then_inc(dve_seq, 1)
                            dve.wait_ge(dve_seq, v(dve_seq))
                            o, w, t8 = RAW_P, RAW_S * (SB - 1), ST * (SB - 1)
                            strip = lambda z: z[:, :, o:o + w].rearrange("p m (b t) -> p m b t", t=RAW_S)[:, :, :, 0:ST]
                            own = act[:, 4 * g:4 * g + 4, SEQ:]
                            tt(own[:, :, 0:t8].rearrange("p m (b t) -> p m b t", t=ST), strip(CV), strip(CE),
                                      ALU.mult).then_inc(dve_seq, 1)
                            dve.wait_ge(dve_seq, v(dve_seq))
                            tt(own[:, :, t8:], CV[:, :, o + w:], CE[:, :, o + w:], ALU.mult).then_inc(silu_ready, 1)
                            dve.wait_ge(silu_ready, v(silu_ready))
                        elif kind == "ba":
                            dt = Q("dt")[:, None, :].to_broadcast([P, 3, 4])
                            tt(ap_, bab[:, :, 4:8], dt, ALU.add).then_inc(adt_ready, 1)
                            dve.wait_ge(adt_ready, v(adt_ready))
                            dve.wait_ge(softplus_ready, 1)
                            stt(la, ap_, 0.0, la, ALU.max, ALU.add).then_inc(dve_seq, 1)
                            dve.wait_ge(dve_seq, v(dve_seq))
                            ts(nea, nea, -1.0, None, ALU.mult).then_inc(dve_seq, 1)
                            dve.wait_ge(dve_seq, v(dve_seq))
                            tt(la, la, nea[:, None, :].to_broadcast([P, 3, 4]), ALU.mult).then_inc(dve_seq, 1)
                            dve.wait_ge(dve_seq, v(dve_seq))
                            ts(eb, eb, 1.0, None, ALU.add).then_inc(dve_seq, 1)
                            dve.wait_ge(dve_seq, v(dve_seq))
                            nc.vector.reciprocal(beta, eb).then_inc(dve_seq, 1)
                            dve.wait_ge(dve_seq, v(dve_seq))
                            ts(nbeta, beta, -1.0, None, ALU.mult).then_inc(ba_ready, 1)
                            dve.wait_ge(ba_ready, v(ba_ready))
                        elif kind == "g_bc":
                            c, n = args[0], CHUNKS[args[0]][1]
                            dve.wait_ge(bc_ready, c + 1)
                            if c:
                                dve.wait_ge(v_copied, c)
                                dve.wait_ge(g_gated, c)
                            nc.vector.tensor_copy(gc[0:n], K(2)[0:n, 0:8]).then_inc(dve_seq, 1)
                            dve.wait_ge(dve_seq, v(dve_seq))
                            tt(tl[0:n], gc[0:n, 4:8], gc[0:n, 0:4], ALU.subtract).then_inc(dve_seq, 1)
                            dve.wait_ge(dve_seq, v(dve_seq))
                            dve.wait_ge(eg_ready, c + 1)
                            for hd in range(HEADS):
                                g = gc[0:n, hd:hd + 1]
                                G = K4(0, P, n)[0:n, hd, :]
                                ts(DT[0:n, hd, 0:n], G, g, g, ALU.min, ALU.subtract).then_inc(dve_seq, 1)
                                dve.wait_ge(dve_seq, v(dve_seq))
                                last = ts(DD[0:n, hd, 0:n], G, g, g, ALU.max, ALU.subtract)
                                if hd < HEADS - 1:
                                    last.then_inc(dve_seq, 1)
                                    dve.wait_ge(dve_seq, v(dve_seq))
                            last.then_inc(ddiff_ready, 1)
                            dve.wait_ge(ddiff_ready, v(ddiff_ready))
                            dve.wait_ge(decay_ready, c + 1)
                            tt(nbeg[0:n], nbeta[0:n, c, :], egc[0:n], ALU.mult).then_inc(gates_ready, 1)
                            dve.wait_ge(gates_ready, v(gates_ready))
                        elif kind == "g_gram":
                            c, n = args[0], CHUNKS[args[0]][1]
                            dve.wait_ge(gram_ready, 2 * c + 1)
                            dve.wait_ge(masked_ready, c + 1)
                            for hd in range(HEADS):
                                stt(DD[0:n, hd, 0:n], K4(3, n, n)[:, hd, :], nbeta[0:n, c, hd:hd + 1],
                                           DD[0:n, hd, 0:n], ALU.mult, ALU.mult).then_inc(dve_seq, 1)
                                dve.wait_ge(dve_seq, v(dve_seq))
                            tt(NT[0:n, :, 0:n], K4(3, n, n), NT[0:n, :, 0:n], ALU.mult).then_inc(dve_seq, 1)
                            dve.wait_ge(dve_seq, v(dve_seq))
                            tt(DT[0:n, :, 0:n], K4(4, n, n), DT[0:n, :, 0:n], ALU.mult).then_inc(dve_seq, 1)
                            dve.wait_ge(dve_seq, v(dve_seq))
                            idn = over_heads(ident, n, n)
                            nc.vector.tensor_copy(XX[0:n, :, 0:n], idn).then_inc(dve_seq, 1)
                            dve.wait_ge(dve_seq, v(dve_seq))
                            nc.vector.tensor_copy(XT[0:n, :, 0:n], idn).then_inc(dve_seq, 1)
                            dve.wait_ge(dve_seq, v(dve_seq))
                            nc.vector.copy_predicated(XX[0:n, :, 0:n], over_heads(masks[:, 8, :], n, n),
                                                             DD[0:n, :, 0:n]).then_inc(dve_seq, 1)
                            dve.wait_ge(dve_seq, v(dve_seq))
                            nc.vector.copy_predicated(XT[0:n, :, 0:n], over_heads(masks[:, 0, :], n, n),
                                                             NT[0:n, :, 0:n]).then_inc(attn_ready, 1)
                            dve.wait_ge(attn_ready, v(attn_ready))
                        elif kind == "g_z":
                            c, n, lv = args[0], CHUNKS[args[0]][1], args[1]
                            dve.wait_ge(z_ready, nth(*item))
                            if lv < levels_of(c) - 1:
                                nc.vector.copy_predicated(XX[0:n, :, 0:n], over_heads(masks[:, 8 + lv, :], n, n), K4(3, n, n))
                            nc.vector.copy_predicated(XT[0:n, :, 0:n], over_heads(masks[:, lv, :], n, n),
                                                             K4(4, n, n)).then_inc(x_updated, 1)
                            dve.wait_ge(x_updated, v(x_updated))
                        elif (kind == "g_ks" and args[0] == 1) or kind == "g_ks2":
                            c, n = args[0], CHUNKS[args[0]][1]
                            dve.wait_ge(kdv_ready, c + 1)
                            if c == SAMPLE:
                                dve.wait_ge(ks2_ready, 1)
                            else:
                                dve.wait_ge(ks_ready, 1)
                            for hd in range(HEADS):
                                last = stt(VR[0:n, hd, :], K4(0, n, P)[:, hd, :], nbeg[0:n, hd:hd + 1], VR[0:n, hd, :],
                                           ALU.mult, ALU.add)
                                if hd < HEADS - 1:
                                    last.then_inc(dve_seq, 1)
                                    dve.wait_ge(dve_seq, v(dve_seq))
                            last.then_inc(rhs_ready, 1)
                            dve.wait_ge(rhs_ready, v(rhs_ready))
                        elif kind in ("g_o", "h_o"):
                            c, n = args[0], CHUNKS[args[0]][1]
                            gdn = kind == "g_o"
                            dve.wait_ge((o_ready if gdn else h_o_ready), c + 1)
                            if c == SAMPLE:
                                continue
                            if not gdn and c == 0:
                                dve.wait_ge(gdn_out, 32)
                            for hd in range(HEADS):
                                Sh = S[:, hd * P:hd * P + P]
                                if c == 0:
                                    last = nc.vector.tensor_copy(Sh, K4(3, P, P)[:, hd, :])
                                else:
                                    last = stt(Sh, Sh, eg[:, hd, n - 1:n], K4(3, P, P)[:, hd, :], ALU.mult, ALU.add)
                                if hd < HEADS - 1:
                                    last.then_inc(dve_seq, 1)
                                    dve.wait_ge(dve_seq, v(dve_seq))
                            last.then_inc((s_updated if gdn else h_s_updated), 1)
                            dve.wait_ge((s_updated if gdn else h_s_updated), v((s_updated if gdn else h_s_updated)))
                        elif kind in ("g_n", "h_n"):
                            c, n = args[0], CHUNKS[args[0]][1]
                            gdn = kind == "g_n"
                            dve.wait_ge((ors_ready if gdn else h_ors), c + 1)
                            flat = lambda z: z.rearrange("p h n -> p (h n)")[:, 0:4 * n]
                            stt(flat(XT[:]), K(2)[:, 0:4 * n], Q("gn" if gdn else "hn"), flat(sq[0][:]),
                                       ALU.mult, ALU.mult).then_inc((onormed if gdn else h_onormed), 1)
                            dve.wait_ge((onormed if gdn else h_onormed), v((onormed if gdn else h_onormed)))
                        elif kind == "g_s":
                            hd = args[0]
                            dve.wait_ge(sstep_ready, hd + 1)
                            dve.wait_ge(sdecayed, hd + 1)
                            state_piece(gstate[:, hd], fourb(K(3 * (hd % 2))), fourb(K(3 * (hd % 2) + 1))).then_inc(sst_updated, 1)
                            dve.wait_ge(sst_updated, v(sst_updated))
                        elif kind == "h_f":
                            dve.wait_ge(f_expf, 1)
                            ts(kB[:], kB[:], EXP_BOUND, 1.0, ALU.min, ALU.add).then_inc(f_bounded, 1)
                            dve.wait_ge(f_lb1, 1)
                            tt(t2, t2, t1, ALU.subtract).then_inc(dve_seq, 1)
                            dve.wait_ge(dve_seq, v(dve_seq))
                            ts(t1, fB[:], 0.0, None, ALU.min).then_inc(dve_seq, 1)
                            dve.wait_ge(dve_seq, v(dve_seq))
                            for hd in range(HEADS):
                                stt(fB[:, hd, :], t1[:, hd, :], Q("llb", hd), fB[:, hd, :], ALU.add, ALU.subtract).then_inc(dve_seq, 1)
                                dve.wait_ge(dve_seq, v(dve_seq))
                            tt(fB[:], fB[:], t1, ALU.max).then_inc(dve_seq, 1)
                            dve.wait_ge(dve_seq, v(dve_seq))
                            tt(t1, fB[:], t2, ALU.add).then_inc(dve_seq, 1)
                            dve.wait_ge(dve_seq, v(dve_seq))
                            dve.wait_ge(f_sigmoid, 1)
                            for hd in range(HEADS):
                                ts(kB[:, hd, :], kB[:, hd, :], Q("oml", hd), None, ALU.mult).then_inc(dve_seq, 1)
                                dve.wait_ge(dve_seq, v(dve_seq))
                            for hd in range(HEADS):
                                last = nc.vector.tensor_tensor_scan(fB[:, hd, :], C("reset"), t1[:, hd, :], 0.0,
                                                                    ALU.mult, ALU.add)
                                if hd < HEADS - 1:
                                    last.then_inc(dve_seq, 1)
                                    dve.wait_ge(dve_seq, v(dve_seq))
                            last.then_inc(f_ready, 1)
                            dve.wait_ge(f_ready, v(f_ready))
                        elif kind == "h_e":
                            c, n = args[0], CHUNKS[args[0]][1]
                            b = chunk(fB, c)
                            if c:
                                dve.wait_ge(h_t_ready, c)
                            if c == SAMPLE:
                                b3 = seqs(b)
                                last = tt(seqs(DD[:, :, 0:n]), b3[:, :, :, ST - 1:ST].to_broadcast([P, 4, SB, ST]), b3,
                                          ALU.subtract)
                            else:
                                last = tt(DD[:, :, 0:n], b[:, :, n - 1:n].to_broadcast([P, 4, n]), b, ALU.subtract)
                            last.then_inc(h_kdiff, 1)
                            dve.wait_ge(h_kdiff, v(h_kdiff))
                        elif kind == "h_l":
                            c, n, lv = args[0], CHUNKS[args[0]][1], nth(*item)
                            hf = LEVELS[args[1]]
                            buf = (NT, XX)[lv % 2]
                            if lv > 2:
                                dve.wait_ge(h_m_ready, lv - 2)
                            b, o = blocks(chunk(fB, c), hf), blocks(buf[:, :, 0:n], hf)
                            ref = b[:, :, :, hf - 1:hf].to_broadcast([P, 4, n // (2 * hf), hf])
                            tt(o[:, :, :, 0:hf], ref, b[:, :, :, 0:hf], ALU.subtract).then_inc(dve_seq, 1)
                            dve.wait_ge(dve_seq, v(dve_seq))
                            tt(o[:, :, :, hf:], b[:, :, :, hf:], ref, ALU.subtract).then_inc(h_ldiff, 1)
                            dve.wait_ge(h_ldiff, v(h_ldiff))
                        elif kind == "h_t":
                            c, n = args[0], CHUNKS[args[0]][1]
                            dve.wait_ge(h_attn0, c + 1)
                            dve.wait_ge(h_t_ready, c + 1)
                            nc.vector.copy_predicated(DT[0:n, :, 0:n], over_heads(masks[:, DIAG, :], n, n),
                                                             K4(1, n, n)).then_inc(h_diag_done, 1)
                            dve.wait_ge(h_diag_done, v(h_diag_done))
                        elif kind == "h_m":
                            c, n, lv = args[0], CHUNKS[args[0]][1], nth(*item)
                            dve.wait_ge(h_m_ready, lv)
                            nc.vector.copy_predicated(DT[0:n, :, 0:n], over_heads(masks[:, args[1], :], n, n),
                                                             K4(3 + lv % 2, n, n)).then_inc(h_m_read, 1)
                            dve.wait_ge(h_m_read, v(h_m_read))
                        elif kind == "h_s":
                            hd = args[0]
                            dve.wait_ge(h_sstep, hd + 1)
                            dve.wait_ge(h_sdec, hd + 1)
                            state_piece(by_seq(hg_piece[hd]), fourb(K(3 * (hd % 2))), fourb(K(3 * (hd % 2) + 1))).then_inc(h_sst, 1)
                            dve.wait_ge(h_sst, v(h_sst))
                        elif kind == "r_a":
                            c, n = args[0], CHUNKS[args[0]][1]
                            dve.wait_ge(r_a_ready, c + 1)
                            dm = C("dmS", 64) if c == SAMPLE else C("dmP")
                            tt(DT[0:n, :, 0:n], K4(1, n, n), dm.rearrange("p (h n) -> p h n", h=4), ALU.mult).then_inc(r_attn, 1)
                            dve.wait_ge(r_attn, v(r_attn))
                        elif kind == "r_o":
                            c, n = args[0], CHUNKS[args[0]][1]
                            dve.wait_ge(r_o_ready, c + 1)
                            if c == 0:
                                dve.wait_ge(hg_out, 16)
                            for hd in range(HEADS):
                                Sh = S_ret[:, hd * DV_RET:(hd + 1) * DV_RET]
                                src = K((4, 0)[hd // 2])[:, (hd % 2) * DV_RET:(hd % 2 + 1) * DV_RET]
                                if c == 0:
                                    last = nc.vector.tensor_copy(Sh, src)
                                else:
                                    last = stt(Sh, Sh, GAMMA[hd] ** n, src, ALU.mult, ALU.add)
                                if hd < HEADS - 1:
                                    last.then_inc(dve_seq, 1)
                                    dve.wait_ge(dve_seq, v(dve_seq))
                            last.then_inc(r_s_updated, 1)
                            dve.wait_ge(r_s_updated, v(r_s_updated))
                        elif kind == "r_s":
                            p_ = args[0]
                            dve.wait_ge(r_sstep, p_ + 1)
                            dec = GAMMA[p_ // 2] ** ST
                            for g, b in ((0, 4), (1, 0)):
                                S3 = by_seq(ret_piece[p_])[:, 4 * g:4 * g + 4, :]
                                last = stt(S3, S3, dec, fourb(K(b)), ALU.mult, ALU.add)
                                if g == 0:
                                    last.then_inc(dve_seq, 1)
                                    dve.wait_ge(dve_seq, v(dve_seq))
                            last.then_inc(r_sst, 1)
                            dve.wait_ge(r_sst, v(r_sst))
                        elif kind == "r_n":
                            c, n = args[0], CHUNKS[args[0]][1]
                            dve.wait_ge(r_ors, c + 1)
                            flat = lambda z: z.rearrange("p h n -> p (h n)")[:, 0:4 * n]
                            tt(flat(XT[:]), K(2)[:, 0:4 * n], flat(XX[:]), ALU.mult).then_inc(dve_seq, 1)
                            dve.wait_ge(dve_seq, v(dve_seq))
                            tt(flat(NT[:]), K(3)[:, 0:4 * n], flat(XX[:]), ALU.mult).then_inc(r_onormed, 1)
                            dve.wait_ge(r_onormed, v(r_onormed))

                @block.gpsimd
                def _(pool):
                    pl = Steps()
                    tt = nc.gpsimd.tensor_tensor

                    def per_layer(ap):
                        return ap[bass.ds(layer, 1)].rearrange("a p n -> (a p) n")

                    def spread(vals, to):
                        return tt(to[0:64, :, :], vals[:, None, :].to_broadcast([64, 4, P]),
                                  C("seqm", 64)[:, :, None].to_broadcast([64, 4, P]), ALU.mult)

                    def store_hg(i):
                        pool.wait_ge(h_sst, i + 1)
                        pool.dma_start(o_hg_s[bass.ds(layer, 1), i].rearrange("a p n -> (a p) n"), hg_piece[i]) \
                            .then_inc(hg_moved[i], 16)

                    def store_ret(i):
                        pool.wait_ge(r_sst, i + 1)
                        pool.dma_start(o_ret_s[bass.ds(layer, 1), i].rearrange("a p n -> (a p) n"), ret_piece[i]) \
                            .then_inc(ret_moved[i], 16)

                    pool.dma_start(hist, per_layer(st_conv)).then_inc(hist_loaded, 16)
                    nc.gpsimd.memset(raw[:, :, 0:HIST], 0.0).then_inc(hist_placed, 1)
                    pool.wait_ge(hist_placed, pl(hist_placed))
                    pool.wait_ge(hist_loaded, 16)
                    for b in range(SB):
                        o = RAW_P + RAW_S * b
                        last = nc.gpsimd.tensor_copy(raw[:, :, o:o + HIST],
                                                     hist.rearrange("p (m b t) -> p m b t", m=12, b=SB)[:, :, b, :])
                        if b < SB - 1:
                            last.then_inc(pool_seq, 1)
                            pool.wait_ge(pool_seq, pl(pool_seq))
                    last.then_inc(hist_placed, 1)
                    pool.wait_ge(hist_placed, pl(hist_placed))
                    for item in SCHEDULE:
                        kind, args = item[0], item[1:]
                        if kind == "unit":
                            u = args[0]
                            k, slot, m, i = UNITS[u]
                            if k in ("br_b", "br_c"):
                                pool.wait_ge(bank_read[u % BANKS], bank_no(u))
                                tt(merged[:, i, :], merged[:, i, :], gate[:, i, :], ALU.add).then_inc(merged_added, 1)
                                pool.wait_ge(merged_added, pl(merged_added))
                            elif k == "up":
                                pool.wait_ge(bank_read[u % BANKS], bank_no(u))
                                tt(hid[:, i, :], hid[:, i, :], hid[:, i, :], ALU.mult).then_inc(hid_ready, 1)
                                pool.wait_ge(hid_ready, pl(hid_ready))
                        elif kind == "silu":
                            g = args[0]
                            pool.wait_ge(silu_ready, g + 1)
                            if g < 2:
                                sqr = (kB, zB)[g]
                                part = act[:, 4 * g:4 * g + 4, :]
                                tt(sqr[:], part, part, ALU.mult).then_inc(l2sq_ready, 1)
                            else:
                                for b in range(9):
                                    o = SEQ if b == 0 else RAW_P + RAW_S * (b - 1) + ST
                                    nc.gpsimd.tensor_copy(newc[:, :, b, :], raw[:, :, o:o + HIST]).then_inc(pool_seq, 1)
                                    pool.wait_ge(pool_seq, pl(pool_seq))
                                pool.dma_start(per_layer(o_conv), newc.rearrange("p m b t -> p (m b t)")) \
                                    .then_inc(conv_out, 16)
                                pool.dma_start(arena[:, 0:4096], per_layer(st_gdn)).then_inc(gst_loaded, 16)
                        elif kind == "l2":
                            m = args[0]
                            pool.wait_ge(l2rs_ready, m + 1)
                            tt(act[:, m, :], act[:, m, :], l2buf(m), ALU.mult).then_inc(l2_ready, 1)
                            pool.wait_ge(l2_ready, pl(l2_ready))
                        elif kind == "g_bc":
                            c, (t0, n) = args[0], CHUNKS[args[0]]
                            pool.wait_ge(decay_ready, c + 1)
                            pool.wait_ge(l2_ready, 8)
                            pool.wait_ge(negb_ready, c + 1)
                            tt(DT[0:n, :, 0:n], DT[0:n, :, 0:n], over_heads(up_mask(c), n, n), ALU.mult).then_inc(pool_seq, 1)
                            pool.wait_ge(pool_seq, pl(pool_seq))
                            tt(NT[0:n, :, 0:n], NT[0:n, :, 0:n], DT[0:n, :, 0:n], ALU.mult).then_inc(masked_ready, 1)
                            pool.wait_ge(masked_ready, pl(masked_ready))
                            tt(qg[:, :, 0:n], act[:, 0:4, t0:t0 + n], eg[:, :, 0:n], ALU.mult).then_inc(qg_ready, 1)
                            pool.wait_ge(qg_ready, pl(qg_ready))
                        elif kind in ("g_n", "h_n"):
                            c, (t0, n) = args[0], CHUNKS[args[0]]
                            gdn = kind == "g_n"
                            pool.wait_ge((onormed if gdn else h_onormed), c + 1)
                            z = zA if gdn else zB
                            if gdn and c == 0:
                                for b in range(1, 4):
                                    pool.wait_ge(bank_read[(UNIT_AT["z_a", b]) % BANKS], bank_no(UNIT_AT["z_a", b]))
                            if not gdn and c == 0:
                                for b in range(1, 4):
                                    pool.wait_ge(bank_read[(UNIT_AT["z_b", b]) % BANKS], bank_no(UNIT_AT["z_b", b]))
                            xt = XT[:].rearrange("p h n -> p (h n)")[:, 0:4 * n].rearrange("p (h n) -> p h n", h=4)
                            tt(z[:, :, t0:t0 + n], z[:, :, t0:t0 + n], xt, ALU.mult).then_inc((g_gated if gdn else h_gated), 1)
                            pool.wait_ge((g_gated if gdn else h_gated), pl((g_gated if gdn else h_gated)))
                            if c == 1 and gdn:
                                pool.wait_ge(s_updated, 2)
                                pool.dma_start(per_layer(o_gdn_p), S[:, 0:512]).then_inc(gdn_out, 16)
                                pool.wait_ge(gdn_out, 16)
                            if c == 1 and not gdn:
                                pool.wait_ge(h_s_updated, 2)
                                pool.dma_start(per_layer(o_hg_p), S[:, 0:512]).then_inc(hg_out, 16)
                        elif kind == "g_s":
                            hd = args[0]
                            if hd == 0:
                                pool.wait_ge(o_ready, 3)
                            if hd > 1:
                                pool.wait_ge(sstep_ready, hd - 1)
                            spread(vn[0:64, hd, :], (PP, XT)[hd % 2]).then_inc(vm_ready, 1)
                            dec = eg[:, hd, 0:64].rearrange("p (b t) -> p b t", b=SB)[:, :, ST - 1:ST]
                            tt(gstate[:, hd], gstate[:, hd], dec.to_broadcast([P, SB, P]), ALU.mult).then_inc(sdecayed, 1)
                            if hd == HEADS - 1:
                                pool.wait_ge(sst_updated, HEADS)
                                pool.dma_start(per_layer(o_gdn_s), arena[:, 0:4096]).then_inc(gdn_out, 16)
                        elif kind == "h_e":
                            c, (t0, n) = args[0], CHUNKS[args[0]]
                            pool.wait_ge(h_eb_ready, c + 1)
                            if c == 0:
                                for b in range(1, 4):
                                    pool.wait_ge(bank_read[(UNIT_AT["q_b", b]) % BANKS], bank_no(UNIT_AT["q_b", b]))
                                pool.wait_ge(f_ready, 1)
                                pool.wait_ge(unit_done, unit_no(UNIT_AT["br_a", 7]))
                                pool.wait_ge(gdn_out, 32)
                                for i in range(HEADS):
                                    pool.dma_start(hg_piece[i], st_hg[bass.ds(layer, 1), i].rearrange("a p n -> (a p) n")) \
                                        .then_inc(hg_moved[i], 16)
                            tt(qg[:, :, 0:n], qB[:, :, t0:t0 + n], eg[:, :, 0:n], ALU.mult).then_inc(h_qg_ready, 1)
                            pool.wait_ge(h_qg_ready, pl(h_qg_ready))
                            nc.gpsimd.memset(DT[0:n, :, 0:n], 0.0).then_inc(h_attn0, 1)
                            pool.wait_ge(h_attn0, pl(h_attn0))
                            pool.wait_ge(h_kdexp, c + 1)
                            tt(DD[:, :, 0:n], DD[:, :, 0:n], kB[:, :, t0:t0 + n], ALU.mult).then_inc(h_kd, 1)
                            pool.wait_ge(h_kd, pl(h_kd))
                        elif kind == "h_l":
                            c, (t0, n), lv = args[0], CHUNKS[args[0]], nth(*item)
                            hf = LEVELS[args[1]]
                            buf = (NT, XX)[lv % 2]
                            pool.wait_ge(h_lexp, lv)
                            o, q, k = blocks(buf[:, :, 0:n], hf), blocks(chunk(qB, c), hf), blocks(chunk(kB, c), hf)
                            tt(o[:, :, :, 0:hf], o[:, :, :, 0:hf], k[:, :, :, 0:hf], ALU.mult).then_inc(pool_seq, 1)
                            pool.wait_ge(pool_seq, pl(pool_seq))
                            tt(o[:, :, :, hf:], o[:, :, :, hf:], q[:, :, :, hf:], ALU.mult).then_inc(h_lev_ready, 1)
                            pool.wait_ge(h_lev_ready, pl(h_lev_ready))
                        elif kind == "h_s":
                            hd = args[0]
                            if hd > 1:
                                pool.wait_ge(h_sstep, hd - 1)
                            spread(iB[0:64, SAMPLE, hd * P:hd * P + P], (PP, XT)[hd % 2]).then_inc(h_vm, 1)
                            pool.wait_ge(h_old_read, hd + 1)
                            dec = eg[:, hd, 0:64].rearrange("p (b t) -> p b t", b=SB)[:, :, ST - 1:ST]
                            Sp = by_seq(hg_piece[hd])
                            tt(Sp, Sp, dec.to_broadcast([P, SB, P]), ALU.mult).then_inc(h_sdec, 1)
                            if hd:
                                store_hg(hd - 1)
                            if hd == HEADS - 1:
                                store_hg(hd)
                        elif kind == "r_a":
                            c, (t0, n) = args[0], CHUNKS[args[0]]
                            pool.wait_ge(temp_used, ROT_NO[UNIT_AT["k_c", 3]] + 1)
                            if c:
                                pool.wait_ge(r_s_updated, c)
                            inn = C("innS") if c == SAMPLE else C("innP")
                            tt(qg[:, :, 0:n], qC[:, :, t0:t0 + n], inn.rearrange("p (h n) -> p h n", h=4), ALU.mult).then_inc(r_qg, 1)
                            pool.wait_ge(r_qg, pl(r_qg))
                            if c == 0:
                                for i in range(HEADS):
                                    pool.wait_ge(hg_moved[i], 32)
                                pool.wait_ge(h_gated, 3)
                                pool.wait_ge(unit_done, unit_no(UNIT_AT["br_b", 7]))
                                for i in range(2 * HEADS):
                                    pool.dma_start(ret_piece[i], st_ret[bass.ds(layer, 1), i].rearrange("a p n -> (a p) n")) \
                                        .then_inc(ret_moved[i], 16)
                        elif kind == "r_s":
                            p_ = args[0]
                            hd, f = p_ // 2, p_ % 2
                            if p_ > 1:
                                pool.wait_ge(r_sstep, p_ - 1)
                            spread(vC[0:64, SAMPLE, hd * DV_RET + f * P:hd * DV_RET + f * P + P], (PP, XT)[p_ % 2]).then_inc(r_vm, 1)
                            if p_:
                                store_ret(p_ - 1)
                            if p_ == 2 * HEADS - 1:
                                store_ret(p_)
                        elif kind == "r_n":
                            c, (t0, n) = args[0], CHUNKS[args[0]]
                            pool.wait_ge(r_onormed, c + 1)
                            if c == 0:
                                for b in range(5, 8):
                                    pool.wait_ge(bank_read[(UNIT_AT["g_c", b]) % BANKS], bank_no(UNIT_AT["g_c", b]))
                            for f, src in enumerate((XT, NT)):
                                z = gC.rearrange("p (h f) t -> p h f t", f=2)[:, :, f, t0:t0 + n]
                                sv = src[:].rearrange("p h n -> p (h n)")[:, 0:4 * n].rearrange("p (h n) -> p h n", h=4)
                                last = tt(z, z, sv, ALU.mult)
                                if f == 0:
                                    last.then_inc(pool_seq, 1)
                                    pool.wait_ge(pool_seq, pl(pool_seq))
                            last.then_inc(r_gated, 1)
                            pool.wait_ge(r_gated, pl(r_gated))
                            if c == 1:
                                pool.wait_ge(r_s_updated, 2)
                                pool.dma_start(per_layer(o_ret_p), S_ret) \
                                    .then_inc(ret_out, 16)
                    pool.wait_ge(conv_out, 16)
                    pool.wait_ge(gdn_out, 32)
                    pool.wait_ge(hg_out, 16)
                    pool.wait_ge(ret_out, 16)
                    pool.wait_ge(gst_loaded, 16)
                    for i in range(HEADS):
                        pool.wait_ge(hg_moved[i], 32)
                    for i in range(2 * HEADS):
                        pool.wait_ge(ret_moved[i], 32)
            clear_semaphores()

        with nc.Block() as block:
            @block.vector
            def _(dve):
                for kt in range(KT):
                    nc.vector.scalar_tensor_tensor(h[:, kt, :], x[:, kt, :], nfin[:, kt:kt + 1], rs[:], ALU.mult,
                                                   ALU.mult).then_inc(y_ready, 1)

            @block.sync
            def _(sp):
                for kt in range(0, KT, 2):
                    sp.wait_ge(y_ready, kt + 2)
                    sp.dma_start(y_out[:, kt:kt + 2, :], h[:, kt:kt + 2, :]).then_inc(y_out_sem, 16)
                sp.wait_ge(y_out_sem, 8 * KT)


_OUTS = (("y", (P, KT, T)), ("o_conv", (DEPTH, P, 324)), ("o_gdn_p", (DEPTH, P, 512)), ("o_hg_p", (DEPTH, P, 512)),
         ("o_ret_p", (DEPTH, P, 1024)), ("o_gdn_s", (DEPTH, P, 4096)), ("o_hg_s", (DEPTH, 4, P, 1024)),
         ("o_ret_s", (DEPTH, 8, P, 1024)))


def _slots(w, k_tiles):
    return w.reshape(k_tiles, P, -1).transpose(1, 0, 2).reshape(P, -1)


def kernel(**inputs):
    import numpy as _np
    import concourse.bacc as _bacc
    from concourse import mybir as _mybir
    from concourse.bass_utils import run_bass_kernel_spmd as _run

    a = {k: _np.asarray(v) for k, v in inputs.items()}
    f = _np.float32

    def features(z):
        z = z.reshape(z.shape[:-1] + (-1, P))
        return _np.moveaxis(z, -1, 0)

    x = _np.concatenate([a["x_prompt"].reshape(SEQ, D), a["x_sample"].reshape(SB * ST, D)])
    pack = _np.empty((DEPTH, NSLOT, P, SLOT), f)
    for l in range(DEPTH):
        for s, name in enumerate(SLOT_NAMES):
            if name in W_IN_COLUMN:
                c = W_IN_COLUMN[name]
                pack[l, s] = _slots(a["w_in"][l][:, c:c + 512], 8)
            elif name in ("br_a", "br_b"):
                pack[l, s] = _slots(a["w_br_gdn" if name == "br_a" else "w_br_hgrn"][l], 4)
            elif name.startswith("down"):
                i = int(name[4:])
                pack[l, s] = _slots(a["w_down"][l][:, P * i:P * i + P], 32)
            else:
                i = int(name[-1])
                w = {"b": "w_br_ret", "o": "w_out", "u": "w_up"}[name[0]]
                pack[l, s] = _slots(a[w][l][:, 512 * i:512 * i + 512], 8)
    wba = _np.stack([_slots(a["w_in"][l][:, BA_COLUMN:BA_COLUMN + 8], 8) for l in range(DEPTH)])
    par = _np.zeros((P, DEPTH, NPAR), f)

    def put(name, z):
        s, e = PAR[name]
        par[:, :, s:e] = z

    put("nm", features(a["norm_mix"]))
    put("nf", features(a["norm_ffn"]))
    put("cw", features(a["gdn_conv"]).reshape(P, DEPTH, 48))
    put("gn", features(a["gdn_norm"]))
    put("hn", features(a["hgrn_norm"]))
    put("alog", a["gdn_a_log"][None])
    put("dt", a["gdn_dt_bias"][None])
    lb = features(a["hgrn_lb"])
    const, mask = shape_constants()
    arrays = {
        "x_in": _np.ascontiguousarray(x.T.reshape(KT, P, T).transpose(1, 0, 2)),
        "wpack": pack, "wba": wba, "par": par, "nfin": _np.ascontiguousarray(features(a["norm_final"])),
        "lb": _np.ascontiguousarray(lb), "const_in": const, "mask_in": mask,
        "st_conv": _np.ascontiguousarray(
            a["state_gdn_conv"].reshape(DEPTH, SB, HIST, 12, P).transpose(0, 4, 3, 1, 2).reshape(DEPTH, P, 288)),
        "st_gdn": _np.ascontiguousarray(a["state_gdn"].transpose(0, 3, 2, 1, 4).reshape(DEPTH, P, 4096)),
        "st_hg": _np.ascontiguousarray(a["state_hgrn"].transpose(0, 2, 3, 1, 4).reshape(DEPTH, 4, P, 1024)),
        "st_ret": _np.ascontiguousarray(
            a["state_ret"].reshape(DEPTH, SB, 4, P, 2, P).transpose(0, 2, 4, 3, 1, 5).reshape(DEPTH, 8, P, 1024)),
    }
    nc = _bacc.Bacc("TRN2", target_bir_lowering=False, num_devices=1)
    args = [nc.dram_tensor("d_" + k, z.shape, _mybir.dt.from_np(z.dtype), kind="ExternalInput").ap() for k, z in arrays.items()]
    args += [nc.dram_tensor(k, s, _mybir.dt.float32, kind="ExternalOutput").ap() for k, s in _OUTS]
    trunk(nc, *args)
    r = _run(nc, [{"d_" + k: z for k, z in arrays.items()}], core_ids=[0]).results[0]
    y = r["y"].transpose(1, 0, 2).reshape(D, T).T
    cv = r["o_conv"].reshape(DEPTH, P, 12, 9, HIST).transpose(0, 3, 4, 2, 1).reshape(DEPTH, 9, HIST, 12 * P)

    def prompt_state(z, dv):
        return _np.ascontiguousarray(z.reshape(DEPTH, P, 4, dv).transpose(0, 2, 1, 3)[:, None])

    out = (y[:SEQ].reshape(1, SEQ, D), y[SEQ:].reshape(SB, ST, D),
           prompt_state(r["o_gdn_p"], P), cv[:, 0:1], prompt_state(r["o_hg_p"], P), prompt_state(r["o_ret_p"], DV_RET),
           r["o_gdn_s"].reshape(DEPTH, P, 4, SB, P).transpose(0, 3, 2, 1, 4), cv[:, 1:],
           r["o_hg_s"].reshape(DEPTH, 4, P, SB, P).transpose(0, 3, 1, 2, 4),
           r["o_ret_s"].reshape(DEPTH, 4, 2, P, SB, P).transpose(0, 4, 1, 3, 2, 5).reshape(DEPTH, SB, 4, P, DV_RET))
    return tuple(_np.ascontiguousarray(z) for z in out)
```

```python
import math
from contextlib import ExitStack

import numpy as np

import concourse.bass as bass
from concourse import mybir
from concourse.alu_op_type import AluOpType as ALU

ACT = mybir.ActivationFunctionType
F32 = mybir.dt.float32
U8 = mybir.dt.uint8

P = 128
DEPTH = 2
D = 1024
KT = D // P
SEQ, SB, ST = 256, 8, 8
T = SEQ + SB * ST
HEADS = 4
DV_RET = 256
D_FF = 4 * D
EPS = 1e-6
POOL_LOW = 5
PAST = 2048
CHUNKS = ((0, P), (P, P), (SEQ, SB * ST))
SAMPLE = 2
HIST = 3
RAW_P = HIST + SEQ
RAW_S = HIST + ST
RAW = RAW_P + SB * RAW_S
CONV = RAW - HIST
CV_RING = 6
LEVELS = (1, 2, 4, 8, 16, 32, 64)
DIAG = 7
NEG_BIG = -1e30

SLOT = 4096
PIECE = SLOT // 4
RING = 6
AHEAD = 4
SPLIT_RING = 3
SLOT_NAMES = (["q_a", "k_a", "v_a", "f_b", "z_a", "q_b", "i_b", "z_b", "gate_a0", "gate_a1", "br_a", "q_c", "k_c",
               "v_c0", "v_c1", "g_c0", "g_c1", "gate_b0", "gate_b1", "br_b", "gate_c0", "gate_c1", "br_c0", "br_c1",
               "out0", "out1"] + [f"up{i}" for i in range(8)] + [f"down{i}" for i in range(8)])
NSLOT = len(SLOT_NAMES)
NPIECE = 4 * NSLOT
W_IN_COLUMN = {"q_a": 0, "k_a": 512, "v_a": 1024, "z_a": 1536, "q_b": 2056, "f_b": 2568, "i_b": 3080, "z_b": 3592,
               "q_c": 4104, "k_c": 4616, "v_c0": 5128, "v_c1": 5640, "g_c0": 6152, "g_c1": 6664,
               "gate_a0": 7176, "gate_a1": 7688, "gate_b0": 8200, "gate_b1": 8712, "gate_c0": 9224, "gate_c1": 9736}
BA_COLUMN = 2048

PAR = {}
NPAR = 0
for _name, _n in (("nm", 8), ("nf", 8), ("cw", 48), ("gn", 1), ("hn", 1), ("alog", 4), ("dt", 4), ("llb", 4), ("nllb", 4),
                  ("oml", 4)):
    PAR[_name] = (NPAR, NPAR + _n)
    NPAR += _n

CST = {}
NCONST = 0
for _name, _n in (("ident", P), ("ones", P), ("upP", P), ("upS", 64), ("sameS", 64), ("cos", T), ("sin", T),
                  ("dmP", 4 * P), ("dmS", 4 * 64), ("innP", 4 * P), ("innS", 4 * 64), ("tailP", 4), ("tailS", 4),
                  ("reset", T), ("seqm", 4), ("eps", 1), ("one", 1), ("lnq", 1), ("zero", 1)):
    CST[_name] = (NCONST, NCONST + _n)
    NCONST += _n
GAMMA = [1.0 - 2.0 ** (-5.0 - h) for h in range(HEADS)]


def shape_constants():
    c = np.zeros((P, NCONST), np.float32)

    def put(name, a):
        s, e = CST[name]
        c[:a.shape[0], s:e] = a.reshape(a.shape[0], -1)

    i = np.arange(P)
    put("ident", np.eye(P))
    put("ones", np.ones((P, P)))
    put("upP", (i[:, None] <= i[None, :]) * 1.0)
    s = np.arange(64)
    same = (s[:, None] // ST) == (s[None, :] // ST)
    put("upS", ((s[:, None] <= s[None, :]) & same) * 1.0)
    put("sameS", same * 1.0)
    half = P // 2
    inv = (np.float32(10000.0) ** (-np.arange(half, dtype=np.float32) / np.float32(half))).astype(np.float32)
    pos = np.concatenate([np.arange(SEQ), np.tile(PAST + np.arange(ST), SB)]).astype(np.float32)
    ang = (pos[None, :] * inv[:, None]).astype(np.float32).astype(np.float64)
    put("cos", np.concatenate([np.cos(ang), np.cos(ang)]))
    put("sin", np.concatenate([-np.sin(ang), np.sin(ang)]))
    g = np.array(GAMMA)
    rel = i[None, :] - i[:, None]
    put("dmP", np.where(rel[:, None, :] >= 0, g[None, :, None] ** np.maximum(rel, 0)[:, None, :], 0.0))
    rel = s[None, :] - s[:, None]
    put("dmS", np.where((rel >= 0)[:, None, :] & same[:, None, :], g[None, :, None] ** np.maximum(rel, 0)[:, None, :], 0))
    put("innP", np.broadcast_to((g[:, None] ** (i + 1)[None, :])[None], (P, 4, P)))
    put("innS", np.broadcast_to((g[:, None] ** (s % ST + 1)[None, :])[None], (P, 4, 64)))
    put("tailP", g[None, :] ** (P - 1 - i)[:, None])
    put("tailS", g[None, :] ** (ST - 1 - s % ST)[:, None])
    start = np.ones(T)
    start[[0, P]] = 0
    start[SEQ::ST] = 0
    put("reset", np.broadcast_to(start, (P, T)))
    put("seqm", ((s // ST) % 4)[:, None] == np.arange(4)[None, :])
    put("eps", np.full((P, 1), EPS))
    put("one", np.full((P, 1), 1.0))
    put("lnq", np.full((P, 1), -0.5 * math.log(P)))
    m = np.zeros((P, 15, P), np.float32)
    for lv, h in enumerate(LEVELS):
        pair = (i[:, None] // (2 * h)) == (i[None, :] // (2 * h))
        up = pair & (i[:, None] % (2 * h) < h) & (i[None, :] % (2 * h) >= h)
        m[:, lv] = up
        m[:, 8 + lv] = up.T
    m[:, DIAG] = np.eye(P)
    return c, m


UNITS = []
UNIT_AT = {}


def _units(kind, slots, tiles):
    k = 0
    for s in slots:
        for m in range(tiles):
            UNIT_AT[(kind, k)] = len(UNITS)
            UNITS.append((kind, SLOT_NAMES.index(s) if s else None, m, k))
            k += 1


for _kind, _slots, _tiles in (
        ("raw", ["q_a", "k_a", "v_a"], 4), ("f_b", ["f_b"], 4), ("z_a", ["z_a"], 4), ("ba", [None], 1),
        ("q_b", ["q_b"], 4), ("i_b", ["i_b"], 3), ("z_b", ["z_b"], 4), ("gate_a", ["gate_a0", "gate_a1"], 4),
        ("br_a", ["br_a"], 8), ("q_c", ["q_c"], 4), ("k_c", ["k_c"], 4), ("v_c", ["v_c0", "v_c1"], 3),
        ("g_c", ["g_c0", "g_c1"], 4), ("gate_b", ["gate_b0", "gate_b1"], 4), ("br_b", ["br_b"], 8),
        ("gate_c", ["gate_c0", "gate_c1"], 4), ("br_c", ["br_c0", "br_c1"], 4), ("out", ["out0", "out1"], 4),
        ("up", [f"up{i}" for i in range(8)], 4), ("down", [f"down{i}" for i in range(8)], 1)):
    _units(_kind, _slots, _tiles)
NU = len(UNITS)
TOKEN_MAJOR = ("i_b", "v_c")
PIECES_OF = {}
PIECE_END = {}
_parts = 0
for _u, (_k, _s, _m, _i) in enumerate(UNITS):
    if _s is None:
        PIECES_OF[_u] = []
    elif _k in TOKEN_MAJOR:
        PIECES_OF[_u] = [4 * _s + _q for _q in ((0, 1), (2,), (3,))[_m]]
    elif _k == "down":
        PIECES_OF[_u] = [4 * _s + _q for _q in range(4)]
    elif _k in ("br_a", "br_b"):
        PIECES_OF[_u] = [4 * _s + _m // 2]
    else:
        PIECES_OF[_u] = [4 * _s + _m]
    for _p in PIECES_OF[_u]:
        if (_k == "down" or _k in TOKEN_MAJOR) and _p % 4 < 3:
            _parts += 1
            PIECE_END[_p] = ("part", _parts, _u)
        else:
            PIECE_END[_p] = ("unit", _u, _u)
BANKS = 3
SILU_KINDS = ("z_a", "q_b", "z_b", "g_c")
TEMP_UNITS = [u for u, x in enumerate(UNITS) if x[0] in SILU_KINDS + ("q_c", "k_c")]
TEMP_ORDER = {u: n for n, u in enumerate(TEMP_UNITS)}
SILU_NO = {u: n for n, u in enumerate(u for u in TEMP_UNITS if UNITS[u][0] in SILU_KINDS)}
ROT_NO = {u: n for n, u in enumerate(u for u in TEMP_UNITS if UNITS[u][0] not in SILU_KINDS)}
EXP_BOUND = 1e18
TABLE_SET = "natural_log_exp_and_others"


def unit_list(*kinds):
    return [("unit", u) for u, x in enumerate(UNITS) if x[0] in kinds]


SLACK = {"g_bc": 4.0, "g_gram": 3.0, "g_p": 0.8, "g_z": 1.2, "g_s": 0.5, "h_m": 0.7, "h_l": 0.3, "r_s": 0.5, "l2": 0.3,
         "h_fa": 0.5, "h_fb": 0.5, "r_load": 0.0, "z_split": 0.0}


def merge(core, units):
    slack = [SLACK.get(item[0], 1.0) for item in core]
    out, done, sum_ = [], 0, 0.0
    for item, w in zip(core, slack):
        out.append(item)
        sum_ += w
        upto = int(sum_ * len(units) / sum(slack) + 0.5)
        out += units[done:upto]
        done = upto
    return out + units[done:]


def levels_of(c):
    return 3 if c == SAMPLE else 7


FORGET_AT = 2
GDN_CORE = []
for _c in range(3):
    GDN_CORE += [("g_bc", _c), ("g_gram", _c)]
    for _lv in range(1, levels_of(_c)):
        GDN_CORE += [("g_p", _c, _lv), ("g_z", _c, _lv)]
    GDN_CORE += [("g_ks", _c)] if _c else []
    GDN_CORE += [("g_ks2", _c)] if _c == SAMPLE else []
    GDN_CORE += [("g_v", _c), ("g_o", _c), ("g_n", _c), ("z_split", "a", _c)]
HG_CORE = []
for _c in range(3):
    HG_CORE += [("h_e", _c), ("h_l", _c, 0), ("h_t", _c)]
    for _lv in range(levels_of(_c)):
        if _lv + 1 < levels_of(_c):
            HG_CORE.append(("h_l", _c, _lv + 1))
        HG_CORE.append(("h_m", _c, _lv))
    HG_CORE += [("h_o", _c)] if _c != SAMPLE else [("h_s", h) for h in range(HEADS)]
    HG_CORE += [("h_n", _c), ("z_split", "b", _c)]
RET_CORE = []
for _c in range(3):
    RET_CORE += [("r_a", _c)]
    RET_CORE += [("r_load", 0)] if _c == 1 else []
    RET_CORE += [("r_o", _c)] if _c != SAMPLE else [("r_s", p) for p in range(2 * HEADS)]
    RET_CORE += [("r_n", _c)] + ([("z_split", "c", i) for i in range(3)] if _c == SAMPLE else [])


def one_behind(units, kind):
    out = []
    for m, item in enumerate(units):
        out += [item] + ([(kind, m - 1)] if m else [])
    return out + [(kind, len(units) - 1)]


def with_squares(units, norm):
    out = []
    for m, item in enumerate(units):
        out += [item, ("take_square", norm, m)] + ([("square", norm, m - 1)] if m else [])
    return out + [("square", norm, len(units) - 1), ("rms", norm)]


GDN_TAIL = [("g_s", _h) for _h in range(HEADS)]
HG_EARLY = 4
RET_EARLY = 6
for _n in range(2 * HEADS):
    _at = [i for i, x in enumerate(GDN_CORE) if x[0] == "g_z"][_n + FORGET_AT]
    GDN_CORE.insert(_at + 1, (("h_fa", "h_fb")[_n % 2], _n // 2))

def conv_pipeline(units):
    out = []
    for s, item in enumerate(units):
        out.append(item)
        for kind, lag, tiles in (("conv_sig", 4, 12), ("conv_bound", 3, 12), ("conv", 1, 12), ("conv_exp", 2, 12),
                                 ("silu", 5, 12), ("l2", 6, 8)):
            if 0 <= s - lag < tiles:
                out.append((kind, s - lag))
    return out


SCHEDULE = ([("scale", 0)] + conv_pipeline(unit_list("raw", "f_b", "z_a"))
            + unit_list("ba") + [("ba",)]
            + merge(GDN_CORE, unit_list("q_b", "i_b", "z_b", "gate_a"))
            + merge(GDN_TAIL + HG_CORE[:HG_EARLY], unit_list("br_a")) + [("h_load",)]
            + merge(HG_CORE[HG_EARLY:], unit_list("q_c", "k_c", "v_c", "g_c", "gate_b"))
            + merge(RET_CORE[:RET_EARLY], unit_list("br_b")) + [("r_load", 1)]
            + merge(RET_CORE[RET_EARLY:], unit_list("gate_c")) + one_behind(unit_list("br_c"), "m_split")
            + with_squares(unit_list("out"), 1) + [("scale", 1)]
            + one_behind(unit_list("up"), "hid_split") + with_squares(unit_list("down"), 0))


def with_splits(schedule):
    before, after = {}, {}
    for p in range(SPLIT_RING, NPIECE):
        kind, _, u = PIECE_END[p - SPLIT_RING]
        part_of_down = kind == "part" and UNITS[u][0] == "down"
        (before if part_of_down else after).setdefault(u, []).append(("split", p))
    out, pending = [("split", 0)], []
    for item in schedule:
        u = item[1] if item[0] == "unit" else None
        if item[0] == "gate_sig":
            pending.append(item)
            continue
        if u is not None:
            out, pending = out + pending + before.get(u, []), after.get(u, [])
        out.append(item)
        if item == ("scale", 0):
            out += [("split", p) for p in range(1, SPLIT_RING)]
    return out


def with_gates(schedule):
    out = []
    for item in schedule:
        out.append(item)
        if item[0] == "unit" and UNITS[item[1]][0] in ("gate_a", "gate_b", "gate_c") and UNITS[item[1]][3] % 2:
            n = "abc".index(UNITS[item[1]][0][5]), UNITS[item[1]][3] // 2
            out += [("gate_bound",) + n, ("gate_sig",) + n]
    return out


SCHEDULE = with_splits(with_gates(SCHEDULE))
STAGE_NO = {}
for _item in SCHEDULE:
    STAGE_NO[_item] = sum(1 for x in STAGE_NO if x[0] == _item[0])


def nth(*item):
    return STAGE_NO[item] + 1


def trunk(nc, x_in, wpack, wba, par_in, nfin_in, lbd_in, const_in, mask_in, st_conv, st_gdn, st_hg, st_ret,
          y_out, o_conv, o_gdn_p, o_hg_p, o_ret_p, o_gdn_s, o_hg_s, o_ret_s):
    with ExitStack() as ctx:
        def sb(name, shape, dt=F32):
            return ctx.enter_context(nc.sbuf_tensor(name, shape, dt))

        single_pass = {}

        def sb_split(name, shape):
            at = (nc.sbuf_base + 31) // 32 * 32
            z = sb(name, shape)
            single_pass[name] = nc.alloc_sbuf_tensor_at(name + "_r32", shape, mybir.dt.float32r, offset=at)
            return z

        all_sems = []

        def sem(name):
            s = ctx.enter_context(nc.semaphore(name))
            all_sems.append(s)
            return s

        ring = sb_split("ring", [P, RING, PIECE])
        w_high = sb_split("w_high", [P, SPLIT_RING, PIECE])
        x = sb("x", [P, KT, T])
        h_pad = sb_split("h_low", [P, KT * T + 64])
        h = h_pad[:, 0:KT * T].rearrange("p (m t) -> p m t", m=KT)
        h_high_pad = sb_split("h_high", [P, KT * T + 64])
        h_high = h_high_pad[:, 0:KT * T].rearrange("p (m t) -> p m t", m=KT)
        HID = 32 * T
        arena = sb_split("arena", [P, HID])
        hid = arena[:, 0:32 * T].rearrange("p (m t) -> p m t", m=32)
        RAWN = 12 * RAW
        raw = arena[:, 0:RAWN].rearrange("p (m t) -> p m t", m=12)
        act = arena[:, RAWN:RAWN + 12 * T].rearrange("p (m t) -> p m t", m=12)
        _o = RAWN + 12 * T
        zA = arena[:, _o:_o + 4 * T].rearrange("p (m t) -> p m t", m=4)
        _o += 4 * T
        newc = arena[:, _o:_o + 324].rearrange("p (m b t) -> p m b t", m=12, b=9)
        gstate = arena[:, 0:4096].rearrange("p (h b v) -> p h b v", h=4, b=8)
        qC = arena[:, 0:4 * T].rearrange("p (m t) -> p m t", m=4)
        kC = arena[:, 4 * T:8 * T].rearrange("p (m t) -> p m t", m=4)
        gC_high = arena[:, 0:8 * T].rearrange("p (m t) -> p m t", m=8)
        zA_high = act[:, 8:12, :]
        gC = arena[:, 8 * T:16 * T].rearrange("p (m t) -> p m t", m=8)
        vC = arena[:, 16 * T:16 * T + 3072].rearrange("p (c v) -> p c v", c=3)
        merged = sb_split("merged", [P, KT, T])
        gate = sb_split("gate", [P, KT, T])
        mflat = merged[:, :, :].rearrange("p m t -> p (m t)")
        gflat = gate[:, :, :].rearrange("p m t -> p (m t)")
        conv_tile = lambda i: gflat[:, CONV * (i % CV_RING):CONV * (i % CV_RING) + CONV]
        exp_tile = lambda i: mflat[:, CONV * (i % CV_RING):CONV * (i % CV_RING) + CONV]
        t1, t2 = merged[:, 0:4, :], merged[:, 4:8, :]
        fB = sb_split("fB", [P, 4, T])
        qB = sb_split("qB", [P, 4, T])
        kB = sb_split("kB", [P, 4, T])
        zB = sb_split("zB", [P, 4, T])
        iB = sb("iB", [P, 3, 512])
        l2buf = lambda m: (kB, zB)[m // 4][:, m % 4, :]
        temp = sb("temp", [P, 2, T])
        hist = temp[:, :, :].rearrange("p a t -> p (a t)")[:, 0:288]
        cst = sb("cst", [P, NCONST])
        masks = sb("masks", [P, 15, P], U8)
        parAll = sb("parAll", [P, DEPTH, NPAR])
        par = sb("par", [P, NPAR])
        nfin = sb("nfin", [P, KT])
        lb2 = sb("lb2", [P, DEPTH, HEADS])
        wbaT = sb_split("wbaT", [P, 64])
        wba_high = sb_split("wba_high", [P, 64])
        lbt = temp[:, 0, :]
        small = sb("small", [P, 160])
        rs = sb("rs", [P, T])
        eg = sb("eg", [P, 4, P])
        DT = sb("DT", [P, 4, P])
        DD = sb("DD", [P, 4, P])
        NT = sb("NT", [P, 4, P])
        XX = sb("XX", [P, 4, P])
        XT = sb("XT", [P, 4, P])
        PP = sb("PP", [P, 4, P])
        Kd = sb("Kd", [P, 4, P])
        VR = sb("VR", [P, 4, P])
        vn = sb("vn", [P, 4, P])
        qg = sb("qg", [P, 4, P])
        sq0 = sb("sq0", [P, 4, P])
        sq = (sq0, DD)
        S = sb("S", [P, 512])
        S_ret = iB[:, :, :].rearrange("p c v -> p (c v)")[:, 0:1024]
        sst = sb("sst", [P, 2, 8, P])
        _tail = [arena[:, 8192 + 1024 * i:8192 + 1024 * i + 1024] for i in range(2)]
        _own = [sst[:, i].rearrange("p b v -> p (b v)") for i in range(2)]
        _after = [z[:, :, :].rearrange("p m t -> p (m t)")[:, 0:1024] for z in (qB, kB, fB, zB)]
        hg_piece = _own + _tail
        ret_piece = _tail + _own + _after

        _hid_high = [(0, gate), (8, merged), (16, qB), (20, kB), (24, fB), (28, zB)]

        def hid_high(i):
            start, z = [x for x in _hid_high if x[0] <= i][-1]
            return z[:, i - start, :]

        def r32(ap):
            return bass.AP(single_pass[ap.tensor.name], ap.offset, ap.ap)

        def high(ap):
            return r32(ap).bitcast(F32)

        def by_seq(piece):
            return piece.rearrange("p (b v) -> p b v", b=SB)

        ps = ctx.enter_context(nc.psum_tensor("ps", [P, 8, 512], F32))

        def K(i):
            return ps[:, BANKS + i, :]

        def K4(i, rows, n):
            return ps[0:rows, BANKS + i, 0:4 * n].rearrange("p (h n) -> p h n", h=4)

        def C(name, rows=P):
            s, e = CST[name]
            return cst[0:rows, s:e]

        def Q(name, i=None):
            s, e = PAR[name]
            return par[:, s:e] if i is None else par[:, s + i:s + i + 1]

        ident, ones = C("ident"), C("ones")
        bab = small[:, 0:24].rearrange("p (c n) -> p c n", c=3)
        eb = small[:, 24:36].rearrange("p (c n) -> p c n", c=3)
        beta = small[:, 36:48].rearrange("p (c n) -> p c n", c=3)
        nbeta = small[:, 48:60].rearrange("p (c n) -> p c n", c=3)
        la = small[:, 60:72].rearrange("p (c n) -> p c n", c=3)
        ap_ = small[:, 72:84].rearrange("p (c n) -> p c n", c=3)
        nea = small[:, 84:88]
        gc = small[:, 88:96]
        tl = small[:, 96:100]
        egc = small[:, 100:104]
        etl = small[:, 104:108]
        nbeg = small[:, 108:112]

        def chunk(ap, c):
            t0, n = CHUNKS[c]
            return ap[:, :, t0:t0 + n]

        def up_mask(c):
            return C("upS", 64) if c == SAMPLE else C("upP")

        def over_heads(ap, rows, n):
            return ap[0:rows, None, 0:n].to_broadcast([rows, 4, n])

        def seqs(ap):
            return ap.rearrange("p m (b t) -> p m b t", b=SB)

        def blocks(ap, half):
            return ap.rearrange("p h (k t) -> p h k t", t=2 * half)

        loaded, x_loaded = sem("inputs_loaded"), sem("x_loaded")
        slot_in = [sem(f"slot{i}_loaded") for i in range(RING)]
        w_high_ready, w_split = sem("w_high_ready"), sem("w_split")
        piece_used = sem("piece_used")
        unit_done = sem("unit_done")
        bank_read = [sem(f"bank{i}_read") for i in range(BANKS)]
        act_seq, dve_seq, pool_seq = sem("act_seq"), sem("dve_seq"), sem("pool_seq")
        x_squared = sem("x_squared")
        sumsq_ready = sem("sumsq_ready")
        rms_ready = sem("rms_ready")
        h_late_ready = sem("h_late_ready")
        h_scaled, h_high_ready, h_ready = sem("h_scaled"), sem("h_high_ready"), sem("h_ready")
        z_high_ready, z_split = sem("z_high_ready"), sem("z_split")
        merged_high_ready, merged_ready = sem("merged_high_ready"), sem("merged_ready")
        hid_squared, hid_high_ready = sem("hid_squared"), sem("hid_high_ready")
        wba_high_ready, wba_ready = sem("wba_high_ready"), sem("wba_ready")
        hist_loaded = sem("hist_loaded")
        hist_placed = sem("hist_placed")
        par_ready = sem("par_ready")
        wba_loaded = sem("wba_loaded")
        conv_ready = sem("conv_ready")
        conv_exp_ready = sem("conv_exp_ready")
        silu_ready = sem("silu_ready")
        l2sq_ready = sem("l2sq_ready")
        l2sum_ready = sem("l2sum_ready")
        l2rs_ready = sem("l2rs_ready")
        l2_ready = sem("l2_ready")
        adt_ready = sem("adt_ready")
        softplus_ready = sem("softplus_ready")
        ba_ready = sem("ba_ready")
        bc_ready = sem("bc_ready")
        eg_ready = sem("eg_ready")
        negb_ready = sem("negb_ready")
        ddiff_ready = sem("ddiff_ready")
        decay_ready = sem("decay_ready")
        gates_ready = sem("gates_ready")
        masked_ready = sem("masked_ready")
        qg_ready = sem("qg_ready")
        gram_ready = sem("gram_ready")
        attn_ready = sem("attn_ready")
        kdv_ready = sem("kdv_ready")
        p_ready = sem("p_ready")
        p_copied = sem("p_copied")
        z_ready = sem("z_ready")
        x_updated = sem("x_updated")
        ks_ready = sem("ks_ready")
        ks_copied = sem("ks_copied")
        ks2_ready = sem("ks2_ready")
        rhs_ready = sem("rhs_ready")
        v_ready = sem("v_ready")
        v_copied = sem("v_copied")
        o_ready = sem("o_ready")
        o_squared = sem("o_squared")
        s_updated = sem("s_updated")
        osum_ready = sem("osum_ready")
        ors_ready = sem("ors_ready")
        onormed = sem("onormed")
        g_gated = sem("g_gated")
        gst_loaded = sem("gst_loaded")
        vm_ready = sem("vm_ready")
        sstep_ready = sem("sstep_ready")
        sdecayed = sem("sdecayed")
        sst_updated = sem("sst_updated")
        f_temp1 = sem("f_temp1")
        f_temp2 = sem("f_temp2")
        f_expf = sem("f_expf")
        f_lb1 = sem("f_lb1")
        f_ready = sem("f_ready")
        h_eb_ready = sem("h_eb_ready")
        h_kdiff = sem("h_kdiff")
        h_kdexp = sem("h_kdexp")
        h_kd = sem("h_kd")
        h_qg_ready = sem("h_qg_ready")
        h_attn0 = sem("h_attn0")
        h_t_ready = sem("h_t_ready")
        h_kdT = sem("h_kdT")
        h_diag_done = sem("h_diag_done")
        h_ldiff = sem("h_ldiff")
        h_lexp = sem("h_lexp")
        h_lev_ready = sem("h_lev_ready")
        h_m_ready = sem("h_m_ready")
        h_m_read = sem("h_m_read")
        h_o_ready = sem("h_o_ready")
        h_o_squared = sem("h_o_squared")
        h_s_updated = sem("h_s_updated")
        h_osum = sem("h_osum")
        h_ors = sem("h_ors")
        h_onormed = sem("h_onormed")
        h_gated = sem("h_gated")
        h_vm = sem("h_vm")
        h_sstep = sem("h_sstep")
        h_sdec = sem("h_sdec")
        h_sst = sem("h_sst")
        r_a_ready = sem("r_a_ready")
        r_kd = sem("r_kd")
        r_attn = sem("r_attn")
        r_qg = sem("r_qg")
        r_o_ready = sem("r_o_ready")
        r_squared = sem("r_squared")
        r_s_updated = sem("r_s_updated")
        r_osum = sem("r_osum")
        r_ors = sem("r_ors")
        r_onormed = sem("r_onormed")
        r_gated = sem("r_gated")
        r_vm = sem("r_vm")
        r_sstep = sem("r_sstep")
        r_sst = sem("r_sst")
        temp_ready = sem("temp_ready")
        temp_bounded = sem("temp_bounded")
        temp_sigmoid = sem("temp_sigmoid")
        conv_bounded = sem("conv_bounded")
        conv_sigmoid = sem("conv_sigmoid")
        gates_bounded = sem("gates_bounded")
        gates_sigmoid = sem("gates_sigmoid")
        f_bounded = sem("f_bounded")
        f_sigmoid = sem("f_sigmoid")
        temp_used = sem("temp_used")
        merged_added = sem("merged_added")
        hid_ready = sem("hid_ready")
        conv_out = sem("conv_out")
        gdn_out = sem("gdn_out")
        hg_out = sem("hg_out")
        ret_out = sem("ret_out")
        hg_moved = [sem(f"hg_moved{i}") for i in range(4)]
        ret_moved = [sem(f"ret_moved{i}") for i in range(8)]
        h_old_read, r_old_read = sem("h_old_read"), sem("r_old_read")
        slots_ahead = sem("slots_ahead")
        y_ready, y_out_sem = sem("y_ready"), sem("y_stored")

        class Steps:

            def __init__(self):
                self.n = {}

            def __call__(self, q):
                self.n[q.name] = self.n.get(q.name, 0) + 1
                return self.n[q.name]

        def unit_no(u):
            return u + 1

        def bank_no(u):
            return u // BANKS + 1

        with nc.Block() as block:
            @block.sync
            def _(sp):
                sp.dma_start(x[:], x_in).then_inc(x_loaded, 16)
                sp.dma_start(cst[:], const_in).then_inc(loaded, 16)
                sp.dma_start(mflat[:, 0:15 * P], mask_in.rearrange("p m n -> p (m n)")).then_inc(loaded, 16)
                sp.dma_start(parAll[:], par_in).then_inc(loaded, 16)
                sp.dma_start(nfin[:], nfin_in).then_inc(loaded, 16)
                sp.dma_start(lb2[:], lbd_in).then_inc(loaded, 16)
                for s in range(AHEAD):
                    sp.dma_start(ring[:, s, :], wpack[0, s]).then_inc(slots_ahead, 16)
                sp.wait_ge(slots_ahead, 16 * AHEAD)

            @block.tensor
            def _(pe):
                pe.wait_ge(x_squared, 1)
                pe.wait_ge(loaded, 80)
                for kt in range(KT):
                    last = nc.tensor.matmul(K(0)[:, 0:T], ones, h[:, kt, :], start=(kt == 0), stop=(kt == KT - 1))
                last.then_inc(sumsq_ready, 1)

            @block.gpsimd
            def _(pool):
                pl = Steps()
                nc.gpsimd.memset(small[:], 0.0).then_inc(pool_seq, 1)
                pool.wait_ge(pool_seq, pl(pool_seq))
                for z in (h_pad, h_high_pad):
                    nc.gpsimd.memset(high(z[:, KT * T:]), 0.0).then_inc(pool_seq, 1)
                    pool.wait_ge(pool_seq, pl(pool_seq))

            @block.vector
            def _(dve):
                v = Steps()
                dve.wait_ge(loaded, 80)
                nc.vector.tensor_copy(masks[:].rearrange("p m n -> p (m n)"), mflat[:, 0:15 * P]).then_inc(dve_seq, 1)
                dve.wait_ge(dve_seq, v(dve_seq))
                o = {k: PAR[k][0] for k in ("llb", "nllb", "oml")}
                nc.vector.memset(parAll[:, 0, o["llb"]:o["llb"] + 4], NEG_BIG).then_inc(dve_seq, 1)
                dve.wait_ge(dve_seq, v(dve_seq))
                nc.vector.memset(parAll[:, 0, o["nllb"]:o["nllb"] + 4], -NEG_BIG).then_inc(dve_seq, 1)
                dve.wait_ge(dve_seq, v(dve_seq))
                nc.vector.memset(parAll[:, 0, o["oml"]:o["oml"] + 4], 1.0).then_inc(dve_seq, 1)
                dve.wait_ge(dve_seq, v(dve_seq))
                m, d = lbt[:, 0:4], lbt[:, 16:20]
                nc.vector.tensor_tensor(d, lb2[:, 1, :], lb2[:, 0, :], ALU.subtract).then_inc(f_temp2, 1)
                dve.wait_ge(f_temp2, v(f_temp2))
                nc.vector.tensor_scalar(m, d, 0.0, None, ALU.min).then_inc(dve_seq, 1)
                dve.wait_ge(dve_seq, v(dve_seq))
                dve.wait_ge(f_temp1, 1)
                llb = parAll[:, 1, o["llb"]:o["llb"] + 4]
                nc.vector.tensor_tensor(llb, m, lbt[:, 8:12], ALU.subtract).then_inc(dve_seq, 1)
                dve.wait_ge(dve_seq, v(dve_seq))
                nc.vector.tensor_scalar(parAll[:, 1, o["nllb"]:o["nllb"] + 4], llb, -1.0, None, ALU.mult).then_inc(dve_seq, 1)
                dve.wait_ge(dve_seq, v(dve_seq))
                nc.vector.tensor_scalar(lbt[:, 12:16], lbt[:, 4:8], 1.0, None, ALU.add).then_inc(dve_seq, 1)
                dve.wait_ge(dve_seq, v(dve_seq))
                nc.vector.reciprocal(parAll[:, 1, o["oml"]:o["oml"] + 4], lbt[:, 12:16]).then_inc(dve_seq, 1)
                dve.wait_ge(dve_seq, v(dve_seq))

            @block.scalar
            def _(a):
                s = Steps()
                a.preload_act_table_set(TABLE_SET)
                a.wait_ge(x_loaded, 16)
                nc.scalar.activation(h, x[:], ACT.Square).then_inc(x_squared, 1)
                a.wait_ge(loaded, 80)
                a.wait_ge(f_temp2, 1)
                nc.scalar.activation(lbt[:, 4:8], lbt[:, 16:20], ACT.Exp).then_inc(act_seq, 1)
                a.wait_ge(act_seq, s(act_seq))
                nc.scalar.activation(lbt[:, 8:12], lbt[:, 16:20], ACT.Abs).then_inc(act_seq, 1)
                a.wait_ge(act_seq, s(act_seq))
                nc.scalar.activation(lbt[:, 8:12], lbt[:, 8:12], ACT.Exp, scale=-1.0).then_inc(act_seq, 1)
                a.wait_ge(act_seq, s(act_seq))
                nc.scalar.activation(lbt[:, 8:12], lbt[:, 8:12], ACT.Ln, bias=C("one")).then_inc(f_temp1, 1)
                a.wait_ge(sumsq_ready, 1)
                nc.scalar.activation(rs[:], K(0)[:, 0:T], ACT.Ln, bias=C("eps"), scale=1.0 / D).then_inc(act_seq, 1)
                a.wait_ge(act_seq, s(act_seq))
                nc.scalar.activation(rs[:], rs[:], ACT.Exp, scale=-0.5)
                a.wait_ge(f_temp1, s(f_temp1))

        def clear_semaphores():
            with nc.Block() as block:
                @block.gpsimd
                def _(pool):
                    pool.dma_reset()
                    numbers = sorted(q.num for q in all_sems)
                    first = numbers[0]
                    for n, after in zip(numbers, numbers[1:] + [None]):
                        if after != n + 1:
                            pool.sem_clear(range(first, n + 1))
                            first = after

        clear_semaphores()

        with nc.Fori(0, DEPTH) as layer:
            with nc.Block() as block:
                @block.sync
                def _(sp):
                    sp.dma_start(wbaT[:], wba[bass.ds(layer, 1)].rearrange("a p n -> (a p) n")) \
                        .then_inc(wba_loaded, 16)
                    for s in range(AHEAD, NPIECE):
                        if s >= RING:
                            end, number, _ = PIECE_END[s - RING]
                            if end == "unit":
                                sp.wait_ge(unit_done, unit_no(number))
                            else:
                                sp.wait_ge(piece_used, number)
                        sp.dma_start(ring[:, s % RING, :], wpack[bass.ds(layer, 1), s].rearrange("a p n -> (a p) n")) \
                            .then_inc(slot_in[s % RING], 16)
                    for s in range(AHEAD):
                        end, number, _ = PIECE_END[NPIECE + s - RING]
                        if end == "unit":
                            sp.wait_ge(unit_done, unit_no(number))
                        else:
                            sp.wait_ge(piece_used, number)
                        sp.dma_start(ring[:, s, :], wpack[bass.ds(DEPTH - 1 - layer, 1), s].rearrange("a p n -> (a p) n")) \
                            .then_inc(slots_ahead, 16)
                    sp.wait_ge(slots_ahead, 16 * AHEAD)

                @block.tensor
                def _(pe):
                    mm = nc.tensor.matmul

                    def product(out, w, x_, start, stop):
                        mm(out, r32(w[0]), r32(x_[0]), start=start, stop=False)
                        mm(out, r32(w[0]), r32(x_[1]), start=False, stop=False)
                        return mm(out, r32(w[1]), r32(x_[0]), start=False, stop=stop)

                    def parts(p):
                        return (w_high[:, p % SPLIT_RING, :],
                                ring[:, p % RING, :])

                    def tokens(kt, t0):
                        return (h_high_pad[:, kt * T + t0:kt * T + t0 + P], h_pad[:, kt * T + t0:kt * T + t0 + P])

                    def unit(u):
                        kind, slot, m, k = UNITS[u]
                        bank = ps[:, u % BANKS, :]
                        if kind in TOKEN_MAJOR:
                            if m == 0:
                                for w in range(u, u + BANKS):
                                    pe.wait_ge(bank_read[w % BANKS], w // BANKS)
                            for p in PIECES_OF[u]:
                                pe.wait_ge(w_split, p + 1)
                                wp = [z.rearrange("p (k n) -> p k n", k=2) for z in parts(p)]
                                for c, (t0, n) in enumerate(CHUNKS):
                                    for q in range(2):
                                        kt = 2 * (p % 4) + q
                                        last = product(ps[:, (u - m + c) % BANKS, :], tokens(kt, t0), [z[:, q, :] for z in wp],
                                                       kt == 0, kt == KT - 1)
                                    if p % 4 == 3:
                                        last.then_inc(unit_done, 1)
                                if p % 4 < 3:
                                    last.then_inc(piece_used, 1)
                            return
                        if u >= BANKS:
                            pe.wait_ge(bank_read[u % BANKS], u // BANKS)
                        if kind == "ba":
                            pe.wait_ge(wba_ready, 1)
                            wb = [z[:].rearrange("p (k n) -> p k n", k=KT) for z in (wba_high, wbaT)]
                            for c, (t0, n) in enumerate(CHUNKS):
                                for kt in range(KT):
                                    last = product(bank[:, 8 * c:8 * c + 8], tokens(kt, t0), [z[:, kt, :] for z in wb],
                                                   kt == 0, kt == KT - 1)
                            last.then_inc(unit_done, 1)
                            return
                        src_high, src_low = h_high, h
                        if kind == "br_a":
                            src_high, src_low = zA_high, zA
                            pe.wait_ge(z_split, 3)
                        elif kind == "br_b":
                            src_high, src_low = fB, zB
                            pe.wait_ge(z_split, 6)
                        elif kind == "br_c":
                            src_high, src_low = gC_high, gC
                            pe.wait_ge(z_split, 9)
                        per_piece = 4 if kind in ("br_a", "br_b") else 8
                        for j, p in enumerate(PIECES_OF[u]):
                            pe.wait_ge(w_split, p + 1)
                            start = PIECE // 2 * (m % 2) if per_piece == 4 else 0
                            wp = [z[:, start:start + per_piece * P].rearrange("p (k n) -> p k n", k=per_piece) for z in parts(p)]
                            for q in range(per_piece):
                                kt = 8 * j + q
                                if kind == "out":
                                    pe.wait_ge(merged_ready, kt + 1)
                                elif kind == "down":
                                    pe.wait_ge(hid_ready, kt + 1)
                                elif src_low is h:
                                    norm = int(kind == "up")
                                    if kt < POOL_LOW:
                                        pe.wait_ge(h_ready, POOL_LOW * norm + kt + 1)
                                    else:
                                        pe.wait_ge(h_late_ready, (KT - POOL_LOW) * norm + kt - POOL_LOW + 1)
                                if kind == "out":
                                    act_parts = (gate[:, kt, :], merged[:, kt, :])
                                elif kind == "down":
                                    act_parts = (hid_high(kt), hid[:, kt, :])
                                else:
                                    act_parts = (src_high[:, kt, :], src_low[:, kt, :])
                                last = product(bank[:, 0:T], [z[:, q, :] for z in wp], act_parts, kt == 0,
                                               j == len(PIECES_OF[u]) - 1 and q == per_piece - 1)
                            if j < len(PIECES_OF[u]) - 1:
                                last.then_inc(piece_used, 1)
                        last.then_inc(unit_done, 1)

                    def four(bank, n_out, lhs, rhs, rows):
                        for hd in range(HEADS):
                            last = mm(K4(bank, rows, n_out)[:, hd, :], lhs(hd), rhs(hd), start=True, stop=True)
                        return last

                    for item in SCHEDULE:
                        kind, args = item[0], item[1:]
                        if kind == "unit":
                            unit(args[0])
                        elif kind == "square":
                            norm, m = args
                            pe.wait_ge(x_squared, nth(*item))
                            if norm == 1 and m == 0:
                                pe.wait_ge(r_s_updated, 2)
                            last = mm(K(0)[:, 0:T], ones, h[:, m, :], start=(m == 0), stop=(m == KT - 1))
                            if m == KT - 1:
                                last.then_inc(sumsq_ready, 1)
                        elif kind == "l2":
                            m = args[0]
                            pe.wait_ge(l2sq_ready, m + 1)
                            if m >= 2:
                                pe.wait_ge(l2rs_ready, m - 1)
                            mm(K(m % 2)[:, 0:T], ones, l2buf(m), start=True, stop=True) \
                                .then_inc(l2sum_ready, 1)
                        elif kind == "g_bc":
                            c, n = args[0], CHUNKS[args[0]][1]
                            pe.wait_ge(ba_ready, 1)
                            pe.wait_ge(l2rs_ready, 8)
                            pe.wait_ge(silu_ready, 12)
                            if c:
                                pe.wait_ge(onormed, c)
                                pe.wait_ge(s_updated, c)
                                pe.wait_ge(kdv_ready, c)
                            for hd in range(HEADS):
                                mm(K4(0, P, n)[:, hd, :], la[0:n, c, hd:hd + 1].to_broadcast([n, P]), up_mask(c),
                                   start=True, stop=True)
                            for hd in range(HEADS):
                                mm(K4(1, P, n)[:, hd, :], beta[0:n, c, hd:hd + 1].to_broadcast([n, P]),
                                   ident[0:n, 0:n], start=True, stop=True)
                            mm(K(2)[0:n, 0:4], up_mask(c), la[0:n, c, :], start=True, stop=True)
                            mm(K(2)[0:n, 4:8], C("sameS", 64) if c == SAMPLE else ones, la[0:n, c, :],
                               start=True, stop=True).then_inc(bc_ready, 1)
                        elif kind == "g_gram":
                            c, (t0, n) = args[0], CHUNKS[args[0]]
                            pe.wait_ge(l2_ready, 8)
                            pe.wait_ge(eg_ready, c + 1)
                            pe.wait_ge(negb_ready, c + 1)
                            pe.wait_ge(ddiff_ready, c + 1)
                            q = lambda hd: act[:, hd, t0:t0 + n]
                            k = lambda hd: act[:, 4 + hd, t0:t0 + n]
                            four(3, n, k, k, n)
                            four(4, n, k, q, n).then_inc(gram_ready, 1)
                            for hd in range(HEADS):
                                nc.tensor.transpose(K4(0, n, P)[:, hd, :], k(hd), ident)
                            for hd in range(HEADS):
                                last = nc.tensor.transpose(K4(1, n, P)[:, hd, :], act[:, 8 + hd, t0:t0 + n], ident)
                            last.then_inc(gram_ready, 1)
                        elif kind == "g_p":
                            c, n = args[0], CHUNKS[args[0]][1]
                            pe.wait_ge(attn_ready, c + 1)
                            if nth(*item) > 1:
                                pe.wait_ge(x_updated, nth(*item) - 1)
                            four(2, n, lambda hd: NT[0:n, hd, 0:n], lambda hd: XX[0:n, hd, 0:n], n).then_inc(p_ready, 1)
                        elif kind == "g_z":
                            c, n = args[0], CHUNKS[args[0]][1]
                            pe.wait_ge(p_copied, nth(*item))
                            if args[1] < levels_of(c) - 1:
                                four(3, n, lambda hd: XT[0:n, hd, 0:n], lambda hd: PP[0:n, hd, 0:n], n)
                            four(4, n, lambda hd: PP[0:n, hd, 0:n], lambda hd: XT[0:n, hd, 0:n], n).then_inc(z_ready, 1)
                        elif kind == "g_ks":
                            c, (t0, n) = args[0], CHUNKS[args[0]]
                            pe.wait_ge(kdv_ready, c + 1)
                            if c == SAMPLE:
                                pe.wait_ge(gst_loaded, 16)
                                for hd in range(HEADS):
                                    for b in range(SB):
                                        last = mm(K4(0, P, n)[:, hd, ST * b:ST * b + ST], gstate[:, hd, b, :],
                                                  act[:, 4 + hd, t0 + ST * b:t0 + ST * b + ST], start=True, stop=True)
                                last.then_inc(ks_ready, 1)
                            else:
                                four(0, P, lambda hd: act[:, 4 + hd, t0:t0 + n], lambda hd: S[:, hd * P:hd * P + P],
                                     n).then_inc(ks_ready, 1)
                        elif kind == "g_ks2":
                            pe.wait_ge(ks_copied, 1)
                            n = CHUNKS[SAMPLE][1]
                            for hd in range(HEADS):
                                last = nc.tensor.transpose(K4(0, n, P)[:, hd, :], PP[:, hd, 0:n], ident)
                            last.then_inc(ks2_ready, 1)
                        elif kind == "g_v":
                            c, n = args[0], CHUNKS[args[0]][1]
                            pe.wait_ge(kdv_ready, c + 1)
                            pe.wait_ge(x_updated, sum(levels_of(i) - 1 for i in range(c + 1)))
                            if c:
                                pe.wait_ge(rhs_ready, c)
                            four(1, P, lambda hd: XT[0:n, hd, 0:n], lambda hd: VR[0:n, hd, :], n).then_inc(v_ready, 1)
                        elif kind in ("g_o", "h_o"):
                            c, n = args[0], CHUNKS[args[0]][1]
                            gdn = kind == "g_o"
                            if gdn:
                                pe.wait_ge(v_copied, c + 1)
                                pe.wait_ge(qg_ready, c + 1)
                                if c == SAMPLE:
                                    pe.wait_ge(gst_loaded, 16)
                            else:
                                pe.wait_ge(h_m_read, sum(levels_of(i) for i in range(c + 1)))
                                pe.wait_ge(h_qg_ready, c + 1)
                                pe.wait_ge(h_kdT, c + 1)
                                pe.wait_ge(onormed, 3)
                                if c:
                                    pe.wait_ge(h_onormed, c)
                            val = (lambda hd: vn[0:n, hd, :]) if gdn else (lambda hd: iB[0:n, c, hd * P:hd * P + P])
                            for hd in range(HEADS):
                                o = K4(2, P, n)[:, hd, :]
                                last = mm(o, val(hd), DT[0:n, hd, 0:n], start=True, stop=(c == 0))
                                if c == 1:
                                    last = mm(o, S[:, hd * P:hd * P + P], qg[:, hd, :], start=False, stop=True)
                                if c == SAMPLE:
                                    for b in range(SB):
                                        t = slice(ST * b, ST * b + ST)
                                        last = mm(o[:, t], gstate[:, hd, b, :], qg[:, hd, t], start=False, stop=(b == SB - 1))
                            if c != SAMPLE:
                                for hd in range(HEADS):
                                    last = mm(K4(3, P, P)[:, hd, :], Kd[0:n, hd, :], val(hd), start=True, stop=True)
                            last.then_inc(o_ready if gdn else h_o_ready, 1)
                        elif kind in ("g_n", "h_n"):
                            c, n = args[0], CHUNKS[args[0]][1]
                            pe.wait_ge((o_squared if kind == "g_n" else h_o_squared), c + 1)
                            if kind == "h_n" and c:
                                pe.wait_ge(h_s_updated, min(c, 2))
                            if kind == "h_n" and c == SAMPLE:
                                pe.wait_ge(h_sst, HEADS)
                            mm(K(4)[:, 0:4 * n], ones, sq[0][:].rearrange("p h n -> p (h n)")[:, 0:4 * n], start=True, stop=True) \
                                .then_inc(osum_ready if kind == "g_n" else h_osum, 1)
                        elif kind == "g_s":
                            hd = args[0]
                            pe.wait_ge(vm_ready, hd + 1)
                            if hd == 1:
                                pe.wait_ge(ors_ready, 3)
                            if hd > 1:
                                pe.wait_ge(sst_updated, hd - 1)
                            for g in range(2):
                                r = slice(32 * g, 32 * g + 32)
                                last = mm(K(3 * (hd % 2) + g), Kd[r, hd, :], (PP, XT)[hd % 2][r, :, :], start=True, stop=True)
                            last.then_inc(sstep_ready, 1)
                        elif kind == "h_t":
                            c, (t0, n) = args[0], CHUNKS[args[0]]
                            pe.wait_ge(h_kd, c + 1)
                            pe.wait_ge(sst_updated, HEADS)
                            if c:
                                pe.wait_ge(h_diag_done, c)
                                pe.wait_ge(h_kdT, c)
                            for hd in range(HEADS):
                                nc.tensor.transpose(K4(0, n, P)[:, hd, :], DD[:, hd, 0:n], ident)
                            four(1, n, lambda hd: kB[:, hd, t0:t0 + n], lambda hd: qB[:, hd, t0:t0 + n], n).then_inc(h_t_ready, 1)
                        elif kind == "h_m":
                            c, n, lv = args[0], CHUNKS[args[0]][1], nth(*item)
                            pe.wait_ge(h_lev_ready, lv)
                            if lv > 2:
                                pe.wait_ge(h_m_read, lv - 2)
                            if lv == 1:
                                pe.wait_ge(s_updated, 2)
                            if lv > 1:
                                pe.wait_ge(h_diag_done, c + 1)
                            if c and args[1] == 0:
                                pe.wait_ge(h_s_updated, c)
                                pe.wait_ge(h_ors, c)
                            buf = (NT, XX)[lv % 2]
                            four(3 + lv % 2, n, lambda hd: buf[:, hd, 0:n], lambda hd: buf[:, hd, 0:n], n).then_inc(h_m_ready, 1)
                        elif kind == "h_s":
                            hd, n = args[0], CHUNKS[SAMPLE][1]
                            pe.wait_ge(hg_moved[hd], 16)
                            pe.wait_ge(h_m_read, sum(levels_of(i) for i in range(3)))
                            pe.wait_ge(h_qg_ready, 3)
                            pe.wait_ge(h_kdT, 3)
                            pe.wait_ge(h_onormed, 2)
                            o = K4(2, P, n)[:, hd, :]
                            mm(o, iB[0:n, SAMPLE, hd * P:hd * P + P], DT[0:n, hd, 0:n], start=True, stop=False)
                            for b in range(SB):
                                t = slice(ST * b, ST * b + ST)
                                last = mm(o[:, t], by_seq(hg_piece[hd])[:, b, :], qg[:, hd, t], start=False, stop=(b == SB - 1))
                            last.then_inc(h_old_read, 1)
                            pe.wait_ge(h_vm, hd + 1)
                            if hd > 1:
                                pe.wait_ge(h_sst, hd - 1)
                            for g in range(2):
                                r = slice(32 * g, 32 * g + 32)
                                last = mm(K(3 * (hd % 2) + g), Kd[r, hd, :], (PP, XT)[hd % 2][r, :, :], start=True, stop=True)
                            last.then_inc(h_sstep, 1)
                        elif kind == "r_a":
                            c, (t0, n) = args[0], CHUNKS[args[0]]
                            if c == 0:
                                pe.wait_ge(bank_read[UNIT_AT["k_c", 3] % BANKS], UNIT_AT["k_c", 3] // BANKS + 1)
                                pe.wait_ge(temp_used, ROT_NO[UNIT_AT["k_c", 3]] + 1)
                                pe.wait_ge(h_sst, HEADS)
                            else:
                                pe.wait_ge(r_s_updated, c)
                                pe.wait_ge(r_ors, c)
                            for hd in range(HEADS):
                                nc.tensor.transpose(K4(0, n, P)[:, hd, :], kC[:, hd, t0:t0 + n], ident)
                            four(1, n, lambda hd: kC[:, hd, t0:t0 + n], lambda hd: qC[:, hd, t0:t0 + n], n).then_inc(r_a_ready, 1)
                        elif kind == "r_o":
                            c, n = args[0], CHUNKS[args[0]][1]
                            pe.wait_ge(r_kd, c + 1)
                            pe.wait_ge(r_attn, c + 1)
                            pe.wait_ge(r_qg, c + 1)
                            pe.wait_ge(h_onormed, 3)
                            pe.wait_ge(h_ors, 3)
                            if c:
                                pe.wait_ge(r_onormed, c)
                            for f in range(2):
                                for hd in range(HEADS):
                                    o = K4(2 + f, P, n)[:, hd, :]
                                    v = slice(hd * DV_RET + f * P, hd * DV_RET + f * P + P)
                                    last = mm(o, vC[0:n, c, v], DT[0:n, hd, 0:n], start=True, stop=(c == 0))
                                    if c:
                                        mm(o, S_ret[:, v], qg[:, hd, :], start=False, stop=True)
                            for hd in range(HEADS):
                                b = (4, 0)[hd // 2]
                                last = mm(K(b)[:, (hd % 2) * DV_RET:(hd % 2 + 1) * DV_RET], Kd[0:n, hd, :],
                                          vC[0:n, c, hd * DV_RET:(hd + 1) * DV_RET], start=True, stop=True)
                            last.then_inc(r_o_ready, 1)
                        elif kind == "r_s":
                            p_, n = args[0], CHUNKS[SAMPLE][1]
                            hd, f = p_ // 2, p_ % 2
                            pe.wait_ge(ret_moved[p_], 16)
                            pe.wait_ge(r_kd, 3)
                            pe.wait_ge(r_attn, 3)
                            pe.wait_ge(r_qg, 3)
                            pe.wait_ge(r_onormed, 2)
                            o = K4(2 + f, P, n)[:, hd, :]
                            v = slice(hd * DV_RET + f * P, hd * DV_RET + f * P + P)
                            mm(o, vC[0:n, SAMPLE, v], DT[0:n, hd, 0:n], start=True, stop=False)
                            for b in range(SB):
                                t = slice(ST * b, ST * b + ST)
                                last = mm(o[:, t], by_seq(ret_piece[p_])[:, b, :], qg[:, hd, t], start=False, stop=(b == SB - 1))
                            last.then_inc(r_old_read, 1)
                            pe.wait_ge(r_vm, p_ + 1)
                            if p_:
                                pe.wait_ge(r_sst, p_)
                            for g, b in ((0, 4), (1, 0)):
                                r = slice(32 * g, 32 * g + 32)
                                last = mm(K(b), Kd[r, hd, :], (PP, XT)[p_ % 2][r, :, :], start=True, stop=True)
                            last.then_inc(r_sstep, 1)
                        elif kind == "r_n":
                            c, n = args[0], CHUNKS[args[0]][1]
                            pe.wait_ge(r_squared, c + 1)
                            for f in range(2):
                                last = mm(K(1)[:, 0:4 * n], ones, sq[f][:].rearrange("p h n -> p (h n)")[:, 0:4 * n],
                                          start=(f == 0), stop=(f == 1))
                            last.then_inc(r_osum, 1)

                @block.scalar
                def _(a):
                    s = Steps()
                    fn = nc.scalar.activation
                    a.preload_act_table_set(TABLE_SET)

                    def sigmoid_of(z):
                        fn(z, z, ACT.Ln).then_inc(act_seq, 1)
                        a.wait_ge(act_seq, s(act_seq))
                        return fn(z, z, ACT.Exp, scale=-1.0)

                    def rsqrt_of(out, src, scale, bias=None):
                        fn(out, src, ACT.Ln, bias=C("eps"), scale=scale).then_inc(act_seq, 1)
                        a.wait_ge(act_seq, s(act_seq))
                        return fn(out, out, ACT.Exp, scale=-0.5, bias=C("zero") if bias is None else bias)

                    for item in SCHEDULE:
                        kind, args = item[0], item[1:]
                        if kind == "split":
                            p = args[0]
                            place = p % RING
                            if p >= AHEAD:
                                a.wait_ge(slot_in[place], 16 * (p // RING + (place >= AHEAD)))
                            if p >= SPLIT_RING:
                                end, number, _ = PIECE_END[p - SPLIT_RING]
                                if end == "unit":
                                    a.wait_ge(unit_done, unit_no(number))
                                else:
                                    a.wait_ge(piece_used, number)
                            w = ring[:, place, :]
                            fn(r32(w_high[:, p % SPLIT_RING, :]), w, ACT.Copy).then_inc(w_high_ready, 1)
                        elif kind == "scale":
                            if args[0] == 1:
                                a.wait_ge(unit_done, unit_no(UNIT_AT["gate_c", 7]))
                            for kt in range(KT):
                                a.wait_ge(h_scaled, KT * args[0] + kt + 1)
                                fn(r32(h_high[:, kt, :]), h[:, kt, :], ACT.Copy).then_inc(h_high_ready, 1)
                            if args[0] == 0:
                                a.wait_ge(wba_loaded, 16)
                                fn(r32(wba_high[:]), wbaT[:], ACT.Copy).then_inc(wba_high_ready, 1)
                        elif kind == "z_split":
                            br, c = args
                            t0, n = CHUNKS[c]
                            if br == "a":
                                a.wait_ge(g_gated, c + 1)
                            elif br == "b":
                                a.wait_ge(h_gated, c + 1)
                            else:
                                a.wait_ge(r_gated, c + 1)
                            z, z_high = {"a": (zA, zA_high), "b": (zB, fB), "c": (gC, gC_high)}[br]
                            fn(r32(z_high[:, :, t0:t0 + n]), z[:, :, t0:t0 + n], ACT.Copy).then_inc(z_high_ready, 1)
                        elif kind == "m_split":
                            a.wait_ge(merged_added, KT + args[0] + 1)
                            fn(r32(gate[:, args[0], :]), merged[:, args[0], :], ACT.Copy).then_inc(merged_high_ready, 1)
                        elif kind == "hid_split":
                            i = args[0]
                            a.wait_ge(hid_squared, i + 1)
                            if i >= 16 and i % 4 == 0:
                                a.wait_ge(ret_moved[4 + (i - 16) // 4], 32)
                            fn(r32(hid_high(i)), hid[:, i, :], ACT.Copy).then_inc(hid_high_ready, 1)
                        elif kind == "take_square":
                            norm, m = args
                            u = UNIT_AT["out" if norm else "down", m]
                            a.wait_ge(bank_read[u % BANKS], bank_no(u))
                            if m == 0:
                                a.wait_ge(unit_done, unit_no(UNIT_AT["gate_c", 7] if norm else UNIT_AT["up", 31]))
                            fn(h[:, m, :], x[:, m, :], ACT.Square).then_inc(x_squared, 1)
                        elif kind == "rms":
                            a.wait_ge(sumsq_ready, nth(*item))
                            rsqrt_of(rs[:], K(0)[:, 0:T], 1.0 / D).then_inc(rms_ready, 1)
                        elif kind == "unit":
                            u = args[0]
                            k, slot, m, i = UNITS[u]
                            bank = ps[:, u % BANKS, :]
                            if k in ("raw", "f_b", "gate_a", "gate_b", "gate_c", "up", "q_c", "k_c") \
                                    or k in SILU_KINDS:
                                a.wait_ge(unit_done, unit_no(u))
                            if k == "raw":
                                fn(raw[:, i, HIST:RAW_P], bank[:, 0:SEQ], ACT.Copy).then_inc(act_seq, 1)
                                a.wait_ge(act_seq, s(act_seq))
                                fn(raw[:, i, RAW_P:].rearrange("p (b t) -> p b t", b=SB)[:, :, HIST:],
                                               bank[:, SEQ:T].rearrange("p (b t) -> p b t", b=SB), ACT.Copy).then_inc(bank_read[u % BANKS], 1)
                                a.wait_ge(bank_read[u % BANKS], bank_no(u))
                            elif k == "f_b":
                                fn(fB[:, i, :], bank[:, 0:T], ACT.Copy).then_inc(bank_read[u % BANKS], 1)
                                a.wait_ge(bank_read[u % BANKS], bank_no(u))
                            elif k in TOKEN_MAJOR and m == 2:
                                if k == "v_c":
                                    a.wait_ge(gdn_out, 32)
                                half = i // 3
                                for c, (t0, n) in enumerate(CHUNKS):
                                    w = u - 2 + c
                                    a.wait_ge(unit_done, unit_no(w))
                                    dst = iB[0:n, c, :] if k == "i_b" else vC[0:n, c, 512 * half:512 * half + 512]
                                    fn(dst, ps[0:n, w % BANKS, :], ACT.Copy).then_inc(bank_read[w % BANKS], 1)
                                    a.wait_ge(bank_read[w % BANKS], bank_no(w))
                            elif k in SILU_KINDS or k in ("q_c", "k_c"):
                                j = TEMP_ORDER[u]
                                if j >= 2:
                                    before = TEMP_UNITS[j - 2]
                                    if before in SILU_NO:
                                        a.wait_ge(bank_read[before % BANKS], bank_no(before))
                                    else:
                                        a.wait_ge(temp_used, ROT_NO[before] + 1)
                                if k in SILU_KINDS:
                                    fn(temp[:, j % 2, :], bank[:, 0:T], ACT.Exp, scale=-1.0).then_inc(temp_ready, 1)
                                    a.wait_ge(temp_bounded, SILU_NO[u] + 1)
                                    sigmoid_of(temp[:, j % 2, :]).then_inc(temp_sigmoid, 1)
                                else:
                                    fn(temp[0:64, j % 2, :], bank[64:P, 0:T], ACT.Copy).then_inc(act_seq, 1)
                                    a.wait_ge(act_seq, s(act_seq))
                                    fn(temp[64:P, j % 2, :], bank[0:64, 0:T], ACT.Copy).then_inc(temp_ready, 1)
                                    a.wait_ge(temp_ready, s(temp_ready))
                            elif k in ("gate_a", "gate_b", "gate_c"):
                                if k == "gate_a":
                                    a.wait_ge(silu_ready, 12)
                                elif k == "gate_b":
                                    a.wait_ge(bank_read[(UNIT_AT["br_a", i]) % BANKS], bank_no(UNIT_AT["br_a", i]))
                                else:
                                    a.wait_ge(merged_added, i + 1)
                                fn(gate[:, i, :], bank[:, 0:T], ACT.Exp, scale=-1.0).then_inc(bank_read[u % BANKS], 1)
                                a.wait_ge(bank_read[u % BANKS], bank_no(u))
                            elif k == "up":
                                if i == 0:
                                    a.wait_ge(unit_done, unit_no(UNIT_AT["br_c", 7]))
                                if i * T <= 8192 < (i + 1) * T:
                                    a.wait_ge(ret_moved[0], 32)
                                    a.wait_ge(ret_moved[1], 32)
                                fn(hid[:, i, :], bank[:, 0:T], ACT.Relu).then_inc(bank_read[u % BANKS], 1)
                                a.wait_ge(bank_read[u % BANKS], bank_no(u))
                        elif kind == "gate_sig":
                            br, j = args
                            a.wait_ge(gates_bounded, 4 * br + j + 1)
                            sigmoid_of(gate[:, 2 * j:2 * j + 2, :]).then_inc(gates_sigmoid, 1)
                        elif kind == "conv_exp":
                            i = args[0]
                            a.wait_ge(conv_ready, i + 1)
                            if i >= CV_RING:
                                a.wait_ge(silu_ready, i - CV_RING + 1)
                            fn(exp_tile(i), conv_tile(i), ACT.Exp, scale=-1.0).then_inc(conv_exp_ready, 1)
                        elif kind == "conv_sig":
                            a.wait_ge(conv_bounded, args[0] + 1)
                            sigmoid_of(exp_tile(args[0])).then_inc(conv_sigmoid, 1)
                        elif kind == "l2":
                            m = args[0]
                            a.wait_ge(l2sum_ready, m + 1)
                            rsqrt_of(l2buf(m), K(m % 2)[:, 0:T], 1.0, C("lnq") if m < 4 else None).then_inc(l2rs_ready, 1)
                            a.wait_ge(l2rs_ready, s(l2rs_ready))
                        elif kind == "ba":
                            a.wait_ge(adt_ready, 1)
                            fn(nea, Q("alog"), ACT.Exp).then_inc(act_seq, 1)
                            a.wait_ge(act_seq, s(act_seq))
                            fn(eb, bab[:, :, 0:4], ACT.Exp, scale=-1.0).then_inc(act_seq, 1)
                            a.wait_ge(act_seq, s(act_seq))
                            fn(la, ap_, ACT.Abs).then_inc(act_seq, 1)
                            a.wait_ge(act_seq, s(act_seq))
                            fn(la, la, ACT.Exp, scale=-1.0).then_inc(act_seq, 1)
                            a.wait_ge(act_seq, s(act_seq))
                            fn(la, la, ACT.Ln, bias=C("one")).then_inc(softplus_ready, 1)
                            a.wait_ge(softplus_ready, s(softplus_ready))
                        elif kind == "g_bc":
                            c, (t0, n) = args[0], CHUNKS[args[0]]
                            a.wait_ge(bc_ready, c + 1)
                            if c:
                                a.wait_ge(s_updated, c)
                                a.wait_ge(g_gated, c)
                            fn(eg[:, :, 0:n], K4(0, P, n), ACT.Exp).then_inc(eg_ready, 1)
                            a.wait_ge(eg_ready, s(eg_ready))
                            fn(NT[0:n, :, 0:n], K4(1, P, n)[0:n], ACT.Copy, scale=-1.0).then_inc(negb_ready, 1)
                            a.wait_ge(negb_ready, s(negb_ready))
                            a.wait_ge(ddiff_ready, c + 1)
                            fn(egc[0:n], gc[0:n, 0:4], ACT.Exp).then_inc(act_seq, 1)
                            a.wait_ge(act_seq, s(act_seq))
                            fn(etl[0:n], tl[0:n], ACT.Exp).then_inc(act_seq, 1)
                            a.wait_ge(act_seq, s(act_seq))
                            fn(DD[0:n, :, 0:n], DD[0:n, :, 0:n], ACT.Exp, scale=-1.0).then_inc(act_seq, 1)
                            a.wait_ge(act_seq, s(act_seq))
                            fn(DT[0:n, :, 0:n], DT[0:n, :, 0:n], ACT.Exp).then_inc(decay_ready, 1)
                            a.wait_ge(decay_ready, s(decay_ready))
                        elif kind == "g_gram":
                            c, n = args[0], CHUNKS[args[0]][1]
                            a.wait_ge(gram_ready, 2 * (c + 1))
                            for hd in range(HEADS):
                                fn(Kd[0:n, hd, :], K4(0, n, P)[:, hd, :], ACT.Copy, scale=etl[0:n, hd:hd + 1]).then_inc(act_seq, 1)
                                a.wait_ge(act_seq, s(act_seq))
                                last = fn(VR[0:n, hd, :], K4(1, n, P)[:, hd, :], ACT.Copy, scale=beta[0:n, c, hd:hd + 1])
                                if hd < HEADS - 1:
                                    last.then_inc(act_seq, 1)
                                    a.wait_ge(act_seq, s(act_seq))
                            last.then_inc(kdv_ready, 1)
                            a.wait_ge(kdv_ready, s(kdv_ready))
                        elif kind == "g_p":
                            n = CHUNKS[args[0]][1]
                            a.wait_ge(p_ready, nth(*item))
                            fn(PP[0:n, :, 0:n], K4(2, n, n), ACT.Copy).then_inc(p_copied, 1)
                            a.wait_ge(p_copied, s(p_copied))
                        elif kind == "g_ks" and args[0] == SAMPLE:
                            a.wait_ge(ks_ready, 2)
                            fn(PP[:, :, 0:64], K4(0, P, 64), ACT.Copy).then_inc(ks_copied, 1)
                            a.wait_ge(ks_copied, s(ks_copied))
                        elif kind == "g_v":
                            c, n = args[0], CHUNKS[args[0]][1]
                            a.wait_ge(v_ready, c + 1)
                            fn(vn[0:n], K4(1, n, P), ACT.Copy).then_inc(v_copied, 1)
                            a.wait_ge(v_copied, s(v_copied))
                        elif kind in ("g_o", "h_o"):
                            c, n = args[0], CHUNKS[args[0]][1]
                            gdn = kind == "g_o"
                            a.wait_ge((o_ready if gdn else h_o_ready), c + 1)
                            fn(sq[0][:].rearrange("p h n -> p (h n)")[:, 0:4 * n], K(2)[:, 0:4 * n], ACT.Square).then_inc((o_squared if gdn else h_o_squared), 1)
                            a.wait_ge((o_squared if gdn else h_o_squared), s((o_squared if gdn else h_o_squared)))
                        elif kind in ("g_n", "h_n"):
                            c, n = args[0], CHUNKS[args[0]][1]
                            gdn = kind == "g_n"
                            a.wait_ge((osum_ready if gdn else h_osum), c + 1)
                            rsqrt_of(sq[0][:].rearrange("p h n -> p (h n)")[:, 0:4 * n], K(4)[:, 0:4 * n], 1.0 / P).then_inc((ors_ready if gdn else h_ors), 1)
                            a.wait_ge((ors_ready if gdn else h_ors), s((ors_ready if gdn else h_ors)))
                        elif kind == "h_fa":
                            hd = args[0]
                            if hd == 0:
                                a.wait_ge(l2_ready, 8)
                                a.wait_ge(silu_ready, 12)
                            fn(kB[:, hd, :], fB[:, hd, :], ACT.Exp).then_inc(f_expf, 1)
                            fn(t1[:, hd, :], fB[:, hd, :], ACT.Abs).then_inc(act_seq, 1)
                            a.wait_ge(act_seq, s(act_seq))
                            fn(t1[:, hd, :], t1[:, hd, :], ACT.Exp, scale=-1.0).then_inc(act_seq, 1)
                            a.wait_ge(act_seq, s(act_seq))
                            fn(t1[:, hd, :], t1[:, hd, :], ACT.Ln, bias=C("one")).then_inc(act_seq, 1)
                            a.wait_ge(act_seq, s(act_seq))
                            fn(t2[:, hd, :], fB[:, hd, :], ACT.Abs, bias=Q("nllb", hd)).then_inc(act_seq, 1)
                            a.wait_ge(act_seq, s(act_seq))
                            fn(t2[:, hd, :], t2[:, hd, :], ACT.Exp, scale=-1.0).then_inc(act_seq, 1)
                            a.wait_ge(act_seq, s(act_seq))
                            fn(t2[:, hd, :], t2[:, hd, :], ACT.Ln, bias=C("one")).then_inc(f_lb1, 1)
                        elif kind == "h_fb":
                            a.wait_ge(f_bounded, args[0] + 1)
                            sigmoid_of(kB[:, args[0], :]).then_inc(f_sigmoid, 1)
                        elif kind == "h_e":
                            c, n = args[0], CHUNKS[args[0]][1]
                            a.wait_ge(f_ready, HEADS)
                            if c:
                                a.wait_ge(h_s_updated, c)
                            else:
                                a.wait_ge(sdecayed, HEADS)
                            fn(eg[:, :, 0:n], chunk(fB, c), ACT.Exp).then_inc(h_eb_ready, 1)
                            a.wait_ge(h_eb_ready, s(h_eb_ready))
                            a.wait_ge(h_kdiff, c + 1)
                            fn(DD[:, :, 0:n], DD[:, :, 0:n], ACT.Exp).then_inc(h_kdexp, 1)
                            a.wait_ge(h_kdexp, s(h_kdexp))
                        elif kind == "h_t":
                            c, n = args[0], CHUNKS[args[0]][1]
                            a.wait_ge(h_t_ready, c + 1)
                            fn(Kd[0:n], K4(0, n, P), ACT.Copy).then_inc(h_kdT, 1)
                            a.wait_ge(h_kdT, s(h_kdT))
                        elif kind == "h_l":
                            c, n, lv = args[0], CHUNKS[args[0]][1], nth(*item)
                            buf = (NT, XX)[lv % 2]
                            a.wait_ge(h_ldiff, lv)
                            fn(buf[:, :, 0:n], buf[:, :, 0:n], ACT.Exp).then_inc(h_lexp, 1)
                            a.wait_ge(h_lexp, s(h_lexp))
                        elif kind == "h_s" and args[0] == HEADS - 1:
                            a.wait_ge(h_sstep, HEADS)
                            fn(sq[0][:].rearrange("p h n -> p (h n)")[:, 0:256], K(2)[:, 0:256], ACT.Square).then_inc(h_o_squared, 1)
                            a.wait_ge(h_o_squared, s(h_o_squared))
                        elif kind == "r_a":
                            c, n = args[0], CHUNKS[args[0]][1]
                            a.wait_ge(r_a_ready, c + 1)
                            tail = C("tailS", 64) if c == SAMPLE else C("tailP")
                            for hd in range(HEADS):
                                last = fn(Kd[0:n, hd, :], K4(0, n, P)[:, hd, :], ACT.Copy, scale=tail[:, hd:hd + 1])
                                if hd < HEADS - 1:
                                    last.then_inc(act_seq, 1)
                                    a.wait_ge(act_seq, s(act_seq))
                            last.then_inc(r_kd, 1)
                            a.wait_ge(r_kd, s(r_kd))
                        elif kind == "r_o" or (kind == "r_s" and args[0] == 7):
                            c = args[0] if kind == "r_o" else SAMPLE
                            n = CHUNKS[c][1]
                            if kind == "r_o":
                                a.wait_ge(r_o_ready, c + 1)
                            else:
                                a.wait_ge(r_sstep, 8)
                            fn(sq[0][:].rearrange("p h n -> p (h n)")[:, 0:4 * n], K(2)[:, 0:4 * n], ACT.Square).then_inc(act_seq, 1)
                            a.wait_ge(act_seq, s(act_seq))
                            fn(sq[1][:].rearrange("p h n -> p (h n)")[:, 0:4 * n], K(3)[:, 0:4 * n], ACT.Square).then_inc(r_squared, 1)
                            a.wait_ge(r_squared, s(r_squared))
                        elif kind == "r_n":
                            c, n = args[0], CHUNKS[args[0]][1]
                            a.wait_ge(r_osum, c + 1)
                            rsqrt_of(XX[:].rearrange("p h n -> p (h n)")[:, 0:4 * n], K(1)[:, 0:4 * n], 1.0 / DV_RET).then_inc(r_ors, 1)
                            a.wait_ge(r_ors, s(r_ors))

                @block.vector
                def _(dve):
                    v = Steps()
                    tt, ts, stt = nc.vector.tensor_tensor, nc.vector.tensor_scalar, nc.vector.scalar_tensor_tensor
                    nc.vector.tensor_copy(par[:], parAll[:, bass.ds(layer, 1), :].rearrange("p a n -> p (a n)")).then_inc(par_ready, 1)
                    dve.wait_ge(par_ready, v(par_ready))

                    def state_piece(S3, lo, hi, hd=None):
                        tt(S3[:, 0:4, :], S3[:, 0:4, :], lo, ALU.add).then_inc(dve_seq, 1)
                        dve.wait_ge(dve_seq, v(dve_seq))
                        return tt(S3[:, 4:8, :], S3[:, 4:8, :], hi, ALU.add)

                    def fourb(ap):
                        return ap.rearrange("p (b v) -> p b v", b=4)

                    for item in SCHEDULE:
                        kind, args = item[0], item[1:]
                        if kind == "split":
                            p = args[0]
                            dve.wait_ge(w_high_ready, p + 1)
                            w = ring[:, p % RING, :]
                            tt(r32(w), w, high(w_high[:, p % SPLIT_RING, :]), ALU.subtract).then_inc(w_split, 1)
                        elif kind == "hid_split":
                            i = args[0]
                            dve.wait_ge(hid_high_ready, i + 1)
                            tt(r32(hid[:, i, :]), hid[:, i, :], high(hid_high(i)), ALU.subtract).then_inc(hid_ready, 1)
                        elif kind == "scale":
                            norm = args[0]
                            if norm:
                                dve.wait_ge(rms_ready, 1)
                                dve.wait_ge(sumsq_ready, 1)
                            for kt in range(KT):
                                stt(h[:, kt, :], x[:, kt, :], Q("nf" if norm else "nm", kt), rs[:], ALU.mult, ALU.mult) \
                                    .then_inc(h_scaled, 1)
                            for kt in range(POOL_LOW, KT):
                                dve.wait_ge(h_high_ready, KT * norm + kt + 1)
                                tt(r32(h[:, kt, :]), h[:, kt, :], high(h_high[:, kt, :]), ALU.subtract).then_inc(h_late_ready, 1)
                            if norm == 0:
                                dve.wait_ge(wba_high_ready, 1)
                                tt(r32(wbaT[:]), wbaT[:], high(wba_high[:]), ALU.subtract).then_inc(wba_ready, 1)
                        elif kind == "unit":
                            u = args[0]
                            k, slot, m, i = UNITS[u]
                            bank = ps[:, u % BANKS, :]
                            if k == "ba":
                                dve.wait_ge(unit_done, unit_no(u))
                                nc.vector.tensor_copy(bab[:, 0:2, :], bank[:, 0:16].rearrange("p (c n) -> p c n", c=2)).then_inc(dve_seq, 1)
                                dve.wait_ge(dve_seq, v(dve_seq))
                                nc.vector.tensor_copy(bab[0:64, 2, :], bank[0:64, 16:24]).then_inc(bank_read[u % BANKS], 1)
                                dve.wait_ge(bank_read[u % BANKS], bank_no(u))
                            elif k in SILU_KINDS:
                                j = TEMP_ORDER[u]
                                dve.wait_ge(temp_ready, j + 1)
                                tm = temp[:, j % 2, :]
                                ts(tm, tm, EXP_BOUND, 1.0, ALU.min, ALU.add).then_inc(temp_bounded, 1)
                                dve.wait_ge(temp_sigmoid, SILU_NO[u] + 1)
                                if k == "q_b" and i == 0:
                                    dve.wait_ge(l2_ready, 8)
                                if k == "z_b" and i == 0:
                                    dve.wait_ge(l2_ready, 8)
                                dst = {"z_a": zA, "z_b": zB, "q_b": qB, "g_c": gC}[k][:, i, :]
                                stt(dst, bank[:, 0:T], P ** -0.5 if k == "q_b" else 1.0, tm,
                                                ALU.mult, ALU.mult).then_inc(bank_read[u % BANKS], 1)
                                dve.wait_ge(bank_read[u % BANKS], bank_no(u))
                            elif k in ("q_c", "k_c"):
                                j = TEMP_ORDER[u]
                                dve.wait_ge(temp_ready, j + 1)
                                if i == 0:
                                    dve.wait_ge(unit_done, unit_no(UNIT_AT["br_a", 7]))
                                    dve.wait_ge(gdn_out, 32)
                                dst = (qC if k == "q_c" else kC)[:, i, :]
                                sc = 1.0 if k == "q_c" else P ** -0.5
                                tm = temp[:, j % 2, :]
                                stt(dst, bank[:, 0:T], sc, C("cos"), ALU.mult, ALU.mult).then_inc(bank_read[u % BANKS], 1)
                                dve.wait_ge(bank_read[u % BANKS], bank_no(u))
                                stt(tm, tm, sc, C("sin"), ALU.mult, ALU.mult).then_inc(dve_seq, 1)
                                dve.wait_ge(dve_seq, v(dve_seq))
                                tt(dst, dst, tm, ALU.add).then_inc(temp_used, 1)
                                dve.wait_ge(temp_used, v(temp_used))
                            elif k in ("br_a", "br_b", "br_c"):
                                g = gate[:, i, :]
                                dve.wait_ge(gates_sigmoid, 4 * "abc".index(k[3]) + i // 2 + 1)
                                dve.wait_ge(unit_done, unit_no(u))
                                tt(merged[:, i, :] if k == "br_a" else g, bank[:, 0:T], g, ALU.mult).then_inc(bank_read[u % BANKS], 1)
                                dve.wait_ge(bank_read[u % BANKS], bank_no(u))
                            elif k in ("out", "down"):
                                dve.wait_ge(unit_done, unit_no(u))
                                tt(x[:, i, :], x[:, i, :], bank[:, 0:T], ALU.add).then_inc(bank_read[u % BANKS], 1)
                                dve.wait_ge(bank_read[u % BANKS], bank_no(u))
                        elif kind == "gate_bound":
                            br, j = args
                            for w in (0, 1):
                                g = UNIT_AT["gate_" + "abc"[br], 2 * j + w]
                                dve.wait_ge(bank_read[g % BANKS], bank_no(g))
                            z = gate[:, 2 * j:2 * j + 2, :]
                            ts(z, z, EXP_BOUND, 1.0, ALU.min, ALU.add).then_inc(gates_bounded, 1)
                        elif kind == "conv":
                            m = args[0]
                            dve.wait_ge(bank_read[(UNIT_AT["raw", m]) % BANKS], bank_no(UNIT_AT["raw", m]))
                            if m == 0:
                                dve.wait_ge(hist_placed, 2)
                            if m >= CV_RING:
                                dve.wait_ge(silu_ready, m - CV_RING + 1)
                            z = conv_tile(m)
                            ts(z, raw[:, m, 0:CONV], Q("cw", m), None, ALU.mult).then_inc(dve_seq, 1)
                            dve.wait_ge(dve_seq, v(dve_seq))
                            for j in range(1, 4):
                                last = stt(z, raw[:, m, j:j + CONV], Q("cw", 12 * j + m), z, ALU.mult, ALU.add)
                                if j < 3:
                                    last.then_inc(dve_seq, 1)
                                    dve.wait_ge(dve_seq, v(dve_seq))
                            last.then_inc(conv_ready, 1)
                        elif kind == "conv_bound":
                            z = exp_tile(args[0])
                            dve.wait_ge(conv_exp_ready, args[0] + 1)
                            ts(z, z, EXP_BOUND, 1.0, ALU.min, ALU.add).then_inc(conv_bounded, 1)
                        elif kind == "ba":
                            dt = Q("dt")[:, None, :].to_broadcast([P, 3, 4])
                            tt(ap_, bab[:, :, 4:8], dt, ALU.add).then_inc(adt_ready, 1)
                            dve.wait_ge(adt_ready, v(adt_ready))
                            dve.wait_ge(softplus_ready, 1)
                            stt(la, ap_, 0.0, la, ALU.max, ALU.add).then_inc(dve_seq, 1)
                            dve.wait_ge(dve_seq, v(dve_seq))
                            ts(nea, nea, -1.0, None, ALU.mult).then_inc(dve_seq, 1)
                            dve.wait_ge(dve_seq, v(dve_seq))
                            tt(la, la, nea[:, None, :].to_broadcast([P, 3, 4]), ALU.mult).then_inc(dve_seq, 1)
                            dve.wait_ge(dve_seq, v(dve_seq))
                            ts(eb, eb, 1.0, None, ALU.add).then_inc(dve_seq, 1)
                            dve.wait_ge(dve_seq, v(dve_seq))
                            nc.vector.reciprocal(beta, eb).then_inc(dve_seq, 1)
                            dve.wait_ge(dve_seq, v(dve_seq))
                            ts(nbeta, beta, -1.0, None, ALU.mult).then_inc(ba_ready, 1)
                            dve.wait_ge(ba_ready, v(ba_ready))
                        elif kind == "g_bc":
                            c, n = args[0], CHUNKS[args[0]][1]
                            dve.wait_ge(bc_ready, c + 1)
                            if c:
                                dve.wait_ge(v_copied, c)
                                dve.wait_ge(g_gated, c)
                            nc.vector.tensor_copy(gc[0:n], K(2)[0:n, 0:8]).then_inc(dve_seq, 1)
                            dve.wait_ge(dve_seq, v(dve_seq))
                            tt(tl[0:n], gc[0:n, 4:8], gc[0:n, 0:4], ALU.subtract).then_inc(dve_seq, 1)
                            dve.wait_ge(dve_seq, v(dve_seq))
                            dve.wait_ge(eg_ready, c + 1)
                            for hd in range(HEADS):
                                g = gc[0:n, hd:hd + 1]
                                G = K4(0, P, n)[0:n, hd, :]
                                ts(DT[0:n, hd, 0:n], G, g, g, ALU.min, ALU.subtract).then_inc(dve_seq, 1)
                                dve.wait_ge(dve_seq, v(dve_seq))
                                last = ts(DD[0:n, hd, 0:n], G, g, g, ALU.max, ALU.subtract)
                                if hd < HEADS - 1:
                                    last.then_inc(dve_seq, 1)
                                    dve.wait_ge(dve_seq, v(dve_seq))
                            last.then_inc(ddiff_ready, 1)
                            dve.wait_ge(ddiff_ready, v(ddiff_ready))
                            dve.wait_ge(decay_ready, c + 1)
                            tt(nbeg[0:n], nbeta[0:n, c, :], egc[0:n], ALU.mult).then_inc(gates_ready, 1)
                            dve.wait_ge(gates_ready, v(gates_ready))
                        elif kind == "g_gram":
                            c, n = args[0], CHUNKS[args[0]][1]
                            dve.wait_ge(gram_ready, 2 * c + 1)
                            dve.wait_ge(masked_ready, c + 1)
                            for hd in range(HEADS):
                                stt(DD[0:n, hd, 0:n], K4(3, n, n)[:, hd, :], nbeta[0:n, c, hd:hd + 1],
                                           DD[0:n, hd, 0:n], ALU.mult, ALU.mult).then_inc(dve_seq, 1)
                                dve.wait_ge(dve_seq, v(dve_seq))
                            tt(NT[0:n, :, 0:n], K4(3, n, n), NT[0:n, :, 0:n], ALU.mult).then_inc(dve_seq, 1)
                            dve.wait_ge(dve_seq, v(dve_seq))
                            tt(DT[0:n, :, 0:n], K4(4, n, n), DT[0:n, :, 0:n], ALU.mult).then_inc(dve_seq, 1)
                            dve.wait_ge(dve_seq, v(dve_seq))
                            idn = over_heads(ident, n, n)
                            nc.vector.tensor_copy(XX[0:n, :, 0:n], idn).then_inc(dve_seq, 1)
                            dve.wait_ge(dve_seq, v(dve_seq))
                            nc.vector.tensor_copy(XT[0:n, :, 0:n], idn).then_inc(dve_seq, 1)
                            dve.wait_ge(dve_seq, v(dve_seq))
                            nc.vector.copy_predicated(XX[0:n, :, 0:n], over_heads(masks[:, 8, :], n, n),
                                                             DD[0:n, :, 0:n]).then_inc(dve_seq, 1)
                            dve.wait_ge(dve_seq, v(dve_seq))
                            nc.vector.copy_predicated(XT[0:n, :, 0:n], over_heads(masks[:, 0, :], n, n),
                                                             NT[0:n, :, 0:n]).then_inc(attn_ready, 1)
                            dve.wait_ge(attn_ready, v(attn_ready))
                        elif kind == "g_z":
                            c, n, lv = args[0], CHUNKS[args[0]][1], args[1]
                            dve.wait_ge(z_ready, nth(*item))
                            if lv < levels_of(c) - 1:
                                nc.vector.copy_predicated(XX[0:n, :, 0:n], over_heads(masks[:, 8 + lv, :], n, n), K4(3, n, n))
                            nc.vector.copy_predicated(XT[0:n, :, 0:n], over_heads(masks[:, lv, :], n, n),
                                                             K4(4, n, n)).then_inc(x_updated, 1)
                            dve.wait_ge(x_updated, v(x_updated))
                        elif (kind == "g_ks" and args[0] == 1) or kind == "g_ks2":
                            c, n = args[0], CHUNKS[args[0]][1]
                            dve.wait_ge(kdv_ready, c + 1)
                            if c == SAMPLE:
                                dve.wait_ge(ks2_ready, 1)
                            else:
                                dve.wait_ge(ks_ready, 1)
                            for hd in range(HEADS):
                                last = stt(VR[0:n, hd, :], K4(0, n, P)[:, hd, :], nbeg[0:n, hd:hd + 1], VR[0:n, hd, :],
                                           ALU.mult, ALU.add)
                                if hd < HEADS - 1:
                                    last.then_inc(dve_seq, 1)
                                    dve.wait_ge(dve_seq, v(dve_seq))
                            last.then_inc(rhs_ready, 1)
                            dve.wait_ge(rhs_ready, v(rhs_ready))
                        elif kind in ("g_o", "h_o"):
                            c, n = args[0], CHUNKS[args[0]][1]
                            gdn = kind == "g_o"
                            dve.wait_ge((o_ready if gdn else h_o_ready), c + 1)
                            if c == SAMPLE:
                                continue
                            if not gdn and c == 0:
                                dve.wait_ge(gdn_out, 32)
                            for hd in range(HEADS):
                                Sh = S[:, hd * P:hd * P + P]
                                if c == 0:
                                    last = nc.vector.tensor_copy(Sh, K4(3, P, P)[:, hd, :])
                                else:
                                    last = stt(Sh, Sh, eg[:, hd, n - 1:n], K4(3, P, P)[:, hd, :], ALU.mult, ALU.add)
                                if hd < HEADS - 1:
                                    last.then_inc(dve_seq, 1)
                                    dve.wait_ge(dve_seq, v(dve_seq))
                            last.then_inc((s_updated if gdn else h_s_updated), 1)
                            dve.wait_ge((s_updated if gdn else h_s_updated), v((s_updated if gdn else h_s_updated)))
                        elif kind in ("g_n", "h_n"):
                            c, n = args[0], CHUNKS[args[0]][1]
                            gdn = kind == "g_n"
                            dve.wait_ge((ors_ready if gdn else h_ors), c + 1)
                            flat = lambda z: z.rearrange("p h n -> p (h n)")[:, 0:4 * n]
                            stt(flat(XT[:]), K(2)[:, 0:4 * n], Q("gn" if gdn else "hn"), flat(sq[0][:]),
                                       ALU.mult, ALU.mult).then_inc((onormed if gdn else h_onormed), 1)
                            dve.wait_ge((onormed if gdn else h_onormed), v((onormed if gdn else h_onormed)))
                        elif kind == "g_s":
                            hd = args[0]
                            dve.wait_ge(sstep_ready, hd + 1)
                            dve.wait_ge(sdecayed, hd + 1)
                            state_piece(gstate[:, hd], fourb(K(3 * (hd % 2))), fourb(K(3 * (hd % 2) + 1))).then_inc(sst_updated, 1)
                            dve.wait_ge(sst_updated, v(sst_updated))
                        elif kind == "h_fa":
                            k_ = kB[:, args[0], :]
                            dve.wait_ge(f_expf, args[0] + 1)
                            ts(k_, k_, EXP_BOUND, 1.0, ALU.min, ALU.add).then_inc(f_bounded, 1)
                        elif kind == "h_fb":
                            hd = args[0]
                            f_, k_, a1, a2 = fB[:, hd, :], kB[:, hd, :], t1[:, hd, :], t2[:, hd, :]
                            dve.wait_ge(f_lb1, hd + 1)
                            tt(a2, a2, a1, ALU.subtract).then_inc(dve_seq, 1)
                            dve.wait_ge(dve_seq, v(dve_seq))
                            ts(a1, f_, 0.0, None, ALU.min).then_inc(dve_seq, 1)
                            dve.wait_ge(dve_seq, v(dve_seq))
                            stt(f_, a1, Q("llb", hd), f_, ALU.add, ALU.subtract).then_inc(dve_seq, 1)
                            dve.wait_ge(dve_seq, v(dve_seq))
                            tt(f_, f_, a1, ALU.max).then_inc(dve_seq, 1)
                            dve.wait_ge(dve_seq, v(dve_seq))
                            tt(a1, f_, a2, ALU.add).then_inc(dve_seq, 1)
                            dve.wait_ge(dve_seq, v(dve_seq))
                            dve.wait_ge(f_sigmoid, hd + 1)
                            ts(k_, k_, Q("oml", hd), None, ALU.mult).then_inc(dve_seq, 1)
                            dve.wait_ge(dve_seq, v(dve_seq))
                            nc.vector.tensor_tensor_scan(f_, C("reset"), a1, 0.0, ALU.mult, ALU.add).then_inc(f_ready, 1)
                            dve.wait_ge(f_ready, v(f_ready))
                        elif kind == "h_e":
                            c, n = args[0], CHUNKS[args[0]][1]
                            b = chunk(fB, c)
                            if c:
                                dve.wait_ge(h_t_ready, c)
                            if c == SAMPLE:
                                b3 = seqs(b)
                                last = tt(seqs(DD[:, :, 0:n]), b3[:, :, :, ST - 1:ST].to_broadcast([P, 4, SB, ST]), b3,
                                          ALU.subtract)
                            else:
                                last = tt(DD[:, :, 0:n], b[:, :, n - 1:n].to_broadcast([P, 4, n]), b, ALU.subtract)
                            last.then_inc(h_kdiff, 1)
                            dve.wait_ge(h_kdiff, v(h_kdiff))
                        elif kind == "h_l":
                            c, n, lv = args[0], CHUNKS[args[0]][1], nth(*item)
                            hf = LEVELS[args[1]]
                            buf = (NT, XX)[lv % 2]
                            if lv > 2:
                                dve.wait_ge(h_m_ready, lv - 2)
                            b, o = blocks(chunk(fB, c), hf), blocks(buf[:, :, 0:n], hf)
                            ref = b[:, :, :, hf - 1:hf].to_broadcast([P, 4, n // (2 * hf), hf])
                            tt(o[:, :, :, 0:hf], ref, b[:, :, :, 0:hf], ALU.subtract).then_inc(dve_seq, 1)
                            dve.wait_ge(dve_seq, v(dve_seq))
                            tt(o[:, :, :, hf:], b[:, :, :, hf:], ref, ALU.subtract).then_inc(h_ldiff, 1)
                            dve.wait_ge(h_ldiff, v(h_ldiff))
                        elif kind == "h_t":
                            c, n = args[0], CHUNKS[args[0]][1]
                            dve.wait_ge(h_attn0, c + 1)
                            dve.wait_ge(h_t_ready, c + 1)
                            nc.vector.copy_predicated(DT[0:n, :, 0:n], over_heads(masks[:, DIAG, :], n, n),
                                                             K4(1, n, n)).then_inc(h_diag_done, 1)
                            dve.wait_ge(h_diag_done, v(h_diag_done))
                        elif kind == "h_m":
                            c, n, lv = args[0], CHUNKS[args[0]][1], nth(*item)
                            dve.wait_ge(h_m_ready, lv)
                            nc.vector.copy_predicated(DT[0:n, :, 0:n], over_heads(masks[:, args[1], :], n, n),
                                                             K4(3 + lv % 2, n, n)).then_inc(h_m_read, 1)
                            dve.wait_ge(h_m_read, v(h_m_read))
                        elif kind == "h_s":
                            hd = args[0]
                            dve.wait_ge(h_sstep, hd + 1)
                            dve.wait_ge(h_sdec, hd + 1)
                            state_piece(by_seq(hg_piece[hd]), fourb(K(3 * (hd % 2))), fourb(K(3 * (hd % 2) + 1))).then_inc(h_sst, 1)
                            dve.wait_ge(h_sst, v(h_sst))
                        elif kind == "r_a":
                            c, n = args[0], CHUNKS[args[0]][1]
                            dve.wait_ge(r_a_ready, c + 1)
                            dm = C("dmS", 64) if c == SAMPLE else C("dmP")
                            tt(DT[0:n, :, 0:n], K4(1, n, n), dm.rearrange("p (h n) -> p h n", h=4), ALU.mult).then_inc(r_attn, 1)
                            dve.wait_ge(r_attn, v(r_attn))
                        elif kind == "r_o":
                            c, n = args[0], CHUNKS[args[0]][1]
                            dve.wait_ge(r_o_ready, c + 1)
                            if c == 0:
                                dve.wait_ge(hg_out, 16)
                            for hd in range(HEADS):
                                Sh = S_ret[:, hd * DV_RET:(hd + 1) * DV_RET]
                                src = K((4, 0)[hd // 2])[:, (hd % 2) * DV_RET:(hd % 2 + 1) * DV_RET]
                                if c == 0:
                                    last = nc.vector.tensor_copy(Sh, src)
                                else:
                                    last = stt(Sh, Sh, GAMMA[hd] ** n, src, ALU.mult, ALU.add)
                                if hd < HEADS - 1:
                                    last.then_inc(dve_seq, 1)
                                    dve.wait_ge(dve_seq, v(dve_seq))
                            last.then_inc(r_s_updated, 1)
                            dve.wait_ge(r_s_updated, v(r_s_updated))
                        elif kind == "r_s":
                            p_ = args[0]
                            dve.wait_ge(r_sstep, p_ + 1)
                            dec = GAMMA[p_ // 2] ** ST
                            for g, b in ((0, 4), (1, 0)):
                                S3 = by_seq(ret_piece[p_])[:, 4 * g:4 * g + 4, :]
                                last = stt(S3, S3, dec, fourb(K(b)), ALU.mult, ALU.add)
                                if g == 0:
                                    last.then_inc(dve_seq, 1)
                                    dve.wait_ge(dve_seq, v(dve_seq))
                            last.then_inc(r_sst, 1)
                            dve.wait_ge(r_sst, v(r_sst))
                        elif kind == "r_n":
                            c, n = args[0], CHUNKS[args[0]][1]
                            dve.wait_ge(r_ors, c + 1)
                            flat = lambda z: z.rearrange("p h n -> p (h n)")[:, 0:4 * n]
                            tt(flat(XT[:]), K(2)[:, 0:4 * n], flat(XX[:]), ALU.mult).then_inc(dve_seq, 1)
                            dve.wait_ge(dve_seq, v(dve_seq))
                            tt(flat(NT[:]), K(3)[:, 0:4 * n], flat(XX[:]), ALU.mult).then_inc(r_onormed, 1)
                            dve.wait_ge(r_onormed, v(r_onormed))

                @block.gpsimd
                def _(pool):
                    pl = Steps()
                    tt = nc.gpsimd.tensor_tensor

                    def per_layer(ap):
                        return ap[bass.ds(layer, 1)].rearrange("a p n -> (a p) n")

                    def spread(vals, to):
                        return tt(to[0:64, :, :], vals[:, None, :].to_broadcast([64, 4, P]),
                                  C("seqm", 64)[:, :, None].to_broadcast([64, 4, P]), ALU.mult)

                    def store_hg(i):
                        pool.wait_ge(h_sst, i + 1)
                        pool.dma_start(o_hg_s[bass.ds(layer, 1), i].rearrange("a p n -> (a p) n"), hg_piece[i]) \
                            .then_inc(hg_moved[i], 16)

                    def store_ret(i):
                        pool.wait_ge(r_sst, i + 1)
                        pool.dma_start(o_ret_s[bass.ds(layer, 1), i].rearrange("a p n -> (a p) n"), ret_piece[i]) \
                            .then_inc(ret_moved[i], 16)

                    def fill_history():
                        nc.gpsimd.memset(raw[:, :, 0:HIST], 0.0).then_inc(hist_placed, 1)
                        pool.wait_ge(hist_placed, pl(hist_placed))
                        pool.wait_ge(hist_loaded, 16)
                        for b in range(SB):
                            o = RAW_P + RAW_S * b
                            last = nc.gpsimd.tensor_copy(raw[:, :, o:o + HIST],
                                                         hist.rearrange("p (m b t) -> p m b t", m=12, b=SB)[:, :, b, :])
                            if b < SB - 1:
                                last.then_inc(pool_seq, 1)
                                pool.wait_ge(pool_seq, pl(pool_seq))
                        last.then_inc(hist_placed, 1)
                        pool.wait_ge(hist_placed, pl(hist_placed))

                    pool.dma_start(hist, per_layer(st_conv)).then_inc(hist_loaded, 16)
                    for item in SCHEDULE:
                        kind, args = item[0], item[1:]
                        if kind == "scale":
                            for kt in range(POOL_LOW):
                                pool.wait_ge(h_high_ready, KT * args[0] + kt + 1)
                                tt(r32(h[:, kt, :]), h[:, kt, :], high(h_high[:, kt, :]), ALU.subtract).then_inc(h_ready, 1)
                            if args[0] == 0:
                                fill_history()
                        elif kind == "z_split":
                            br, c = args
                            t0, n = CHUNKS[c]
                            z, z_high = {"a": (zA, zA_high), "b": (zB, fB), "c": (gC, gC_high)}[br]
                            pool.wait_ge(z_high_ready, "abc".index(br) * 3 + c + 1)
                            tt(r32(z[:, :, t0:t0 + n]), z[:, :, t0:t0 + n], high(z_high[:, :, t0:t0 + n]), ALU.subtract).then_inc(z_split, 1)
                        elif kind == "m_split":
                            i = args[0]
                            pool.wait_ge(merged_high_ready, i + 1)
                            tt(r32(merged[:, i, :]), merged[:, i, :], high(gate[:, i, :]), ALU.subtract).then_inc(merged_ready, 1)
                        elif kind == "unit":
                            u = args[0]
                            k, slot, m, i = UNITS[u]
                            if k in ("br_b", "br_c"):
                                pool.wait_ge(bank_read[u % BANKS], bank_no(u))
                                tt(merged[:, i, :], merged[:, i, :], gate[:, i, :], ALU.add).then_inc(merged_added, 1)
                                pool.wait_ge(merged_added, pl(merged_added))
                            elif k == "up":
                                pool.wait_ge(bank_read[u % BANKS], bank_no(u))
                                tt(hid[:, i, :], hid[:, i, :], hid[:, i, :], ALU.mult).then_inc(hid_squared, 1)
                        elif kind == "silu":
                            i = args[0]
                            pool.wait_ge(conv_sigmoid, i + 1)
                            cv, ce, own = conv_tile(i), exp_tile(i), act[:, i, SEQ:]
                            tt(act[:, i, 0:SEQ], cv[:, 0:SEQ], ce[:, 0:SEQ], ALU.mult).then_inc(pool_seq, 1)
                            pool.wait_ge(pool_seq, pl(pool_seq))
                            o, w, t8 = RAW_P, RAW_S * (SB - 1), ST * (SB - 1)
                            strip = lambda z: z[:, o:o + w].rearrange("p (b t) -> p b t", t=RAW_S)[:, :, 0:ST]
                            tt(own[:, 0:t8].rearrange("p (b t) -> p b t", t=ST), strip(cv), strip(ce), ALU.mult).then_inc(pool_seq, 1)
                            pool.wait_ge(pool_seq, pl(pool_seq))
                            tt(own[:, t8:], cv[:, o + w:], ce[:, o + w:], ALU.mult).then_inc(silu_ready, 1)
                            pool.wait_ge(silu_ready, pl(silu_ready))
                            if i < 8:
                                tt(l2buf(i), act[:, i, :], act[:, i, :], ALU.mult).then_inc(l2sq_ready, 1)
                            if i == 11:
                                for b in range(9):
                                    o = SEQ if b == 0 else RAW_P + RAW_S * (b - 1) + ST
                                    nc.gpsimd.tensor_copy(newc[:, :, b, :], raw[:, :, o:o + HIST]).then_inc(pool_seq, 1)
                                    pool.wait_ge(pool_seq, pl(pool_seq))
                                pool.dma_start(per_layer(o_conv), newc.rearrange("p m b t -> p (m b t)")) \
                                    .then_inc(conv_out, 16)
                                pool.dma_start(arena[:, 0:4096], per_layer(st_gdn)).then_inc(gst_loaded, 16)
                        elif kind == "l2":
                            m = args[0]
                            pool.wait_ge(l2rs_ready, m + 1)
                            tt(act[:, m, :], act[:, m, :], l2buf(m), ALU.mult).then_inc(l2_ready, 1)
                            pool.wait_ge(l2_ready, pl(l2_ready))
                        elif kind == "g_bc":
                            c, (t0, n) = args[0], CHUNKS[args[0]]
                            pool.wait_ge(decay_ready, c + 1)
                            pool.wait_ge(l2_ready, 8)
                            pool.wait_ge(negb_ready, c + 1)
                            tt(DT[0:n, :, 0:n], DT[0:n, :, 0:n], over_heads(up_mask(c), n, n), ALU.mult).then_inc(pool_seq, 1)
                            pool.wait_ge(pool_seq, pl(pool_seq))
                            tt(NT[0:n, :, 0:n], NT[0:n, :, 0:n], DT[0:n, :, 0:n], ALU.mult).then_inc(masked_ready, 1)
                            pool.wait_ge(masked_ready, pl(masked_ready))
                            tt(qg[:, :, 0:n], act[:, 0:4, t0:t0 + n], eg[:, :, 0:n], ALU.mult).then_inc(qg_ready, 1)
                            pool.wait_ge(qg_ready, pl(qg_ready))
                        elif kind in ("g_n", "h_n"):
                            c, (t0, n) = args[0], CHUNKS[args[0]]
                            gdn = kind == "g_n"
                            pool.wait_ge((onormed if gdn else h_onormed), c + 1)
                            z = zA if gdn else zB
                            if gdn and c == 0:
                                for b in range(1, 4):
                                    pool.wait_ge(bank_read[(UNIT_AT["z_a", b]) % BANKS], bank_no(UNIT_AT["z_a", b]))
                            if not gdn and c == 0:
                                for b in range(1, 4):
                                    pool.wait_ge(bank_read[(UNIT_AT["z_b", b]) % BANKS], bank_no(UNIT_AT["z_b", b]))
                            xt = XT[:].rearrange("p h n -> p (h n)")[:, 0:4 * n].rearrange("p (h n) -> p h n", h=4)
                            tt(z[:, :, t0:t0 + n], z[:, :, t0:t0 + n], xt, ALU.mult).then_inc((g_gated if gdn else h_gated), 1)
                            pool.wait_ge((g_gated if gdn else h_gated), pl((g_gated if gdn else h_gated)))
                            if c == 1 and gdn:
                                pool.wait_ge(s_updated, 2)
                                pool.dma_start(per_layer(o_gdn_p), S[:, 0:512]).then_inc(gdn_out, 16)
                                pool.wait_ge(gdn_out, 16)
                            if c == 1 and not gdn:
                                pool.wait_ge(h_s_updated, 2)
                                pool.dma_start(per_layer(o_hg_p), S[:, 0:512]).then_inc(hg_out, 16)
                        elif kind == "g_s":
                            hd = args[0]
                            if hd == 0:
                                pool.wait_ge(o_ready, 3)
                            if hd > 1:
                                pool.wait_ge(sstep_ready, hd - 1)
                            spread(vn[0:64, hd, :], (PP, XT)[hd % 2]).then_inc(vm_ready, 1)
                            dec = eg[:, hd, 0:64].rearrange("p (b t) -> p b t", b=SB)[:, :, ST - 1:ST]
                            tt(gstate[:, hd], gstate[:, hd], dec.to_broadcast([P, SB, P]), ALU.mult).then_inc(sdecayed, 1)
                            if hd == HEADS - 1:
                                pool.wait_ge(sst_updated, HEADS)
                                pool.dma_start(per_layer(o_gdn_s), arena[:, 0:4096]).then_inc(gdn_out, 16)
                        elif kind == "h_load":
                            pool.wait_ge(unit_done, unit_no(UNIT_AT["br_a", 7]))
                            pool.wait_ge(gdn_out, 32)
                            for i in range(HEADS):
                                pool.dma_start(hg_piece[i], st_hg[bass.ds(layer, 1), i].rearrange("a p n -> (a p) n")) \
                                    .then_inc(hg_moved[i], 16)
                        elif kind == "r_load":
                            if args[0] == 0:
                                for i in range(HEADS):
                                    pool.wait_ge(hg_moved[i], 32)
                            else:
                                pool.wait_ge(h_gated, 3)
                                pool.wait_ge(unit_done, unit_no(UNIT_AT["br_b", 7]))
                            for i in range(HEADS * args[0], HEADS * args[0] + HEADS):
                                pool.dma_start(ret_piece[i], st_ret[bass.ds(layer, 1), i].rearrange("a p n -> (a p) n")) \
                                    .then_inc(ret_moved[i], 16)
                        elif kind == "h_e":
                            c, (t0, n) = args[0], CHUNKS[args[0]]
                            pool.wait_ge(h_eb_ready, c + 1)
                            if c == 0:
                                for b in range(1, 4):
                                    pool.wait_ge(bank_read[(UNIT_AT["q_b", b]) % BANKS], bank_no(UNIT_AT["q_b", b]))
                                pool.wait_ge(f_ready, HEADS)
                            tt(qg[:, :, 0:n], qB[:, :, t0:t0 + n], eg[:, :, 0:n], ALU.mult).then_inc(h_qg_ready, 1)
                            pool.wait_ge(h_qg_ready, pl(h_qg_ready))
                            nc.gpsimd.memset(DT[0:n, :, 0:n], 0.0).then_inc(h_attn0, 1)
                            pool.wait_ge(h_attn0, pl(h_attn0))
                            pool.wait_ge(h_kdexp, c + 1)
                            tt(DD[:, :, 0:n], DD[:, :, 0:n], kB[:, :, t0:t0 + n], ALU.mult).then_inc(h_kd, 1)
                            pool.wait_ge(h_kd, pl(h_kd))
                        elif kind == "h_l":
                            c, (t0, n), lv = args[0], CHUNKS[args[0]], nth(*item)
                            hf = LEVELS[args[1]]
                            buf = (NT, XX)[lv % 2]
                            pool.wait_ge(h_lexp, lv)
                            o, q, k = blocks(buf[:, :, 0:n], hf), blocks(chunk(qB, c), hf), blocks(chunk(kB, c), hf)
                            tt(o[:, :, :, 0:hf], o[:, :, :, 0:hf], k[:, :, :, 0:hf], ALU.mult).then_inc(pool_seq, 1)
                            pool.wait_ge(pool_seq, pl(pool_seq))
                            tt(o[:, :, :, hf:], o[:, :, :, hf:], q[:, :, :, hf:], ALU.mult).then_inc(h_lev_ready, 1)
                            pool.wait_ge(h_lev_ready, pl(h_lev_ready))
                        elif kind == "h_s":
                            hd = args[0]
                            if hd > 1:
                                pool.wait_ge(h_sstep, hd - 1)
                            spread(iB[0:64, SAMPLE, hd * P:hd * P + P], (PP, XT)[hd % 2]).then_inc(h_vm, 1)
                            pool.wait_ge(h_old_read, hd + 1)
                            dec = eg[:, hd, 0:64].rearrange("p (b t) -> p b t", b=SB)[:, :, ST - 1:ST]
                            Sp = by_seq(hg_piece[hd])
                            tt(Sp, Sp, dec.to_broadcast([P, SB, P]), ALU.mult).then_inc(h_sdec, 1)
                            if hd:
                                store_hg(hd - 1)
                            if hd == HEADS - 1:
                                store_hg(hd)
                        elif kind == "r_a":
                            c, (t0, n) = args[0], CHUNKS[args[0]]
                            pool.wait_ge(temp_used, ROT_NO[UNIT_AT["k_c", 3]] + 1)
                            if c:
                                pool.wait_ge(r_s_updated, c)
                            inn = C("innS") if c == SAMPLE else C("innP")
                            tt(qg[:, :, 0:n], qC[:, :, t0:t0 + n], inn.rearrange("p (h n) -> p h n", h=4), ALU.mult).then_inc(r_qg, 1)
                            pool.wait_ge(r_qg, pl(r_qg))
                        elif kind == "r_s":
                            p_ = args[0]
                            hd, f = p_ // 2, p_ % 2
                            if p_ > 1:
                                pool.wait_ge(r_sstep, p_ - 1)
                            spread(vC[0:64, SAMPLE, hd * DV_RET + f * P:hd * DV_RET + f * P + P], (PP, XT)[p_ % 2]).then_inc(r_vm, 1)
                            if p_:
                                store_ret(p_ - 1)
                            if p_ == 2 * HEADS - 1:
                                store_ret(p_)
                        elif kind == "r_n":
                            c, (t0, n) = args[0], CHUNKS[args[0]]
                            pool.wait_ge(r_onormed, c + 1)
                            if c == 0:
                                for b in range(5, 8):
                                    pool.wait_ge(bank_read[(UNIT_AT["g_c", b]) % BANKS], bank_no(UNIT_AT["g_c", b]))
                            for f, src in enumerate((XT, NT)):
                                z = gC.rearrange("p (h f) t -> p h f t", f=2)[:, :, f, t0:t0 + n]
                                sv = src[:].rearrange("p h n -> p (h n)")[:, 0:4 * n].rearrange("p (h n) -> p h n", h=4)
                                last = tt(z, z, sv, ALU.mult)
                                if f == 0:
                                    last.then_inc(pool_seq, 1)
                                    pool.wait_ge(pool_seq, pl(pool_seq))
                            last.then_inc(r_gated, 1)
                            pool.wait_ge(r_gated, pl(r_gated))
                            if c == 1:
                                pool.wait_ge(r_s_updated, 2)
                                pool.dma_start(per_layer(o_ret_p), S_ret) \
                                    .then_inc(ret_out, 16)
                    pool.wait_ge(conv_out, 16)
                    pool.wait_ge(gdn_out, 32)
                    pool.wait_ge(hg_out, 16)
                    pool.wait_ge(ret_out, 16)
                    pool.wait_ge(gst_loaded, 16)
                    for i in range(HEADS):
                        pool.wait_ge(hg_moved[i], 32)
                    for i in range(2 * HEADS):
                        pool.wait_ge(ret_moved[i], 32)
            clear_semaphores()

        with nc.Block() as block:
            @block.vector
            def _(dve):
                for kt in range(KT):
                    nc.vector.scalar_tensor_tensor(h[:, kt, :], x[:, kt, :], nfin[:, kt:kt + 1], rs[:], ALU.mult,
                                                   ALU.mult).then_inc(y_ready, 1)

            @block.sync
            def _(sp):
                for kt in range(0, KT, 2):
                    sp.wait_ge(y_ready, kt + 2)
                    sp.dma_start(y_out[:, kt:kt + 2, :], h[:, kt:kt + 2, :]).then_inc(y_out_sem, 16)
                sp.wait_ge(y_out_sem, 8 * KT)


_OUTS = (("y", (P, KT, T)), ("o_conv", (DEPTH, P, 324)), ("o_gdn_p", (DEPTH, P, 512)), ("o_hg_p", (DEPTH, P, 512)),
         ("o_ret_p", (DEPTH, P, 1024)), ("o_gdn_s", (DEPTH, P, 4096)), ("o_hg_s", (DEPTH, 4, P, 1024)),
         ("o_ret_s", (DEPTH, 8, P, 1024)))


def _slots(w, k_tiles):
    return w.reshape(k_tiles, P, -1).transpose(1, 0, 2).reshape(P, -1)


def kernel(**inputs):
    import numpy as _np
    import concourse.bacc as _bacc
    from concourse import mybir as _mybir
    from concourse.bass_utils import run_bass_kernel_spmd as _run

    a = {k: _np.asarray(v) for k, v in inputs.items()}
    f = _np.float32

    def features(z):
        z = z.reshape(z.shape[:-1] + (-1, P))
        return _np.moveaxis(z, -1, 0)

    x = _np.concatenate([a["x_prompt"].reshape(SEQ, D), a["x_sample"].reshape(SB * ST, D)])
    pack = _np.empty((DEPTH, NSLOT, P, SLOT), f)

    def by_tile(z, n):
        return _slots(z, n).reshape(P, n, -1, P).transpose(0, 2, 1, 3).reshape(P, SLOT)

    for l in range(DEPTH):
        for s, name in enumerate(SLOT_NAMES):
            if name in W_IN_COLUMN:
                c = W_IN_COLUMN[name]
                w = a["w_in"][l][:, c:c + 512]
                pack[l, s] = _slots(w, 8) if name in ("i_b", "v_c0", "v_c1") else by_tile(w, 8)
            elif name in ("br_a", "br_b"):
                pack[l, s] = by_tile(a["w_br_gdn" if name == "br_a" else "w_br_hgrn"][l], 4)
            elif name.startswith("down"):
                i = int(name[4:])
                pack[l, s] = _slots(a["w_down"][l][:, P * i:P * i + P], 32)
            else:
                i = int(name[-1])
                w = {"b": "w_br_ret", "o": "w_out", "u": "w_up"}[name[0]]
                pack[l, s] = by_tile(a[w][l][:, 512 * i:512 * i + 512], 8)
    wba = _np.stack([_slots(a["w_in"][l][:, BA_COLUMN:BA_COLUMN + 8], 8) for l in range(DEPTH)])
    par = _np.zeros((P, DEPTH, NPAR), f)

    def put(name, z):
        s, e = PAR[name]
        par[:, :, s:e] = z

    put("nm", features(a["norm_mix"]))
    put("nf", features(a["norm_ffn"]))
    put("cw", features(a["gdn_conv"]).reshape(P, DEPTH, 48))
    put("gn", features(a["gdn_norm"]))
    put("hn", features(a["hgrn_norm"]))
    put("alog", a["gdn_a_log"][None])
    put("dt", a["gdn_dt_bias"][None])
    lb = features(a["hgrn_lb"])
    const, mask = shape_constants()
    arrays = {
        "x_in": _np.ascontiguousarray(x.T.reshape(KT, P, T).transpose(1, 0, 2)),
        "wpack": _np.ascontiguousarray(pack.reshape(DEPTH, NSLOT, P, 4, PIECE).transpose(0, 1, 3, 2, 4)).reshape(DEPTH, NPIECE, P, PIECE), "wba": wba, "par": par, "nfin": _np.ascontiguousarray(features(a["norm_final"])),
        "lb": _np.ascontiguousarray(lb), "const_in": const, "mask_in": mask,
        "st_conv": _np.ascontiguousarray(
            a["state_gdn_conv"].reshape(DEPTH, SB, HIST, 12, P).transpose(0, 4, 3, 1, 2).reshape(DEPTH, P, 288)),
        "st_gdn": _np.ascontiguousarray(a["state_gdn"].transpose(0, 3, 2, 1, 4).reshape(DEPTH, P, 4096)),
        "st_hg": _np.ascontiguousarray(a["state_hgrn"].transpose(0, 2, 3, 1, 4).reshape(DEPTH, 4, P, 1024)),
        "st_ret": _np.ascontiguousarray(
            a["state_ret"].reshape(DEPTH, SB, 4, P, 2, P).transpose(0, 2, 4, 3, 1, 5).reshape(DEPTH, 8, P, 1024)),
    }
    nc = _bacc.Bacc("TRN2", target_bir_lowering=False, num_devices=1)
    args = [nc.dram_tensor("d_" + k, z.shape, _mybir.dt.from_np(z.dtype), kind="ExternalInput").ap() for k, z in arrays.items()]
    args += [nc.dram_tensor(k, s, _mybir.dt.float32, kind="ExternalOutput").ap() for k, s in _OUTS]
    trunk(nc, *args)
    r = _run(nc, [{"d_" + k: z for k, z in arrays.items()}], core_ids=[0]).results[0]
    y = r["y"].transpose(1, 0, 2).reshape(D, T).T
    cv = r["o_conv"].reshape(DEPTH, P, 12, 9, HIST).transpose(0, 3, 4, 2, 1).reshape(DEPTH, 9, HIST, 12 * P)

    def prompt_state(z, dv):
        return _np.ascontiguousarray(z.reshape(DEPTH, P, 4, dv).transpose(0, 2, 1, 3)[:, None])

    out = (y[:SEQ].reshape(1, SEQ, D), y[SEQ:].reshape(SB, ST, D),
           prompt_state(r["o_gdn_p"], P), cv[:, 0:1], prompt_state(r["o_hg_p"], P), prompt_state(r["o_ret_p"], DV_RET),
           r["o_gdn_s"].reshape(DEPTH, P, 4, SB, P).transpose(0, 3, 2, 1, 4), cv[:, 1:],
           r["o_hg_s"].reshape(DEPTH, 4, P, SB, P).transpose(0, 3, 1, 2, 4),
           r["o_ret_s"].reshape(DEPTH, 4, 2, P, SB, P).transpose(0, 4, 1, 3, 2, 5).reshape(DEPTH, SB, 4, P, DV_RET))
    return tuple(_np.ascontiguousarray(z) for z in out)
```
